# Optimizing a Trainium2 kernel written in Bass

```python
import jax, jax.numpy as jnp
from jax import lax
import numpy as np

D_MODEL = 1024
BATCH = 1
SEQ = 256
DEPTH = 1
DEC_BATCH = 8
DEC_SEQ = 16
PAST_LEN = 512

CHUNK = 64
MLA_HEADS = 8
MLA_NOPE_DIM = 64
MLA_ROPE_DIM = 32
MLA_V_DIM = 64
MLA_Q_LORA = 384
MLA_KV_LORA = 256
MLA_SCALE = (MLA_NOPE_DIM + MLA_ROPE_DIM) ** -0.5
ROPE_THETA = 10000.0
Q_BLOCK = 128
SWA_HEADS = 8
SWA_KV_HEADS = 2
SWA_GROUP = SWA_HEADS // SWA_KV_HEADS
SWA_HEAD_DIM = 64
SWA_SCALE = SWA_HEAD_DIM ** -0.5
WINDOW = 128
WINDOW_CHUNKS = WINDOW // CHUNK
BAND = (WINDOW_CHUNKS + 1) * CHUNK
MIX_WIDTH = MLA_HEADS * MLA_V_DIM + SWA_HEADS * SWA_HEAD_DIM
IN_SIZES = (MLA_Q_LORA, MLA_KV_LORA, MLA_ROPE_DIM, SWA_HEADS * SWA_HEAD_DIM,
            SWA_KV_HEADS * SWA_HEAD_DIM, SWA_KV_HEADS * SWA_HEAD_DIM)
IN_WIDTH = sum(IN_SIZES)
N_EXPERTS = 32
TOP_K = 4
D_FF = D_MODEL
SWIGLU_LIMIT = 7.0
SWIGLU_ALPHA = 1.702
MOE_BLOCK = 128
RMS_EPS = 1e-6
NEG_INF = -1e30

kernel_name = "hybrid_stream_mla_swa_moe_step"

def rms_norm(x, g):
    xf = x.astype(jnp.float32)
    y = xf * lax.rsqrt(jnp.mean(xf * xf, axis=-1, keepdims=True) + RMS_EPS)
    return (y * g.astype(jnp.float32)).astype(x.dtype)

def modulate(h, shift, scale):
    return h * (1 + scale) + shift

def adaln(c, w_ada, b_ada):
    mod = (jax.nn.silu(c) @ w_ada + b_ada)[:, None, :]
    return jnp.split(mod, 6, axis=-1)

def alibi_slopes():
    return 2.0 ** (-8.0 * jnp.arange(1, SWA_HEADS + 1, dtype=jnp.float32) / SWA_HEADS)

def apply_rope(x, pos):
    half = MLA_ROPE_DIM // 2
    inv_freq = ROPE_THETA ** (-jnp.arange(half, dtype=jnp.float32) * 2.0 / MLA_ROPE_DIM)
    ang = pos.astype(jnp.float32)[:, None] * inv_freq[None, :]
    if x.ndim == 4:
        ang = ang[:, None, :]
    cos, sin = jnp.cos(ang), jnp.sin(ang)
    x1 = x[..., :half].astype(jnp.float32)
    x2 = x[..., half:].astype(jnp.float32)
    return jnp.concatenate([x1 * cos - x2 * sin, x2 * cos + x1 * sin], axis=-1).astype(x.dtype)

def mixer_inputs(h, pos, w_in, g_q, w_uq, g_kv, w_ukv):
    B, S, _ = h.shape
    offs = np.cumsum(IN_SIZES)[:-1].tolist()
    q_lat, kv_lat, k_pe, q_s, k_s, v_s = jnp.split(h @ w_in, offs, axis=-1)
    q = jnp.einsum('bsc,chd->bshd', rms_norm(q_lat, g_q), w_uq)
    q_nope = q[..., :MLA_NOPE_DIM]
    q_pe = apply_rope(q[..., MLA_NOPE_DIM:], pos)
    c_kv = rms_norm(kv_lat, g_kv)
    k_pe = apply_rope(k_pe, pos)
    q_s = q_s.reshape(B, S, SWA_KV_HEADS, SWA_GROUP, SWA_HEAD_DIM)
    k_s = k_s.reshape(B, S, SWA_KV_HEADS, SWA_HEAD_DIM)
    v_s = v_s.reshape(B, S, SWA_KV_HEADS, SWA_HEAD_DIM)
    return q_nope, q_pe, c_kv, k_pe, q_s, k_s, v_s

def mla_prompt(q_nope, q_pe, c_kv, k_pe, w_ukv):
    B, S = c_kv.shape[:2]
    kv = jnp.einsum('bsc,chd->bshd', c_kv, w_ukv)
    k_nope, v = kv[..., :MLA_NOPE_DIM], kv[..., MLA_NOPE_DIM:]
    nq = S // Q_BLOCK
    qn_b = q_nope.reshape(B, nq, Q_BLOCK, MLA_HEADS, MLA_NOPE_DIM).swapaxes(0, 1)
    qp_b = q_pe.reshape(B, nq, Q_BLOCK, MLA_HEADS, MLA_ROPE_DIM).swapaxes(0, 1)
    key_chunk = jnp.arange(S) // CHUNK

    def one_block(args):
        qn, qp, i = args
        s = (jnp.einsum('bqhd,bkhd->bhqk', qn, k_nope)
             + jnp.einsum('bqhr,bkr->bhqk', qp, k_pe)).astype(jnp.float32) * MLA_SCALE
        q_chunk = (i * Q_BLOCK + jnp.arange(Q_BLOCK)) // CHUNK
        s = jnp.where(key_chunk[None, :] <= q_chunk[:, None], s, NEG_INF)
        p = jax.nn.softmax(s, axis=-1).astype(v.dtype)
        return jnp.einsum('bhqk,bkhd->bqhd', p, v)

    o = lax.map(one_block, (qn_b, qp_b, jnp.arange(nq)))
    return o.swapaxes(0, 1).reshape(B, S, MLA_HEADS * MLA_V_DIM)

def mla_sample(q_nope, q_pe, lat, kpe, w_ukv):
    B, Q = q_nope.shape[:2]
    w_uk, w_uv = w_ukv[..., :MLA_NOPE_DIM], w_ukv[..., MLA_NOPE_DIM:]
    q_abs = jnp.einsum('bqhn,chn->bqhc', q_nope, w_uk)
    s = (jnp.einsum('bqhc,bkc->bhqk', q_abs, lat)
         + jnp.einsum('bqhr,bkr->bhqk', q_pe, kpe)).astype(jnp.float32) * MLA_SCALE
    p = jax.nn.softmax(s, axis=-1).astype(lat.dtype)
    o_lat = jnp.einsum('bhqk,bkc->bqhc', p, lat)
    o = jnp.einsum('bqhc,chv->bqhv', o_lat, w_uv)
    return o.reshape(B, Q, MLA_HEADS * MLA_V_DIM)

def sink_attention(q, k, v, rel, valid, sinks, slopes):
    s = jnp.einsum('bnqhgd,bnkhd->bnhgqk', q, k).astype(jnp.float32) * SWA_SCALE
    s = s - slopes.reshape(SWA_KV_HEADS, SWA_GROUP, 1, 1) * jnp.abs(rel).astype(jnp.float32)
    if valid is not None:
        s = jnp.where(valid[None, :, None, None], s, NEG_INF)
    sink = jnp.broadcast_to(sinks.astype(jnp.float32).reshape(SWA_KV_HEADS, SWA_GROUP, 1, 1),
                            s.shape[:-1] + (1,))
    p = jax.nn.softmax(jnp.concatenate([s, sink], axis=-1), axis=-1)[..., :-1]
    return jnp.einsum('bnhgqk,bnkhd->bnqhgd', p.astype(v.dtype), v)

def swa_prompt(q, k, v, sinks, slopes):
    B, S = q.shape[:2]
    nC = S // CHUNK
    pad = jnp.zeros((B, WINDOW, SWA_KV_HEADS, SWA_HEAD_DIM), k.dtype)
    kp = jnp.concatenate([pad, k], axis=1).reshape(B, nC + WINDOW_CHUNKS, CHUNK, SWA_KV_HEADS, SWA_HEAD_DIM)
    vp = jnp.concatenate([pad, v], axis=1).reshape(B, nC + WINDOW_CHUNKS, CHUNK, SWA_KV_HEADS, SWA_HEAD_DIM)
    kb = jnp.concatenate([kp[:, j:j + nC] for j in range(WINDOW_CHUNKS + 1)], axis=2)
    vb = jnp.concatenate([vp[:, j:j + nC] for j in range(WINDOW_CHUNKS + 1)], axis=2)
    qb = q.reshape(B, nC, CHUNK, SWA_KV_HEADS, SWA_GROUP, SWA_HEAD_DIM)
    rel = jnp.arange(CHUNK)[:, None] + WINDOW - jnp.arange(BAND)[None, :]
    key_pos = jnp.arange(nC)[:, None] * CHUNK - WINDOW + jnp.arange(BAND)[None, :]
    valid = jnp.broadcast_to((key_pos >= 0)[:, None, :], (nC, CHUNK, BAND))
    o = sink_attention(qb, kb, vb, rel, valid, sinks, slopes)
    return o.reshape(B, S, SWA_HEADS * SWA_HEAD_DIM)

def swa_sample(q, k_all, v_all, n_cached, sinks, slopes):
    B, Q = q.shape[:2]
    rel = jnp.arange(Q)[:, None] + n_cached - jnp.arange(n_cached + Q)[None, :]
    o = sink_attention(q[:, None], k_all[:, None], v_all[:, None], rel, None, sinks, slopes)
    return o.reshape(B, Q, SWA_HEADS * SWA_HEAD_DIM)

def clamped_swiglu(gu):
    glu = jnp.minimum(gu[..., :D_FF], SWIGLU_LIMIT)
    lin = jnp.clip(gu[..., D_FF:], -SWIGLU_LIMIT, SWIGLU_LIMIT)
    return glu * jax.nn.sigmoid(SWIGLU_ALPHA * glu) * (lin + 1)

def moe_ffn(h, w_router, b_router, w_gate_up, b_gate_up, w_down, b_down):
    T, D = h.shape
    logits = (h @ w_router + b_router).astype(jnp.float32)
    top_val, top_idx = lax.top_k(logits, TOP_K)
    gate = jax.nn.softmax(top_val, axis=-1)
    n_assign = T * TOP_K
    flat_e = top_idx.reshape(n_assign)
    order = jnp.argsort(flat_e)
    sorted_e = flat_e[order]
    counts = jnp.bincount(flat_e, length=N_EXPERTS)
    padded = (counts + MOE_BLOCK - 1) // MOE_BLOCK * MOE_BLOCK
    pad_end = jnp.cumsum(padded)
    pad_start = pad_end - padded
    start = jnp.cumsum(counts) - counts
    dest = pad_start[sorted_e] + jnp.arange(n_assign) - start[sorted_e]
    n_blocks = -(-(n_assign + N_EXPERTS * (MOE_BLOCK - 1)) // MOE_BLOCK)
    n_slots = n_blocks * MOE_BLOCK
    slot_tok = jnp.zeros((n_slots,), jnp.int32).at[dest].set((order // TOP_K).astype(jnp.int32))
    slot_w = jnp.zeros((n_slots,), jnp.float32).at[dest].set(gate.reshape(n_assign)[order])
    block_e = jnp.minimum(jnp.searchsorted(pad_end, jnp.arange(n_blocks) * MOE_BLOCK, side='right'),
                          N_EXPERTS - 1)

    def expert_block(args):
        tok, e = args
        gu = h[tok] @ w_gate_up[e] + b_gate_up[e]
        return clamped_swiglu(gu) @ w_down[e] + b_down[e]

    y = lax.map(expert_block, (slot_tok.reshape(n_blocks, MOE_BLOCK), block_e)).reshape(n_slots, D)
    y = y * slot_w[:, None].astype(y.dtype)
    return jnp.zeros_like(h).at[slot_tok].add(y)

def ffn_sublayer(x, shift, scale, gate, g_norm, w_router, b_router, w_gate_up, b_gate_up, w_down, b_down):
    B, S, D = x.shape
    h = modulate(rms_norm(x, g_norm), shift, scale).reshape(B * S, D)
    y = moe_ffn(h, w_router, b_router, w_gate_up, b_gate_up, w_down, b_down).reshape(B, S, D)
    return x + gate * y

def setup_inputs(seed: int = 0) -> dict:
    key = jax.random.key(seed)
    ks = jax.random.split(key, 26)
    f32 = jnp.float32
    nrm = lambda k, shape, s: jax.random.normal(k, shape, f32) * s
    swa_len = min(WINDOW, PAST_LEN)
    return {
        'x_prompt': nrm(ks[0], (BATCH, SEQ, D_MODEL), 1.0),
        'x_sample': nrm(ks[1], (DEC_BATCH, DEC_SEQ, D_MODEL), 1.0),
        'c_prompt': nrm(ks[2], (BATCH, D_MODEL), 1.0),
        'c_sample': nrm(ks[3], (DEC_BATCH, D_MODEL), 1.0),
        'cache_mla_latent': nrm(ks[4], (DEPTH, DEC_BATCH, PAST_LEN, MLA_KV_LORA), 1.0),
        'cache_mla_krope': nrm(ks[5], (DEPTH, DEC_BATCH, PAST_LEN, MLA_ROPE_DIM), 1.0),
        'cache_swa_k': nrm(ks[6], (DEPTH, DEC_BATCH, swa_len, SWA_KV_HEADS, SWA_HEAD_DIM), 1.0),
        'cache_swa_v': nrm(ks[7], (DEPTH, DEC_BATCH, swa_len, SWA_KV_HEADS, SWA_HEAD_DIM), 1.0),
        'w_ada': nrm(ks[8], (DEPTH, D_MODEL, 6 * D_MODEL), 0.5 * D_MODEL ** -0.5),
        'b_ada': nrm(ks[9], (DEPTH, 6 * D_MODEL), 0.02),
        'g_attn_norm': 1.0 + nrm(ks[10], (DEPTH, D_MODEL), 0.02),
        'w_in': nrm(ks[11], (DEPTH, D_MODEL, IN_WIDTH), D_MODEL ** -0.5),
        'g_q_norm': 1.0 + nrm(ks[12], (DEPTH, MLA_Q_LORA), 0.02),
        'w_uq': nrm(ks[13], (DEPTH, MLA_Q_LORA, MLA_HEADS, MLA_NOPE_DIM + MLA_ROPE_DIM), MLA_Q_LORA ** -0.5),
        'g_kv_norm': 1.0 + nrm(ks[14], (DEPTH, MLA_KV_LORA), 0.02),
        'w_ukv': nrm(ks[15], (DEPTH, MLA_KV_LORA, MLA_HEADS, MLA_NOPE_DIM + MLA_V_DIM), MLA_KV_LORA ** -0.5),
        'swa_sinks': nrm(ks[16], (DEPTH, SWA_HEADS), 0.5),
        'w_out': nrm(ks[17], (DEPTH, MIX_WIDTH, D_MODEL), MIX_WIDTH ** -0.5),
        'g_ffn_norm': 1.0 + nrm(ks[18], (DEPTH, D_MODEL), 0.02),
        'w_router': nrm(ks[19], (DEPTH, D_MODEL, N_EXPERTS), D_MODEL ** -0.5),
        'b_router': nrm(ks[20], (DEPTH, N_EXPERTS), 0.01),
        'w_gate_up': nrm(ks[21], (DEPTH, N_EXPERTS, D_MODEL, 2 * D_FF), D_MODEL ** -0.5),
        'b_gate_up': nrm(ks[22], (DEPTH, N_EXPERTS, 2 * D_FF), 0.02),
        'w_down': nrm(ks[23], (DEPTH, N_EXPERTS, D_FF, D_MODEL), D_FF ** -0.5),
        'b_down': nrm(ks[24], (DEPTH, N_EXPERTS, D_MODEL), 0.02),
        'g_final': 1.0 + nrm(ks[25], (D_MODEL,), 0.02),
    }

def reference(x_prompt, x_sample, c_prompt, c_sample, cache_mla_latent, cache_mla_krope,
              cache_swa_k, cache_swa_v, w_ada, b_ada, g_attn_norm, w_in, g_q_norm, w_uq,
              g_kv_norm, w_ukv, swa_sinks, w_out, g_ffn_norm, w_router, b_router,
              w_gate_up, b_gate_up, w_down, b_down, g_final):
    slopes = alibi_slopes()
    S = x_prompt.shape[1]
    Q = x_sample.shape[1]
    past = cache_mla_latent.shape[2]
    n_win = cache_swa_k.shape[2]
    keep_p = min(WINDOW, S)
    pos_p = jnp.arange(S)
    pos_s = past + jnp.arange(Q)
    xp, xs = x_prompt, x_sample
    lat_p, pe_p, swk_p, swv_p = [], [], [], []
    lat_s, pe_s, swk_s, swv_s = [], [], [], []
    for l in range(DEPTH):
        sh_ap, sc_ap, gt_ap, sh_fp, sc_fp, gt_fp = adaln(c_prompt, w_ada[l], b_ada[l])
        sh_as, sc_as, gt_as, sh_fs, sc_fs, gt_fs = adaln(c_sample, w_ada[l], b_ada[l])

        hp = modulate(rms_norm(xp, g_attn_norm[l]), sh_ap, sc_ap)
        qn, qpe, ckv, kpe, qs, ks, vs = mixer_inputs(hp, pos_p, w_in[l], g_q_norm[l], w_uq[l],
                                                     g_kv_norm[l], w_ukv[l])
        o = jnp.concatenate([mla_prompt(qn, qpe, ckv, kpe, w_ukv[l]),
                             swa_prompt(qs, ks, vs, swa_sinks[l], slopes)], axis=-1)
        xp = xp + gt_ap * (o @ w_out[l])
        lat_p.append(ckv)
        pe_p.append(kpe)
        swk_p.append(ks[:, S - keep_p:])
        swv_p.append(vs[:, S - keep_p:])

        hs = modulate(rms_norm(xs, g_attn_norm[l]), sh_as, sc_as)
        qn, qpe, ckv, kpe, qs, ks, vs = mixer_inputs(hs, pos_s, w_in[l], g_q_norm[l], w_uq[l],
                                                     g_kv_norm[l], w_ukv[l])
        lat_all = jnp.concatenate([cache_mla_latent[l], ckv], axis=1)
        pe_all = jnp.concatenate([cache_mla_krope[l], kpe], axis=1)
        k_all = jnp.concatenate([cache_swa_k[l], ks], axis=1)
        v_all = jnp.concatenate([cache_swa_v[l], vs], axis=1)
        o = jnp.concatenate([mla_sample(qn, qpe, lat_all, pe_all, w_ukv[l]),
                             swa_sample(qs, k_all, v_all, n_win, swa_sinks[l], slopes)], axis=-1)
        xs = xs + gt_as * (o @ w_out[l])
        lat_s.append(ckv)
        pe_s.append(kpe)
        swk_s.append(k_all[:, -n_win:])
        swv_s.append(v_all[:, -n_win:])

        xp = ffn_sublayer(xp, sh_fp, sc_fp, gt_fp, g_ffn_norm[l], w_router[l], b_router[l],
                          w_gate_up[l], b_gate_up[l], w_down[l], b_down[l])
        xs = ffn_sublayer(xs, sh_fs, sc_fs, gt_fs, g_ffn_norm[l], w_router[l], b_router[l],
                          w_gate_up[l], b_gate_up[l], w_down[l], b_down[l])

    y_prompt = rms_norm(xp, g_final)
    y_sample = rms_norm(xs, g_final)
    new_mla_latent_prompt = jnp.stack(lat_p)
    new_mla_krope_prompt = jnp.stack(pe_p)
    new_swa_k_prompt = jnp.stack(swk_p)
    new_swa_v_prompt = jnp.stack(swv_p)
    new_mla_latent_sample = jnp.stack(lat_s)
    new_mla_krope_sample = jnp.stack(pe_s)
    new_swa_k_sample = jnp.stack(swk_s)
    new_swa_v_sample = jnp.stack(swv_s)
    return (y_prompt, y_sample, new_mla_latent_prompt, new_mla_krope_prompt, new_swa_k_prompt,
            new_swa_v_prompt, new_mla_latent_sample, new_mla_krope_sample, new_swa_k_sample,
            new_swa_v_sample)


_drawn_inputs = setup_inputs


def setup_inputs(seed=0):
    import zlib

    import numpy as np

    out = dict(_drawn_inputs(seed))
    spreads = {}
    factors = {'cache_mla_krope': 3.282,
     'g_attn_norm': 2.979,
     'g_q_norm': 8.0,
     'g_kv_norm': 2.907,
     'swa_sinks': 45.912,
     'g_ffn_norm': 2.985,
     'b_router': 4.067,
     'b_gate_up': 8.0,
     'b_down': 25.39,
     'g_final': 7.779}
    for name, (base, spread) in spreads.items():
        noise = np.random.default_rng([zlib.crc32(name.encode()), seed]).standard_normal(out[name].shape)
        drawn = base * np.exp(spread * noise) if base else spread * noise
        out[name] = __import__('jax').numpy.asarray(drawn.astype(out[name].dtype))
    for name, factor in factors.items():
        out[name] = (out[name] * factor).astype(out[name].dtype)
    return out
```

```python
from contextlib import ExitStack

import numpy as np

import concourse.bass as bass
from concourse import mybir

F32 = mybir.dt.float32
BF16 = mybir.dt.bfloat16
I32 = mybir.dt.int32
U32 = mybir.dt.uint32
ALU = mybir.AluOpType
ACT = mybir.ActivationFunctionType
AX = mybir.AxisListType.X

P = 128
D = 1024
KT = D // P
SEQ, NB_DEC, Q_DEC, PAST = 256, 8, 16, 512
NT = 3
NP_T = 2
CHUNK, WINDOW = 64, 128
H, NOPE, ROPE, VD = 8, 64, 32, 64
QK = NOPE + ROPE
QL, KVL = 384, 256
KVH, GRP, HD = 2, 4, 64
IN_W = QL + KVL + ROPE + H * HD + 2 * KVH * HD
O_KV, O_KPE, O_QS = QL, QL + KVL, QL + KVL + ROPE
O_KS = O_QS + H * HD
O_VS = O_KS + KVH * HD
MLA_SCALE = float(QK) ** -0.5
SWA_SCALE = float(HD) ** -0.5
NE, TOPK = 32, 4
DFF = D
EPS = 1e-6
BIG = 1e30

UNIT = 2048
SLOTS = 6
IN_COLS = IN_W // 6
OUT_COLS = 256
N_MOD = 6 * D // 512
EARLY_MOD = 6
MOE_UNITS = 12
NOVF = NT * P * TOPK // (P + 1)
NBLK = NE + NOVF + 1

QUERY_ORDER = (("q", 0), ("q", 1), ("qT", 0), ("q", 2), ("qT", 1), ("qT", 2))

OUT_SHAPES = [
    (1, SEQ, D), (NB_DEC, Q_DEC, D),
    (1, 1, SEQ, KVL), (1, 1, SEQ, ROPE), (1, 1, WINDOW, KVH, HD), (1, 1, WINDOW, KVH, HD),
    (1, NB_DEC, Q_DEC, KVL), (1, NB_DEC, Q_DEC, ROPE),
    (1, NB_DEC, WINDOW, KVH, HD), (1, NB_DEC, WINDOW, KVH, HD),
]


def shape_constants():
    c = {}
    c["ident"] = np.eye(P, dtype=np.float32)
    pos = np.concatenate([np.arange(SEQ), np.tile(PAST + np.arange(Q_DEC), NB_DEC)]).astype(np.float32)
    inv = np.float32(10000.0) ** (-np.arange(ROPE // 2, dtype=np.float32) * np.float32(2.0) / np.float32(ROPE))
    ang = (pos[:, None] * inv[None, :]).astype(np.float32)
    cs = np.concatenate([np.cos(ang), np.sin(ang)], axis=1).astype(np.float32)
    c["rope"] = np.ascontiguousarray(cs.reshape(NT, P, ROPE).transpose(1, 0, 2))
    q = np.arange(SEQ)
    qc, kc = q[:, None] // CHUNK, q[None, :] // CHUNK
    mask = np.where(kc <= qc, 0.0, -BIG).astype(np.float32)
    c["causal"] = np.ascontiguousarray(mask.reshape(NP_T, P, SEQ).transpose(1, 0, 2))
    seen = (kc <= qc) & (kc >= qc - WINDOW // CHUNK)
    dist = np.where(seen, np.abs(q[:, None] - q[None, :]), BIG * 1e4).astype(np.float32)
    c["dist"] = np.ascontiguousarray(dist.reshape(NP_T, P, SEQ).transpose(1, 0, 2))
    slope = 2.0 ** (-8.0 * np.arange(1, H + 1) / H)
    rel = np.abs(np.arange(Q_DEC)[:, None] + WINDOW - np.arange(WINDOW + Q_DEC)[None, :])
    c["alibi"] = (-slope[:, None, None] * rel[None] / SWA_SCALE).reshape(P, WINDOW + Q_DEC).astype(np.float32)
    sel = np.zeros((96, 2, P), np.float32)
    for part in range(3):
        sel[32 * part, 0, :] = 1.0
        for t in range(P):
            sel[32 * part + 1 + t // Q_DEC, 1, t] = 1.0
    c["kind_sel"] = sel
    tri = np.zeros((P, 2, P), np.float32)
    tri[:, 0, :] = np.triu(np.ones((P, P)), 1)
    tri[:, 1, :] = 1.0
    c["before"] = tri
    c["expert_id"] = np.tile(np.arange(NE, dtype=np.float32), (P, 1))
    c["row_expert"] = np.tile((np.arange(96) % 32).astype(np.float32)[:, None], (1, P))
    c["block_id"] = np.tile(np.arange(NOVF, dtype=np.float32)[:, None], (1, NE)).reshape(1, -1).repeat(P, 0)
    c["token_id"] = (np.arange(NT)[None, :] * P + np.arange(P)[:, None]).astype(np.int32)
    return c


def psum_jobs():
    early = [(("mod", n), "v") for n in range(4)]
    early += [(("b" + w, k, f), "v") for k in range(2) for f in range(2) for w in ("scale", "shift")]
    early += [(("hT", t, g), "a") for t in range(NT) for g in range(2)]
    early += [(("u", j, t), "a") for j in range(6) for t in range(NT)]
    early += [(("mod", n), "v") for n in range(4, EARLY_MOD)]
    early += [(("qlT", t), "a") for t in range(NT)]
    early += [(("ckT", t), "a") for t in range(NT)]
    early += [(("qsT", t), "a") for t in range(NT)] + [(("ksT",), "a")]
    early += [(("gate", k, f), "a") for k in range(2) for f in range(2)]
    early += [(("v", t), "a") for t in range(NP_T)]
    early += [((w, t, f), "v" if w == "q" else "a") for w, t in QUERY_ORDER for f in range(2)]
    early += [(("qabs", p), "a") for p in range(4)] + [(("kT", p), "a") for p in range(4)]
    late = [(("oS",), "a")]
    late += [(("o", j, t), "v") for j in range(4) for t in range(NT)]
    late += [(("fgate", k, f), "a") for k in range(2) for f in range(2)]
    late += [(("f" + w, k, f), "v") for k in range(2) for f in range(2) for w in ("scale", "shift")]
    late += [(("fT", t, g), "a") for t in range(NT) for g in range(2)]
    late += [(("logit", t), "v") for t in range(NT)]
    late += [(("rank", t), "v") for t in range(NT)] + [(("count",), "v")]
    return early, late


def attention_items():
    items = []
    for b in range(NB_DEC):
        for j in (2 * b, 2 * b + 1):
            items += [("mla", j // H, j % H), ("swa", j // H, j % H)]
        items += [("mla_s", b, 0), ("swa_s", b, 0)]
    return items



def build(nc, ins, outs):
    (x_in, c_t, cache_lat, cache_lat_t, cache_kr_t, cache_k_t, cache_v, cache_k_rows, ada_w, ada_rows,
     in_w, uq_w, ukv_w, uk_t, out_w, rows_q_kv, sink_cols, router_w, router_b, moe_w, moe_b, g_final,
     c_ident, c_rope, c_causal, c_dist, c_alibi, c_kind, c_before, c_eid, c_rowe, c_blk, c_tok) = ins
    (o_yp, o_ys, o_latp, o_krp, o_kp, o_vp, o_lats, o_krs, o_ks, o_vs) = outs
    stack = ExitStack()

    def sb(name, shape, dt=F32, scope=stack):
        return scope.enter_context(nc.sbuf_tensor(name, shape, dt))

    def sem(name):
        return stack.enter_context(nc.semaphore(name))

    h_rows = nc.dram_tensor("h_rows", [NT * P, D], F32, kind="Internal").ap()
    slot_tok_dram = nc.dram_tensor("slot_tok_dram", [P * NBLK, 1], I32, kind="Internal").ap()
    y_rows = nc.dram_tensor("y_rows", [(NBLK - 1) * P, D], F32, kind="Internal").ap()

    ps = stack.enter_context(nc.psum_tensor("ps", [P, 8, 512], F32))

    ring = sb("ring", [P, SLOTS, UNIT])
    x = sb("x", [P, NT, D])
    mod_parts = sb("mod_parts", [96, 6 * D], BF16)
    gates = sb("gates", [P, 2, D])
    ident = sb("ident", [P, P])
    kind_sel = sb("kind_sel", [96, 2, P], BF16)
    before = sb("before", [P, 2, P], BF16)
    expert_id = sb("expert_id", [P, NE])
    row_expert = sb("row_expert", [96, P])
    block_id = sb("block_id", [P, NOVF, NE])
    token_id = sb("token_id", [P, NT], I32)
    gate_w = sb("gate_w", [P, NT, TOPK])
    y_row_idx = sb("y_row_idx", [P, NT * TOPK], I32)
    tok_addr = sb("tok_addr", [P, NT * TOPK], I32)
    slot_tok = sb("slot_tok", [P, NBLK], I32)
    block_expert = sb("block_expert", [P, NBLK])
    ovf_table = sb("ovf_table", [1, NOVF + 1], I32)
    stat = sb("stat", [P, 64])

    pre = ExitStack()

    def pb(name, shape, dt=F32):
        return sb(name, shape, dt, pre)

    hm = pb("hm", [P, KT, NT * P])
    hq = pb("hq", [P, NT * D])
    qabs = pb("qabs", [P, 2, NB_DEC, H, Q_DEC])
    kT = pb("kT", [QK, H, SEQ])
    w_ukv = pb("w_ukv", [P, 2, H, NOPE + VD])
    v_p = pb("v_p", [P, NP_T, H * VD])
    v_swa = pb("v_swa", [P, NT, KVH * HD])
    qsT = pb("qsT", [P, NP_T, GRP, P])
    qsT_s = pb("qsT_s", [P, NB_DEC, GRP, Q_DEC])
    ksT = pb("ksT", [P, NT * P])
    ckT = pb("ckT", [P, 2, NT * P])
    kpT = pb("kpT", [QK, NT * P])
    q_tok = pb("q_tok", [P, H, QK])
    rope = pb("rope", [P, NT, ROPE])
    rt = pb("rt", [P, 4, 96])
    causal = pb("causal", [P, NP_T, SEQ])
    dist = pb("dist", [P, NP_T, SEQ])
    alibi = pb("alibi", [P, WINDOW + Q_DEC])
    g_qkv = pb("g_qkv", [P, QL + KVL])
    sinks = pb("sinks", [P, H + 1])
    sinks_s = pb("sinks_s", [P, H + 1])
    w_rt = pb("w_rt", [P, KT, NE])
    b_rt = pb("b_rt", [P, NE])
    cT = pb("cT", [P, KT, 9])
    cs = pb("cs", [P, KT, 9])
    mod_rows = pb("mod_rows", [9, 2, 512])
    mod_row = pb("mod_row", [9, 512])
    mod_res = pb("mod_res", [9, 512])
    mod_p2 = pb("mod_p2", [9, 512], BF16)
    row_max = pb("row_max", [P, 48])
    neg_max = pb("neg_max", [P, 48])
    row_sum = pb("row_sum", [P, 48])
    sink_e = pb("sink_e", [P, 48])
    row_inv = pb("row_inv", [P, 48])
    rtr = pb("rtr", [P, 12, NE])
    h = hq[:, :].rearrange("p (t d) -> p t d", t=NT)
    qT = hq[0:QK, 0:NP_T * H * P].rearrange("p (t h n) -> p t h n", t=NP_T, h=H)
    qT_s = hq[0:QK, NP_T * H * P:].rearrange("p (b h q) -> p b h q", b=NB_DEC, h=H)
    hT = hm
    mixT = hm
    w_uq = hm[:, :, :].rearrange("p k t -> p (k t)")[:, 0:3 * H * QK].rearrange("p (k n) -> p k n", k=3)
    qlT = qabs[:, :, :, :, :].rearrange("p a b h q -> p (a b h q)")[:, 0:3 * NT * P].rearrange(
        "p (k t) -> p k t", k=3)
    wukT = kT[0:NOPE, :, :]
    q_flat = q_tok[:, :, :].rearrange("p h d -> p (h d)")
    cv_s = q_flat[:, 0:2 * P].rearrange("p (b n) -> p b n", b=2)
    new_v = q_flat[0:Q_DEC, 2 * P:4 * P].rearrange("p (b n) -> p b n", b=2)
    tail_base = nc.sbuf_base

    su = ExitStack()
    u = sb("u", [P, NT, IN_W], F32, su)
    su.close()

    att = ExitStack()
    latT = sb("latT", [P, 2, 2, PAST], F32, att)
    lat = sb("lat", [P, 2, PAST // P, KVL], F32, att)
    krT = sb("krT", [QK, 2, PAST], F32, att)
    ck_sT = sb("ck_sT", [P, 2, WINDOW], F32, att)
    new_lat = sb("new_lat", [Q_DEC, 2, KVL], F32, att)
    probs = sb("probs", [P, 2, PAST + Q_DEC], F32, att)
    pT = sb("pT", [P, 2, 5 * P], F32, att)
    att.close()

    late = ExitStack()
    bias_parts = sb("bias_parts", [96, 3 * D], BF16, late)
    bias_src = sb("bias_src", [NE, 3 * D], F32, late)
    bias_p2 = sb("bias_p2", [NE, 3 * D], BF16, late)
    late.close()
    pre.close()

    moe = ExitStack()
    x_slots = sb("x_slots", [P, D], F32, moe)
    x_slotsT = sb("x_slotsT", [P, KT, P], F32, moe)
    glu = sb("glu", [P, 2, 512], F32, moe)
    sig = sb("sig", [P, 2, 512], F32, moe)
    lin = sb("lin", [P, 2, 512], F32, moe)
    gsg = sb("gsg", [P, 2, 512], F32, moe)
    act = sb("act", [P, 2, 512], F32, moe)
    actT = sb("actT", [P, KT, P], F32, moe)
    y_blk = sb("y_blk", [P, D], F32, moe)
    sel_e = sb("sel_e", [96, P], BF16, moe)
    cur_idx = sb("cur_idx", [P, 1], I32, moe)
    y_got = sb("y_got", [P, 4, D], F32, moe)
    y_acc = sb("y_acc", [P, D], F32, moe)
    gfin = sb("gfin", [P, D], F32, moe)
    assert nc.sbuf_base <= tail_base
    moe.close()

    S = {}
    for name in (
            "loaded_c loaded_x loaded_small loaded_uq loaded_rows loaded_bias loaded_gfin "
            "psum_filled v_emptied a_emptied unit_used v_step a_step p_step zeroed consts_cast "
            "sig_ready silu_ready ss_ready ms_ready root_ready parts_ready h_done ql_ready ck_ready u_stats "
            "lat_stored out_stored slot_zeroed rows_zeroed v_swa_ready "
            "scored maxed exped normed flipped pT_ready pv_done o_ready mod_extra mod_extra_used caches_ready "
            "x1_ready h_ready bias_ready logits_exp gates_exped probs_top routed h_stored scattered slots_back table_ready "
            "sel_ready bias_done gu_emptied glu_ready sig_done act_ready actT_filled actT_ready "
            "xT_filled xT_ready gathered idx_ready y_copied y_stored x_flip "
            "got0 got1 got2 got3 acc_done fin_ss fin_root fin_ready fin_ms fin_stored gsg_ready pool_gate").split():
        S[name] = sem(name)
    slot_sem = [sem(f"slot_full{s}") for s in range(SLOTS)]
    cache_sem = [sem(f"cache_full{s}") for s in range(2)]
    (x_sem, ) = (S["loaded_x"], )

    early, late_jobs = psum_jobs()
    jobs = early + late_jobs
    number = {key: i for i, (key, _) in enumerate(jobs)}
    engine_of = dict(jobs)
    ordinal, seen = {}, {"v": 0, "a": 0}
    for key, who in jobs:
        seen[who] += 1
        ordinal[key] = seen[who]

    def bank(*key):
        return ps[:, number[key] % 8, :]

    def filled(eng, *key):
        eng.wait_ge(S["psum_filled"], number[key] + 1)

    def emptied(eng, *key):
        eng.wait_ge(S["v_emptied"] if engine_of[key] == "v" else S["a_emptied"], ordinal[key])

    n_early = {w: sum(1 for _, e in early if e == w) for w in "va"}
    n_all = {w: sum(1 for _, e in jobs if e == w) for w in "va"}

    units = [("ada", n, f) for n in range(4) for f in range(2)]
    units += [("in", j) for j in range(6)]
    units += [("ada", n, f) for n in range(4, N_MOD) for f in range(2)]
    units += [("out", j) for j in range(4)]
    unit_no = {k: i for i, k in enumerate(units)}
    N_PRE = len(units)
    HALVES = N_MOD

    def unit(key):
        return ring[:, unit_no[key] % SLOTS, :]

    def unit_here(eng, key):
        n = unit_no[key]
        eng.wait_ge(slot_sem[n % SLOTS], 16 * (n // SLOTS + 1))

    def used_up(eng, key):
        if key[0] == "ada" and key[2] == 0:
            eng.wait_ge(S["unit_used"], key[1] + 1)
        elif key[0] == "ada" and key[1] < EARLY_MOD:
            filled(eng, "mod", key[1])
        elif key[0] == "ada":
            eng.wait_ge(S["mod_extra"], key[1] - EARLY_MOD + 1)
        else:
            filled(eng, "u" if key[0] == "in" else "o", key[1], NT - 1)

    def moe_slot(j):
        return (N_PRE + j) % SLOTS

    def moe_full(i, j):
        return ((N_PRE + j) // SLOTS + 1) * 16 + i * (16 * MOE_UNITS // SLOTS)

    items = attention_items()

    def width(i):
        kind, n, _ = items[i]
        return {"mla": P * (n + 1), "swa": P * (n + 1), "mla_s": PAST + Q_DEC, "swa_s": WINDOW + Q_DEC}[kind]

    def full_tiles(i):
        kind, n, _ = items[i]
        return {"mla": n + 1, "swa": n + 1, "mla_s": PAST // P, "swa_s": 1}[kind]

    def scores(i):
        return ps[:, 2 * (i % 2):2 * (i % 2) + 2, :].rearrange("p a b -> p (a b)")

    block = stack.enter_context(nc.Block())

    @block.sync
    def _(sp):
        for n, key in enumerate(units):
            if n >= SLOTS:
                used_up(sp, units[n - SLOTS])
            if key[0] == "ada":
                src, dst = ada_w[key[1], key[2]], ring[:, n % SLOTS, :]
            elif key[0] == "in":
                src, dst = in_w[key[1]], ring[:, n % SLOTS, 0:KT * IN_COLS]
            else:
                src, dst = out_w[key[1]], ring[:, n % SLOTS, :]
            nc.sync.dma_start(dst, src).then_inc(slot_sem[n % SLOTS], 16)

        def stream(i, expert):
            for j in range(MOE_UNITS):
                sp.wait_ge(S["unit_used"], i * MOE_UNITS + (HALVES + j - SLOTS + 1))
                src = moe_w[bass.ds(expert, 1), j].rearrange("e p n -> (e p) n")
                nc.sync.dma_start(ring[:, moe_slot(j), :], src).then_inc(slot_sem[moe_slot(j)], 16)

        used_up(sp, units[-1])
        with sp.Fori(0, NE) as i:
            stream(i, i)
        sp.wait_ge(S["table_ready"], 1)
        n_ovf = sp.value_load(ovf_table[0:1, NOVF:NOVF + 1], min_val=0, max_val=NOVF)
        with sp.If(n_ovf > 0):
            with sp.Fori(NE, n_ovf + NE) as i:
                expert = sp.value_load(ovf_table[0:1, bass.ds(i - NE, 1)], min_val=0, max_val=NE - 1)
                stream(i, expert)

    @block.gpsimd
    def _(pool):
        pool.wait_ge(S["loaded_small"], 16 * 4)
        qf = q_tok[:, :, :].rearrange("p h d -> p (h d)")
        nc.gpsimd.tensor_copy(kind_sel[:, :, :].rearrange("p a b -> p (a b)"), qf[0:96, 0:2 * P]).then_inc(S["consts_cast"], 1)
        nc.gpsimd.tensor_copy(before[:, :, :].rearrange("p a b -> p (a b)"), qf[:, 2 * P:4 * P]).then_inc(S["consts_cast"], 1)
        nc.gpsimd.memset(slot_tok[:, :], 0).then_inc(S["zeroed"], 1)
        pool.wait_ge(S["zeroed"], 1)
        nc.gpsimd.dma_start(slot_tok_dram.rearrange("(p n) o -> p (n o)", p=P), slot_tok[:, :]).then_inc(
            S["slot_zeroed"], 16)

        zeros = qabs[:, :, :, :, :].rearrange("p a b h q -> p (a b h q)")[:, 0:D]
        nc.gpsimd.memset(zeros, 0.0).then_inc(S["zeroed"], 1)
        pool.wait_ge(S["zeroed"], 2)
        for n in range(NE, NBLK - 1):
            nc.gpsimd.dma_start(y_rows[n * P:(n + 1) * P, :], zeros).then_inc(S["rows_zeroed"], 16)

        for n in range(N_MOD):
            if n == 4:
                nc.gpsimd.dma_start(o_ks[0, :, 0:WINDOW - Q_DEC].rearrange("b t k d -> b t (k d)"),
                                    cache_k_rows[:, Q_DEC:WINDOW]).then_inc(S["out_stored"], 16)
                nc.gpsimd.dma_start(o_vs[0, :, 0:WINDOW - Q_DEC].rearrange("b t k d -> b t (k d)"),
                                    cache_v[:, Q_DEC:WINDOW]).then_inc(S["out_stored"], 16)
            if n == EARLY_MOD:
                break
            if n:
                pool.wait_ge(S["parts_ready"], n)
            nc.gpsimd.dma_start(mod_rows[:, :, :], ada_rows[n]).then_inc(S["loaded_rows"], 16)

        filled(pool, "u", 5, NT - 1)
        nc.gpsimd.dma_start(w_uq, uq_w).then_inc(S["loaded_uq"], 16)

        pool.wait_ge(S["ck_ready"], 1)
        for t in range(NP_T):
            nc.gpsimd.dma_start(o_latp[0, 0, t * P:(t + 1) * P], u[:, t, O_KV:O_KPE]).then_inc(S["out_stored"], 16)
            nc.gpsimd.dma_start(o_krp[0, 0, t * P:(t + 1) * P], u[:, t, O_KPE:O_QS]).then_inc(S["out_stored"], 16)
        nc.gpsimd.dma_start(o_kp[0, 0].rearrange("t k d -> t (k d)"), u[:, 1, O_KS:O_VS]).then_inc(S["out_stored"], 16)
        nc.gpsimd.dma_start(o_vp[0, 0].rearrange("t k d -> t (k d)"), u[:, 1, O_VS:IN_W]).then_inc(S["out_stored"], 16)
        nc.gpsimd.dma_start(o_krs[0].rearrange("b q c -> (b q) c"), u[:, 2, O_KPE:O_QS]).then_inc(S["out_stored"], 16)
        nc.gpsimd.dma_start(o_lats[0].rearrange("b q c -> (b q) c"), u[:, 2, O_KV:O_KPE]).then_inc(S["lat_stored"], 16)
        for b in range(NB_DEC):
            rows = slice(b * Q_DEC, (b + 1) * Q_DEC)
            nc.gpsimd.dma_start(o_ks[0, b, WINDOW - Q_DEC:WINDOW].rearrange("t k d -> t (k d)"),
                                u[rows, 2, O_KS:O_VS]).then_inc(S["out_stored"], 16)
            nc.gpsimd.dma_start(o_vs[0, b, WINDOW - Q_DEC:WINDOW].rearrange("t k d -> t (k d)"),
                                u[rows, 2, O_VS:IN_W]).then_inc(S["lat_stored"], 16)
        n_out = 2 + 2 * NP_T + 3 + NB_DEC

        pool.wait_ge(S["out_stored"], 16 * n_out)
        pool.wait_ge(S["lat_stored"], 16 * (1 + NB_DEC))
        pool.wait_ge(S["v_swa_ready"], 1)
        filled(pool, "ksT")
        filled(pool, "ckT", NT - 1)
        filled(pool, "qlT", NT - 1)
        filled(pool, "qsT", NT - 1)
        filled(pool, "qT", NT - 1, 1)
        for b in range(NB_DEC):
            if b >= 2:
                pool.wait_ge(S["pv_done"], 6 * (b - 1))
            k = b % 2
            for dst, src in ((latT[:, k], cache_lat_t[b]), (lat[:, k], cache_lat[b]),
                             (krT[NOPE:QK, k], cache_kr_t[b]), (ck_sT[:, k], cache_k_t[b]), (cv_s[:, k], cache_v[b]),
                             (new_lat[:, k], o_lats[0, b]),
                             (new_v[:, k], o_vs[0, b, WINDOW - Q_DEC:WINDOW].rearrange("t k d -> t (k d)"))):
                nc.gpsimd.dma_start(dst, src).then_inc(cache_sem[k], 16)
            if b < N_MOD - EARLY_MOD:
                pool.wait_ge(S["parts_ready"], EARLY_MOD + b)
                nc.gpsimd.dma_start(mod_rows[:, :, :], ada_rows[EARLY_MOD + b]).then_inc(S["loaded_rows"], 16)

        pool.wait_ge(S["o_ready"], len(items))
        nc.gpsimd.dma_start(bias_src[:, :], moe_b).then_inc(S["loaded_bias"], 16)
        pool.wait_ge(S["loaded_bias"], 16)
        steps = [0]

        def step(ins):
            steps[0] += 1
            ins.then_inc(S["p_step"], 1)
            pool.wait_ge(S["p_step"], steps[0])

        step(nc.gpsimd.tensor_copy(bias_parts[0:NE, :], bias_src[:, :]))
        step(nc.gpsimd.tensor_tensor(bias_src[:, :], bias_src[:, :], bias_parts[0:NE, :], ALU.subtract))
        step(nc.gpsimd.tensor_copy(bias_p2[:, :], bias_src[:, :]))
        step(nc.gpsimd.tensor_tensor(bias_src[:, :], bias_src[:, :], bias_p2[:, :], ALU.subtract))
        step(nc.gpsimd.tensor_copy(bias_parts[NE:2 * NE, :], bias_p2[:, :]))
        nc.gpsimd.tensor_copy(bias_parts[2 * NE:3 * NE, :], bias_src[:, :]).then_inc(S["bias_ready"], 1)
        pool.wait_ge(S["bias_ready"], 1)

        pool.wait_ge(S["routed"], 1)
        pool.wait_ge(S["slot_zeroed"], 16)
        for n in range(NT * TOPK):
            nc.gpsimd.indirect_dma_start(
                out=slot_tok_dram, out_offset=bass.IndirectOffsetOnAxis(ap=tok_addr[:, n:n + 1], axis=0),
                in_=token_id[:, n // TOPK:n // TOPK + 1], in_offset=None).then_inc(S["scattered"], 16)
        pool.wait_ge(S["scattered"], 16 * NT * TOPK)
        nc.gpsimd.dma_start(slot_tok[:, :], slot_tok_dram.rearrange("(p n) o -> p (n o)", p=P)).then_inc(
            S["slots_back"], 16)
        pool.wait_ge(S["slots_back"], 16)
        pool.wait_ge(S["h_stored"], 16 * NT)

        def gather(i, first=False):
            if not first:
                pool.wait_ge(S["gathered"], i * 16)
                pool.wait_ge(S["xT_filled"], i * 2)
            col = slot_tok[:, 0:1] if first else slot_tok[:, bass.ds(i, 1)]
            nc.gpsimd.tensor_copy(cur_idx[:, :], col).then_inc(S["idx_ready"], 1)
            pool.wait_ge(S["idx_ready"], 1 if first else i + 1)
            if not first:
                pool.sem_inc(S["pool_gate"], 1)
            nc.gpsimd.indirect_dma_start(
                out=x_slots[:, :], out_offset=None, in_=h_rows,
                in_offset=bass.IndirectOffsetOnAxis(ap=cur_idx[:, 0:1], axis=0)).then_inc(S["gathered"], 16)

        gather(0, first=True)
        with pool.Fori(0, NE) as i:
            gather(i + 1)
        n_ovf = pool.value_load(ovf_table[0:1, NOVF:NOVF + 1], min_val=0, max_val=NOVF)
        with pool.If(n_ovf > 0):
            with pool.Fori(NE, n_ovf + NE) as i:
                gather(i + 1)

        pool.wait_ge(S["y_stored"], (n_ovf + NE) * 16 + 16)
        pool.sem_inc(S["pool_gate"], 1)
        for n in range(NT * TOPK):
            k = n % TOPK
            if n >= TOPK:
                pool.wait_ge(S["acc_done"], n - TOPK + 1)
            nc.gpsimd.indirect_dma_start(
                out=y_got[:, k, :], out_offset=None, in_=y_rows,
                in_offset=bass.IndirectOffsetOnAxis(ap=y_row_idx[:, n:n + 1], axis=0)).then_inc(S[f"got{k}"], 16)
        pool.wait_ge(S["out_stored"], 16 * n_out)
        pool.wait_ge(S["gathered"], (n_ovf + NE + 1) * 16)

    @block.scalar
    def _(a):
        qf = q_tok[:, :, :].rearrange("p h d -> p (h d)")
        nc.scalar.dma_start(cT[:, :, :], c_t).then_inc(S["loaded_c"], 16)
        for t in range(NT):
            nc.scalar.dma_start(x[:, t, :], x_in[t]).then_inc(S["loaded_x"], 16)
        nc.scalar.dma_start(qf[0:96, 0:2 * P], c_kind).then_inc(S["loaded_small"], 16)
        nc.scalar.dma_start(qf[:, 2 * P:4 * P], c_before).then_inc(S["loaded_small"], 16)
        nc.scalar.dma_start(ident[:, :], c_ident).then_inc(S["loaded_small"], 16)
        nc.scalar.dma_start(kT[0:NOPE, :, :], uk_t).then_inc(S["loaded_small"], 16)
        rest = ((w_ukv[:, :, :, :], ukv_w), (rope[:, :, :], c_rope), (causal[:, :, :], c_causal),
                (dist[:, :, :], c_dist), (alibi[:, :], c_alibi), (g_qkv[:, :], rows_q_kv), (sinks[:, :], sink_cols),
                (w_rt[:, :, :], router_w), (b_rt[:, :], router_b), (expert_id[:, :], c_eid),
                (row_expert[:, :], c_rowe), (block_id[:, :, :], c_blk), (token_id[:, :], c_tok))
        for dst, src in rest:
            nc.scalar.dma_start(dst, src).then_inc(S["loaded_c"], 16)

        a.wait_ge(S["loaded_c"], 16 * (1 + len(rest)))
        csig = rtr[:, :, :].rearrange("p a b -> p (a b)")[:, 0:KT * 9]
        nc.scalar.activation(csig, cT[:, :, :].rearrange("p k n -> p (k n)"), ACT.Sigmoid).then_inc(S["sig_ready"], 1)

        def x_stats(n0):
            for t in range(NT):
                nc.scalar.activation(hq[:, 0:D] if n0 == 0 else hm[:, :, :].rearrange("p k t -> p (k t)")[:, 0:D],
                                     x[:, t, :], ACT.Square, accum_out=stat[:, n0 + t:n0 + t + 1]).then_inc(S["ss_ready"], 1)
                a.wait_ge(S["ss_ready"], (0 if n0 == 0 else NT) + t + 1)
            a.wait_ge(S["ms_ready"], 1 if n0 == 0 else 3)
            nc.scalar.activation(stat[:, n0 + 3:n0 + 6], stat[:, n0 + 6:n0 + 9], ACT.Sqrt).then_inc(S["root_ready"], 1)

        a.wait_ge(S["loaded_x"], 16 * NT)
        x_stats(0)

        def empty(key, dst, src, last=True):
            ins = nc.scalar.copy(dst, src)
            if last:
                ins.then_inc(S["a_emptied"], 1)

        for t in range(NT):
            for g in range(2):
                filled(a, "hT", t, g)
                empty(("hT", t, g), hT[:, 4 * g:4 * g + 4, t * P:(t + 1) * P],
                      bank("hT", t, g).rearrange("p (k n) -> p k n", k=4))
        for j in range(6):
            for t in range(NT):
                filled(a, "u", j, t)
                empty(("u", j, t), u[:, t, j * IN_COLS:(j + 1) * IN_COLS], bank("u", j, t)[:, 0:IN_COLS])
        a.wait_ge(S["a_emptied"], ordinal[("u", 5, NT - 1)])
        a.wait_ge(S["consts_cast"], 2)
        for t in range(NT):
            for c0, n, o in ((0, QL, 16 + t), (O_KV, KVL, 19 + t)):
                nc.scalar.activation(qf[:, 0:n], u[:, t, c0:c0 + n], ACT.Square, scale=float(n) ** -0.5,
                                     accum_out=stat[:, o:o + 1]).then_inc(S["u_stats"], 1)
                a.wait_ge(S["u_stats"], 2 * t + (2 if c0 else 1))
        a.wait_ge(S["ms_ready"], 2)
        nc.scalar.activation(stat[:, 28:34], stat[:, 22:28], ACT.Sqrt).then_inc(S["root_ready"], 1)
        a.wait_ge(S["rows_zeroed"], 16 * NOVF)
        for t in range(NT):
            filled(a, "qlT", t)
            empty(("qlT", t), qlT[:, :, t * P:(t + 1) * P], bank("qlT", t)[:, 0:3 * P].rearrange("p (k n) -> p k n", k=3))
        for t in range(NT):
            filled(a, "ckT", t)
            nc.scalar.copy(kpT[NOPE:QK, t * P:(t + 1) * P], bank("ckT", t)[0:ROPE, 2 * P:3 * P])
            empty(("ckT", t), ckT[:, :, t * P:(t + 1) * P], bank("ckT", t)[:, 0:2 * P].rearrange("p (k n) -> p k n", k=2))
        for t in range(NT):
            filled(a, "qsT", t)
            if t < NP_T:
                empty(("qsT", t), qsT[:, t, :, :], bank("qsT", t).rearrange("p (k n) -> p k n", k=GRP))
            else:
                empty(("qsT", t), qsT_s[:, :, :, :].rearrange("p b g q -> p g b q"),
                      bank("qsT", t).rearrange("p (g b q) -> p g b q", g=GRP, b=NB_DEC))
        filled(a, "ksT")
        empty(("ksT",), ksT[:, :], bank("ksT")[:, 0:NT * P])
        for k in range(2):
            for f in range(2):
                filled(a, "gate", k, f)
                empty(("gate", k, f), gates[:, k, f * 512:(f + 1) * 512], bank("gate", k, f))
        for t in range(NP_T):
            filled(a, "v", t)
            empty(("v", t), v_p[:, t, :], bank("v", t))
        for t in range(NT):
            for f in range(2):
                filled(a, "qT", t, f)
                if t < NP_T:
                    empty(("qT", t, f), qT[:, t, 4 * f:4 * f + 4, :],
                          bank("qT", t, f)[0:QK].rearrange("p (h n) -> p h n", h=4))
                else:
                    empty(("qT", t, f), qT_s[:, :, 4 * f:4 * f + 4, :].rearrange("p b h q -> p h b q"),
                          bank("qT", t, f)[0:QK].rearrange("p (h b q) -> p h b q", h=4, b=NB_DEC))
        for p in range(4):
            filled(a, "qabs", p)
            for hh in range(2):
                for ct in range(2):
                    o = (hh * 2 + ct) * P
                    empty(("qabs", p), qabs[:, ct, :, 2 * p + hh, :],
                          bank("qabs", p)[:, o:o + P].rearrange("p (b q) -> p b q", b=NB_DEC), last=(hh + ct == 2))
        for p in range(4):
            filled(a, "kT", p)
            empty(("kT", p), kT[0:NOPE, 2 * p:2 * p + 2, :], bank("kT", p)[0:NOPE].rearrange("p (h n) -> p h n", h=2),
                  last=False)
            for hh in range(2):
                empty(("kT", p), kT[NOPE:QK, 2 * p + hh, :], kpT[NOPE:QK, 0:SEQ], last=(hh == 1))

        def a_exp(i):
            kind, n, hh = items[i]
            a.wait_ge(S["maxed"], i + 1)
            if i >= 2:
                a.wait_ge(S["flipped"], i - 1)
            scale = MLA_SCALE if kind.startswith("mla") else SWA_SCALE
            nk = width(i)
            ins = nc.scalar.activation(probs[:, i % 2, 0:nk], scores(i)[:, 0:nk], ACT.Exp, bias=neg_max[:, i:i + 1],
                                       scale=scale, accum_out=row_sum[:, i:i + 1])
            if kind.startswith("swa"):
                col = sinks[:, hh:hh + 1] if kind == "swa" else sinks[:, H:H + 1]
                ins = nc.scalar.activation(sink_e[:, i:i + 1], col, ACT.Exp, bias=neg_max[:, i:i + 1])
            ins.then_inc(S["exped"], 1)

        def a_flip(i):
            kind, n, hh = items[i]
            a.wait_ge(S["flipped"], i + 1)
            if i >= 2:
                a.wait_ge(S["pv_done"], i - 1)
            full = full_tiles(i)
            tb = ps[:, 4:6, :].rearrange("p a b -> p (a b)")
            last = nc.scalar.copy(pT[:, i % 2, 0:full * P], tb[:, 0:full * P])
            if kind.endswith("_s"):
                last = nc.scalar.copy(pT[0:Q_DEC, i % 2, full * P:(full + 1) * P], tb[0:Q_DEC, full * P:(full + 1) * P])
            last.then_inc(S["pT_ready"], 1)

        def a_out(i):
            kind, n, hh = items[i]
            a.wait_ge(S["pv_done"], i + 1)
            ob = ps[:, 6, :]
            if kind in ("mla", "swa"):
                r = slice(64 * (hh % 2), 64 * (hh % 2) + 64)
                last = nc.scalar.copy(mixT[r, (4 if kind == "swa" else 0) + hh // 2, n * P:(n + 1) * P], ob[r, 0:P])
            elif kind == "mla_s":
                last = nc.scalar.copy(qabs[:, :, n, :, :].rearrange("p a h q -> p a (h q)"),
                                      ob[:, 0:2 * P].rearrange("p (a n) -> p a n", a=2))
            else:
                c0 = SEQ + n * Q_DEC
                last = nc.scalar.copy(mixT[:, 4:8, c0:c0 + Q_DEC], ob[:, 0:4 * Q_DEC].rearrange("p (a q) -> p a q", a=4))
            last.then_inc(S["o_ready"], 1)

        a_exp(0)
        for i in range(len(items)):
            if i + 1 < len(items):
                a_exp(i + 1)
            a_flip(i)
            if i >= 1:
                a_out(i - 1)
        a_out(len(items) - 1)
        filled(a, "oS")
        empty(("oS",), mixT[:, 0:4, SEQ:SEQ + P], bank("oS").rearrange("p (k n) -> p k n", k=4))
        a.wait_ge(S["x1_ready"], 12)
        for k in range(2):
            for f in range(2):
                filled(a, "fgate", k, f)
                empty(("fgate", k, f), gates[:, k, f * 512:(f + 1) * 512], bank("fgate", k, f))
        x_stats(36)
        emptied(a, "fshift", 1, 1)
        for t in range(NT):
            nc.scalar.dma_start(h_rows[t * P:(t + 1) * P, :], h[:, t, :]).then_inc(S["h_stored"], 16)
        for t in range(NT):
            for g in range(2):
                filled(a, "fT", t, g)
                empty(("fT", t, g), hT[:, 4 * g:4 * g + 4, t * P:(t + 1) * P],
                      bank("fT", t, g).rearrange("p (k n) -> p k n", k=4))
        for t in range(NT):
            a.wait_ge(S["probs_top"], t + 1)
            nc.scalar.activation(gate_w[:, t, :], gate_w[:, t, :], ACT.Exp, bias=stat[:, 50 + t:51 + t],
                                 accum_out=stat[:, 53 + t:54 + t]).then_inc(S["gates_exped"], 1)

        a.wait_ge(S["gates_exped"], NT)
        a.wait_ge(S["table_ready"], 1)
        nc.scalar.dma_start(gfin[:, :], g_final).then_inc(S["loaded_gfin"], 16)
        t_bank = [ps[:, 6, :], ps[:, 7, :]]

        def turn_x(v0, r, bk):
            a.wait_ge(S["xT_filled"], v0 + r + 1)
            nc.scalar.copy(x_slotsT[:, 4 * r:4 * r + 4, :], t_bank[bk].rearrange("p (k n) -> p k n", k=4)).then_inc(
                S["xT_ready"], 1)

        turn_x(0, 0, 0)
        turn_x(0, 1, 1)

        def expert_block(i):
            for f in range(2):
                a.wait_ge(S["glu_ready"], i * 2 + f + 1)
                nc.scalar.activation(sig[:, f, :], glu[:, f, :], ACT.Sigmoid, scale=1.702).then_inc(S["sig_done"], 1)
                if f == 0:
                    a.wait_ge(S["actT_filled"], i * 2 + 1)
                    nc.scalar.copy(actT[:, 0:4, :], t_bank[0].rearrange("p (k n) -> p k n", k=4)).then_inc(S["actT_ready"], 1)
            turn_x(i * 2 + 2, 0, 1)
            turn_x(i * 2 + 2, 1, 0)
            a.wait_ge(S["actT_filled"], i * 2 + 2)
            nc.scalar.copy(actT[:, 4:8, :], t_bank[1].rearrange("p (k n) -> p k n", k=4)).then_inc(S["actT_ready"], 1)
            a.wait_ge(S["unit_used"], i * MOE_UNITS + (HALVES + MOE_UNITS))
            a.wait_ge(S["y_stored"], i * 16 + 16)
            nc.scalar.copy(y_blk[:, :], ps[:, 4:6, :].rearrange("p a b -> p (a b)")).then_inc(S["y_copied"], 1)
            a.wait_ge(S["y_copied"], i + 2)
            nc.scalar.dma_start(y_rows[bass.ds(i * P, P), :], y_blk[:, :]).then_inc(S["y_stored"], 16)

        a.sem_inc(S["y_copied"], 1)
        a.sem_inc(S["y_stored"], 16)
        with a.Fori(0, NE) as i:
            expert_block(i)
        n_ovf = a.value_load(ovf_table[0:1, NOVF:NOVF + 1], min_val=0, max_val=NOVF)
        with a.If(n_ovf > 0):
            with a.Fori(NE, n_ovf + NE) as i:
                expert_block(i)

        for t in range(NT):
            a.wait_ge(S["fin_ready"], 3 * t + 1)
            nc.scalar.activation(glu[:, :, :].rearrange("p a b -> p (a b)"), x[:, t, :], ACT.Square, scale=float(D) ** -0.5,
                                 accum_out=stat[:, 56 + t:57 + t]).then_inc(S["fin_ss"], 1)
            a.wait_ge(S["fin_ready"], 3 * t + 2)
            nc.scalar.activation(stat[:, 59 + t:60 + t], stat[:, 56 + t:57 + t], ACT.Sqrt).then_inc(S["fin_root"], 1)
            a.wait_ge(S["fin_ready"], 3 * t + 3)
            dst = o_yp[0, t * P:(t + 1) * P, :] if t < NP_T else o_ys.rearrange("b q d -> (b q) d")
            nc.scalar.dma_start(dst, x[:, t, :]).then_inc(S["fin_stored"], 16)
        a.wait_ge(S["fin_stored"], 16 * NT)

    @block.vector
    def _(v):
        steps = [0]

        def step(ins):
            steps[0] += 1
            ins.then_inc(S["v_step"], 1)
            v.wait_ge(S["v_step"], steps[0])

        csig = rtr[:, :, :].rearrange("p a b -> p (a b)")[:, 0:KT * 9]
        step(nc.vector.memset(mod_parts[:, :], 0.0))
        v.wait_ge(S["sig_ready"], 1)
        nc.vector.tensor_tensor(cs[:, :, :].rearrange("p k n -> p (k n)"), cT[:, :, :].rearrange("p k n -> p (k n)"),
                                csig, ALU.mult).then_inc(S["silu_ready"], 1)
        nc.vector.tensor_scalar(sinks_s[:, :], sinks[:, :], 1.0 / SWA_SCALE, None, ALU.mult)

        def rms_of_x(n0, ss, ms, root):
            v.wait_ge(S["ss_ready"], ss)
            nc.vector.tensor_scalar(stat[:, n0 + 6:n0 + 9], stat[:, n0:n0 + 3], 1.0 / D, EPS, ALU.mult, ALU.add).then_inc(
                S["ms_ready"], 1)
            v.wait_ge(S["root_ready"], root)
            step(nc.vector.reciprocal(stat[:, n0 + 9:n0 + 12], stat[:, n0 + 3:n0 + 6]))

        rms_of_x(0, NT, 1, 1)

        def mod_chunk(n, src, done):
            cols = slice(n * 512, (n + 1) * 512)
            v.wait_ge(S["loaded_rows"], 16 * (n + 1))
            nc.vector.tensor_tensor(mod_row[:, :], src[0:9], mod_rows[:, 0, :], ALU.add).then_inc(S[done], 1)
            v.wait_ge(S[done], ordinal[("mod", n)] if n < EARLY_MOD else n - EARLY_MOD + 1)
            if n // 2 in (1, 4):
                step(nc.vector.scalar_tensor_tensor(mod_row[:, :], mod_row[:, :], 1.0, mod_rows[:, 1, :], ALU.add, ALU.mult))
            step(nc.vector.tensor_copy(mod_parts[0:9, cols], mod_row[:, :]))
            step(nc.vector.tensor_tensor(mod_res[:, :], mod_row[:, :], mod_parts[0:9, cols], ALU.subtract))
            step(nc.vector.tensor_copy(mod_p2[:, :], mod_res[:, :]))
            step(nc.vector.tensor_tensor(mod_res[:, :], mod_res[:, :], mod_p2[:, :], ALU.subtract))
            step(nc.vector.tensor_copy(mod_parts[32:41, cols], mod_p2[:, :]))
            nc.vector.tensor_copy(mod_parts[64:73, cols], mod_res[:, :]).then_inc(S["parts_ready"], 1)
            v.wait_ge(S["parts_ready"], n + 1)

        for n in range(4):
            filled(v, "mod", n)
            mod_chunk(n, bank("mod", n), "v_emptied")

        def modulated(pre_, inv0):
            for k in range(2):
                tiles = (0, 1) if k == 0 else (2,)
                for f in range(2):
                    cols = slice(f * 512, (f + 1) * 512)
                    filled(v, pre_ + "scale", k, f)
                    for t in tiles:
                        last = nc.vector.scalar_tensor_tensor(h[:, t, cols], x[:, t, cols], stat[:, inv0 + t:inv0 + t + 1],
                                                              bank(pre_ + "scale", k, f), ALU.mult, ALU.mult)
                    last.then_inc(S["v_emptied"], 1)
                    v.wait_ge(S["v_emptied"], ordinal[(pre_ + "scale", k, f)])
                    filled(v, pre_ + "shift", k, f)
                    for t in tiles:
                        last = nc.vector.tensor_tensor(h[:, t, cols], h[:, t, cols], bank(pre_ + "shift", k, f), ALU.add)
                    last.then_inc(S["v_emptied"], 1)

        modulated("b", 9)

        def rope_into(dst, x1, x2, cos, sin, tmp):
            nc.vector.tensor_tensor(tmp[0], x1, cos, ALU.mult)
            nc.vector.tensor_tensor(tmp[1], x2, sin, ALU.mult)
            nc.vector.tensor_tensor(tmp[2], x2, cos, ALU.mult)
            step(nc.vector.tensor_tensor(tmp[3], x1, sin, ALU.mult))
            nc.vector.tensor_tensor(dst[0], tmp[0], tmp[1], ALU.subtract)
            return nc.vector.tensor_tensor(dst[1], tmp[2], tmp[3], ALU.add)

        v.wait_ge(S["u_stats"], 2 * NT)
        step(nc.vector.tensor_scalar(stat[:, 22:28], stat[:, 16:22], EPS, None, ALU.add))
        v.sem_inc(S["ms_ready"], 1)
        v.wait_ge(S["root_ready"], 2)
        step(nc.vector.reciprocal(stat[:, 34:36], stat[:, 28:30]))
        step(nc.vector.reciprocal(stat[:, 12:16], stat[:, 30:34]))
        q_inv = (stat[:, 34:35], stat[:, 35:36], stat[:, 12:13])
        for t in range(NT):
            last = nc.vector.scalar_tensor_tensor(u[:, t, 0:QL], u[:, t, 0:QL], q_inv[t], g_qkv[:, 0:QL], ALU.mult, ALU.mult)
        last.then_inc(S["ql_ready"], 1)
        for t in range(NT):
            nc.vector.scalar_tensor_tensor(u[:, t, O_KV:O_KPE], u[:, t, O_KV:O_KPE], stat[:, 13 + t:14 + t],
                                           g_qkv[:, QL:QL + KVL], ALU.mult, ALU.mult)
        half = ROPE // 2
        tmp = [rt[:, n, 0:NT * half].rearrange("p (t d) -> p t d", t=NT) for n in range(4)]
        rope_into((u[:, :, O_KPE:O_KPE + half], u[:, :, O_KPE + half:O_QS]), u[:, :, O_KPE:O_KPE + half],
                  u[:, :, O_KPE + half:O_QS], rope[:, :, 0:half], rope[:, :, half:ROPE], tmp).then_inc(S["ck_ready"], 1)
        nc.vector.tensor_copy(v_swa[:, :, :], u[:, :, O_VS:IN_W]).then_inc(S["v_swa_ready"], 1)
        for n in (4, 5):
            filled(v, "mod", n)
            mod_chunk(n, bank("mod", n), "v_emptied")

        for t in range(NT):
            for f in range(2):
                filled(v, "q", t, f)
                if t:
                    filled(v, "qT", t - 1, f)
                src = bank("q", t, f)[:, 0:4 * QK].rearrange("p (h d) -> p h d", h=4)
                hs = slice(4 * f, 4 * f + 4)
                cos = rope[:, t:t + 1, 0:half].to_broadcast([P, 4, half])
                sin = rope[:, t:t + 1, half:ROPE].to_broadcast([P, 4, half])
                nc.vector.tensor_copy(q_tok[:, hs, 0:NOPE], src[:, :, 0:NOPE])
                tmp = [rt[:, n, 0:4 * half].rearrange("p (t d) -> p t d", t=4) for n in range(4)]
                rope_into((q_tok[:, hs, NOPE:NOPE + half], q_tok[:, hs, NOPE + half:QK]),
                          src[:, :, NOPE:NOPE + half], src[:, :, NOPE + half:QK], cos, sin, tmp).then_inc(S["v_emptied"], 1)
                emptied(v, "q", t, f)

        mod_next = [EARLY_MOD]

        def v_max(i):
            kind, n, hh = items[i]
            s, nk = scores(i), width(i)
            v.wait_ge(S["scored"], i + 1)
            if kind == "mla":
                step(nc.vector.tensor_tensor(s[:, 0:nk], s[:, 0:nk], causal[:, n, 0:nk], ALU.add))
            elif kind == "swa":
                slope = 2.0 ** (-8.0 * (hh + 1) / H)
                step(nc.vector.scalar_tensor_tensor(s[:, 0:nk], dist[:, n, 0:nk], -slope / SWA_SCALE, s[:, 0:nk],
                                                    ALU.mult, ALU.add))
            elif kind == "swa_s":
                step(nc.vector.tensor_tensor(s[:, 0:nk], s[:, 0:nk], alibi[:, 0:nk], ALU.add))
            step(nc.vector.tensor_reduce(row_max[:, i:i + 1], s[:, 0:nk], AX, ALU.max))
            if kind.startswith("swa"):
                col = sinks_s[:, hh:hh + 1] if kind == "swa" else sinks_s[:, H:H + 1]
                nc.vector.tensor_scalar(neg_max[:, i:i + 1], row_max[:, i:i + 1], col, -SWA_SCALE, ALU.max,
                                        ALU.mult).then_inc(S["maxed"], 1)
            else:
                nc.vector.tensor_scalar(neg_max[:, i:i + 1], row_max[:, i:i + 1], -MLA_SCALE, None, ALU.mult).then_inc(
                    S["maxed"], 1)

        def v_norm(i):
            kind, n, hh = items[i]
            v.wait_ge(S["exped"], i + 1)
            if kind.startswith("swa"):
                step(nc.vector.tensor_tensor(row_sum[:, i:i + 1], row_sum[:, i:i + 1], sink_e[:, i:i + 1], ALU.add))
            step(nc.vector.reciprocal(row_inv[:, i:i + 1], row_sum[:, i:i + 1]))
            nk = width(i)
            nc.vector.tensor_scalar(probs[:, i % 2, 0:nk], probs[:, i % 2, 0:nk], row_inv[:, i:i + 1], None,
                                    ALU.mult).then_inc(S["normed"], 1)

        v_max(0)
        for i in range(len(items)):
            if i + 1 < len(items):
                v_max(i + 1)
            v_norm(i)
            if i % 6 == 5 and i // 6 < N_MOD - EARLY_MOD:
                v.wait_ge(S["mod_extra"], i // 6 + 1)
                mod_chunk(EARLY_MOD + i // 6, ps[:, 7, :], "mod_extra_used")

        for j in range(4):
            cols = slice(j * OUT_COLS, (j + 1) * OUT_COLS)
            for t in range(NT):
                filled(v, "o", j, t)
                emptied(v, "gate", 1, 1)
                if j:
                    v.wait_ge(S["x1_ready"], NT * (j - 1) + t + 1)
                tmp = hq[:, (t % 3) * OUT_COLS:(t % 3 + 1) * OUT_COLS]
                nc.vector.tensor_tensor(tmp, bank("o", j, t)[:, 0:OUT_COLS], gates[:, t // 2, cols], ALU.mult).then_inc(
                    S["v_emptied"], 1)
                v.wait_ge(S["v_emptied"], ordinal[("o", j, t)])
                nc.vector.tensor_tensor(x[:, t, cols], x[:, t, cols], tmp, ALU.add).then_inc(S["x1_ready"], 1)
        rms_of_x(36, 2 * NT, 3, 3)
        modulated("f", 45)

        v.wait_ge(S["v_emptied"], ordinal[("fshift", 1, 1)])
        top = rtr[:, 0, :]
        idx_u = rtr[:, 1, 0:24].bitcast(U32)
        idx_f = rtr[:, 2, 0:12]
        logit = rtr[:, 4:7, :]
        for t in range(NT):
            filled(v, "logit", t)
            nc.vector.tensor_tensor(logit[:, t, :], bank("logit", t)[:, 0:NE], b_rt[:, :], ALU.add).then_inc(S["v_emptied"], 1)
            v.wait_ge(S["v_emptied"], ordinal[("logit", t)])
            step(nc.vector.max(top[:, 8 * t:8 * t + 8], logit[:, t, :]))
            nc.vector.max_index(idx_u[:, 8 * t:8 * t + 8], top[:, 8 * t:8 * t + 8], logit[:, t, :])
            nc.vector.tensor_scalar(stat[:, 50 + t:51 + t], top[:, 8 * t:8 * t + 1], -1.0, None, ALU.mult)
            nc.vector.tensor_copy(gate_w[:, t, :], top[:, 8 * t:8 * t + TOPK]).then_inc(S["probs_top"], 1)
        v.wait_ge(S["probs_top"], NT)
        step(nc.vector.tensor_copy(idx_f.rearrange("p (t k) -> p t k", t=NT),
                                   idx_u.rearrange("p (t k) -> p t k", t=NT)[:, :, 0:TOPK]))
        hot = hq[:, 0:NT * TOPK * NE].rearrange("p (n e) -> p n e", e=NE)
        prod = hq[:, 512:512 + NT * TOPK * NE].rearrange("p (n e) -> p n e", e=NE)
        fld = [hq[:, 1024 + 128 * n:1024 + 128 * n + NT * NE].rearrange("p (t e) -> p t e", t=NT) for n in range(7)]
        chosen = hq[:, 2048:2048 + NT * NE // 2].bitcast(BF16).rearrange("p (t e) -> p t e", t=NT)
        emptied(v, "fT", NT - 1, 1)
        v.wait_ge(S["h_stored"], 16 * NT)
        step(nc.vector.tensor_tensor(hot, expert_id[:, :].unsqueeze(1).to_broadcast([P, NT * TOPK, NE]),
                                     idx_f.unsqueeze(2).to_broadcast([P, NT * TOPK, NE]), ALU.is_equal))
        step(nc.vector.tensor_reduce(fld[0], hot.rearrange("p (t k) e -> p t e k", t=NT), AX, ALU.add))
        nc.vector.tensor_copy(chosen, fld[0]).then_inc(S["logits_exp"], 1)
        rank, big1, big2, blk, pos, f1, f2 = fld
        for t in range(NT):
            filled(v, "rank", t)
            nc.vector.tensor_copy(rank[:, t, :], bank("rank", t)[:, 0:NE]).then_inc(S["v_emptied"], 1)
        filled(v, "count")
        cnt = rtr[:, 7, :]
        nc.vector.tensor_copy(cnt, bank("count")[:, 0:NE]).then_inc(S["v_emptied"], 1)
        v.wait_ge(S["v_emptied"], ordinal[("count",)])
        cum, alt = rtr[:, 8, :], rtr[:, 9, :]
        step(nc.vector.tensor_scalar(alt, cnt, 2.0 * P, None, ALU.is_gt))
        step(nc.vector.scalar_tensor_tensor(cum, cnt, 1.0 * P, alt, ALU.is_gt, ALU.add))
        n_own = rtr[:, 10, :]
        step(nc.vector.tensor_copy(n_own, cum))
        d = 1
        while d < NE:
            nc.vector.tensor_copy(alt[:, 0:d], cum[:, 0:d])
            step(nc.vector.tensor_tensor(alt[:, d:NE], cum[:, d:NE], cum[:, 0:NE - d], ALU.add))
            cum, alt, d = alt, cum, 2 * d
        ovf = prod.rearrange("p n e -> p (n e)")[:, 0:NOVF * NE].rearrange("p (n e) -> p n e", e=NE)
        step(nc.vector.tensor_tensor(ovf, cum.unsqueeze(1).to_broadcast([P, NOVF, NE]), block_id[:, :, :], ALU.is_le))
        nc.vector.memset(block_expert[:, NBLK - 1:NBLK], 0.0)
        nc.vector.tensor_copy(block_expert[:, 0:NE], expert_id[:, :])
        step(nc.vector.tensor_reduce(block_expert[:, NE:NE + NOVF], ovf, AX, ALU.add))
        nc.vector.tensor_copy(ovf_table[0:1, 0:NOVF], block_expert[0:1, NE:NE + NOVF])
        nc.vector.tensor_copy(ovf_table[0:1, NOVF:NOVF + 1], cum[0:1, NE - 1:NE]).then_inc(S["table_ready"], 1)
        first = alt
        step(nc.vector.tensor_tensor(first, cum, n_own, ALU.subtract))
        step(nc.vector.tensor_scalar(first, first, float(NE), None, ALU.add))
        step(nc.vector.tensor_tensor(first, first, expert_id[:, :], ALU.subtract))
        first3 = first.unsqueeze(1).to_broadcast([P, NT, NE])
        eid3 = expert_id[:, :].unsqueeze(1).to_broadcast([P, NT, NE])
        nc.vector.tensor_scalar(big1, rank, float(P), None, ALU.is_ge)
        step(nc.vector.tensor_scalar(big2, rank, 2.0 * P, None, ALU.is_ge))
        step(nc.vector.tensor_tensor(blk, big1, first3, ALU.mult))
        step(nc.vector.tensor_tensor(blk, blk, eid3, ALU.add))
        step(nc.vector.tensor_tensor(blk, blk, big2, ALU.add))
        step(nc.vector.tensor_tensor(big1, big1, big2, ALU.add))
        step(nc.vector.scalar_tensor_tensor(pos, big1, -float(P), rank, ALU.mult, ALU.add))
        nc.vector.scalar_tensor_tensor(f1, blk, float(P), pos, ALU.mult, ALU.add)
        step(nc.vector.scalar_tensor_tensor(f2, pos, float(NBLK), blk, ALU.mult, ALU.add))
        addr_f = rtr[:, 11, 0:NT * TOPK]
        for fsrc, dst in ((f1, y_row_idx), (f2, tok_addr)):
            for t in range(NT):
                last = nc.vector.tensor_tensor(prod[:, t * TOPK:(t + 1) * TOPK, :], hot[:, t * TOPK:(t + 1) * TOPK, :],
                                               fsrc[:, t:t + 1, :].to_broadcast([P, TOPK, NE]), ALU.mult)
            step(last)
            step(nc.vector.tensor_reduce(addr_f, prod, AX, ALU.add))
            step(nc.vector.tensor_copy(dst[:, :], addr_f))
        v.sem_inc(S["routed"], 1)
        v.wait_ge(S["gates_exped"], NT)
        step(nc.vector.reciprocal(stat[:, 50:53], stat[:, 53:56]))
        for t in range(NT):
            last = nc.vector.tensor_scalar(gate_w[:, t, :], gate_w[:, t, :], stat[:, 50 + t:51 + t], None, ALU.mult)
        step(last)
        nc.vector.tensor_scalar(sel_e[:, :], row_expert[:, :], block_expert[0:96, 0:1], None, ALU.is_equal).then_inc(
            S["sel_ready"], 1)

        def expert_block(i):
            v.wait_ge(S["act_ready"], i * 2 + 2)
            for f in range(2):
                v.wait_ge(S["unit_used"], i * MOE_UNITS + (HALVES + 4 * f + 4))
                g_ps, u_ps = ps[:, 2 * f, :], ps[:, 2 * f + 1, :]
                nc.vector.tensor_scalar(glu[:, f, :], g_ps, 7.0, None, ALU.min).then_inc(S["glu_ready"], 1)
                nc.vector.tensor_scalar(lin[:, f, :], u_ps, -7.0, 7.0, ALU.max, ALU.min).then_inc(S["gu_emptied"], 1)
                v.wait_ge(S["sig_done"], i * 2 + f + 1)
                nc.vector.tensor_tensor(gsg[:, f, :], glu[:, f, :], sig[:, f, :], ALU.mult).then_inc(S["gsg_ready"], 1)
                v.wait_ge(S["gsg_ready"], i * 2 + f + 1)
                nc.vector.scalar_tensor_tensor(act[:, f, :], lin[:, f, :], 1.0, gsg[:, f, :], ALU.add, ALU.mult).then_inc(
                    S["act_ready"], 1)
            v.wait_ge(S["bias_done"], i + 1)
            v.wait_ge(S["sel_ready"], i + 1)
            nc.vector.tensor_scalar(sel_e[:, :], row_expert[:, :], block_expert[0:96, bass.ds(i + 1, 1)], None,
                                    ALU.is_equal).then_inc(S["sel_ready"], 1)

        v.sem_inc(S["gu_emptied"], 2)
        v.sem_inc(S["act_ready"], 2)
        with v.Fori(0, NE) as i:
            expert_block(i)
        n_ovf = v.value_load(ovf_table[0:1, NOVF:NOVF + 1], min_val=0, max_val=NOVF)
        with v.If(n_ovf > 0):
            with v.Fori(NE, n_ovf + NE) as i:
                expert_block(i)

        v.wait_ge(S["loaded_gfin"], 16)
        for t in range(NT):
            for k in range(TOPK):
                v.wait_ge(S[f"got{k}"], 16 * (t + 1))
                w = gate_w[:, t, k:k + 1]
                if k == 0:
                    ins = nc.vector.tensor_scalar(y_acc[:, :], y_got[:, k, :], w, None, ALU.mult)
                else:
                    ins = nc.vector.scalar_tensor_tensor(y_acc[:, :], y_got[:, k, :], w, y_acc[:, :], ALU.mult, ALU.add)
                ins.then_inc(S["acc_done"], 1)
                v.wait_ge(S["acc_done"], t * TOPK + k + 1)
            step(nc.vector.tensor_tensor(y_acc[:, :], y_acc[:, :], gates[:, t // 2, :], ALU.mult))
            nc.vector.tensor_tensor(x[:, t, :], x[:, t, :], y_acc[:, :], ALU.add).then_inc(S["fin_ready"], 1)
            v.wait_ge(S["fin_ss"], t + 1)
            nc.vector.tensor_scalar(stat[:, 56 + t:57 + t], stat[:, 56 + t:57 + t], EPS, None, ALU.add).then_inc(
                S["fin_ready"], 1)
            v.wait_ge(S["fin_root"], t + 1)
            step(nc.vector.reciprocal(stat[:, 48:49], stat[:, 59 + t:60 + t]))
            nc.vector.scalar_tensor_tensor(x[:, t, :], x[:, t, :], stat[:, 48:49], gfin[:, :], ALU.mult, ALU.mult).then_inc(
                S["fin_ready"], 1)

    @block.tensor
    def _(pe):
        def open_job(*key):
            n = number[key]
            first = 0 if n < len(early) else len(early)
            if n - 8 >= first:
                emptied(pe, *jobs[n - 8][0])
            return bank(*key)

        def close(ins):
            ins.then_inc(S["psum_filled"], 1)

        def mod_products(n, out, done):
            for f in range(2):
                unit_here(pe, ("ada", n, f))
                w = unit(("ada", n, f)).rearrange("p (k n) -> p k n", k=4)
                for k in range(4):
                    kt = 4 * f + k
                    ins = nc.tensor.matmul(out[0:9], cs[:, kt, :], w[:, k, :], start=(kt == 0), stop=(kt == KT - 1))
                ins.then_inc(S["unit_used"] if f == 0 else S[done], 1)

        def spread(key, chunk, k):
            out = open_job(*key)
            close(nc.tensor.matmul(out, kind_sel[:, k, :], mod_parts[:, chunk * 512:(chunk + 1) * 512], start=True, stop=True))

        def turn(out, src, n_rows=P):
            return nc.tensor.transpose(out, src, ident[0:n_rows, 0:n_rows])

        pe.wait_ge(S["loaded_small"], 16 * 4)
        pe.wait_ge(S["silu_ready"], 1)
        for n in range(4):
            mod_products(n, open_job("mod", n), "psum_filled")
        pe.wait_ge(S["parts_ready"], 4)
        pe.wait_ge(S["consts_cast"], 2)
        for k in range(2):
            for f in range(2):
                spread(("bscale", k, f), 2 + f, k)
                spread(("bshift", k, f), f, k)
        for t in range(NT):
            for g in range(2):
                emptied(pe, "bshift", t // 2, g)
                out = open_job("hT", t, g)
                for k in range(4):
                    kt = 4 * g + k
                    ins = turn(out[:, k * P:(k + 1) * P], h[:, t, kt * P:(kt + 1) * P])
                close(ins)
        emptied(pe, "hT", NT - 1, 1)
        for j in range(6):
            unit_here(pe, ("in", j))
            w = unit(("in", j))[:, 0:KT * IN_COLS].rearrange("p (k n) -> p k n", k=KT)
            for t in range(NT):
                out = open_job("u", j, t)
                for kt in range(KT):
                    ins = nc.tensor.matmul(out[:, 0:IN_COLS], hT[:, kt, t * P:(t + 1) * P], w[:, kt, :],
                                           start=(kt == 0), stop=(kt == KT - 1))
                close(ins)
        for n in (4, 5):
            mod_products(n, open_job("mod", n), "psum_filled")
        pe.wait_ge(S["ql_ready"], 1)
        for t in range(NT):
            out = open_job("qlT", t)
            for k in range(3):
                ins = turn(out[:, k * P:(k + 1) * P], u[:, t, k * P:(k + 1) * P])
            close(ins)
        pe.wait_ge(S["ck_ready"], 1)
        for t in range(NT):
            out = open_job("ckT", t)
            for k in range(2):
                turn(out[:, k * P:(k + 1) * P], u[:, t, O_KV + k * P:O_KV + (k + 1) * P])
            close(turn(out[0:ROPE, 2 * P:3 * P], u[:, t, O_KPE:O_QS]))
        for t in range(NT):
            out = open_job("qsT", t)
            qs = u[:, t, O_QS:O_KS].rearrange("p (g n) -> p g n", g=GRP)
            for g in range(GRP):
                ins = turn(out[:, g * P:(g + 1) * P], qs[:, g])
            close(ins)
        out = open_job("ksT")
        for t in range(NT):
            ins = turn(out[:, t * P:(t + 1) * P], u[:, t, O_KS:O_VS])
        close(ins)
        pe.wait_ge(S["parts_ready"], EARLY_MOD)
        for k in range(2):
            for f in range(2):
                spread(("gate", k, f), 4 + f, k)
        emptied(pe, "ckT", NT - 1)
        for t in range(NP_T):
            out = open_job("v", t)
            for ct in range(2):
                ins = nc.tensor.matmul(out, ckT[:, ct, t * P:(t + 1) * P], w_ukv[:, ct, :, NOPE:NOPE + VD],
                                       start=(ct == 0), stop=(ct == 1))
            close(ins)
        pe.wait_ge(S["loaded_uq"], 16)
        emptied(pe, "qlT", NT - 1)

        def q_products(t, f):
            out = open_job("q", t, f)
            for k in range(3):
                ins = nc.tensor.matmul(out[:, 0:4 * QK], qlT[:, k, t * P:(t + 1) * P], w_uq[:, k, f * 4 * QK:(f + 1) * 4 * QK],
                                       start=(k == 0), stop=(k == 2))
            close(ins)

        def q_turn(t, f):
            emptied(pe, "q", t, f)
            out = open_job("qT", t, f)
            for hh in range(4):
                ins = turn(out[0:QK, hh * P:(hh + 1) * P], q_tok[:, 4 * f + hh, :])
            close(ins)

        for w, t in QUERY_ORDER:
            for f in range(2):
                (q_products if w == "q" else q_turn)(t, f)
        emptied(pe, "qT", NT - 1, 1)

        for p in range(4):
            out = open_job("qabs", p)
            for hh in range(2):
                for ct in range(2):
                    ins = nc.tensor.matmul(out[:, (hh * 2 + ct) * P:(hh * 2 + ct + 1) * P],
                                           wukT[:, 2 * p + hh, ct * P:(ct + 1) * P], qT_s[0:NOPE, :, 2 * p + hh, :],
                                           start=True, stop=True)
            close(ins)
        for p in range(4):
            out = open_job("kT", p)
            for hh in range(2):
                for ct in range(2):
                    ins = nc.tensor.matmul(out[0:NOPE, hh * SEQ:(hh + 1) * SEQ], w_ukv[:, ct, 2 * p + hh, 0:NOPE],
                                           ckT[:, ct, 0:SEQ], start=(ct == 0), stop=(ct == 1))
            close(ins)

        pe.wait_ge(S["v_emptied"], n_early["v"])
        pe.wait_ge(S["a_emptied"], n_early["a"])

        def score(i):
            kind, n, hh = items[i]
            s = scores(i)
            if i >= 2:
                pe.wait_ge(S["exped"], i - 1)
            if kind == "mla":
                ins = nc.tensor.matmul(s[:, 0:width(i)], qT[:, n, hh, :], kT[:, hh, 0:width(i)], start=True, stop=True)
            elif kind == "swa":
                r = slice(64 * (hh // GRP), 64 * (hh // GRP) + 64)
                ins = nc.tensor.matmul(s[:, 0:width(i)], qsT[r, n, hh % GRP, :], ksT[r, 0:width(i)], start=True, stop=True)
            elif kind == "mla_s":
                k = n % 2
                pe.wait_ge(cache_sem[k], 16 * 7 * (n // 2 + 1))
                own = slice(SEQ + n * Q_DEC, SEQ + (n + 1) * Q_DEC)
                for c0, n_c, keys in ((0, PAST, [latT[:, k, 0, :], latT[:, k, 1, :], krT[NOPE:QK, k, :]]),
                                      (PAST, Q_DEC, [ckT[:, 0, own], ckT[:, 1, own], kpT[NOPE:QK, own]])):
                    for ct in range(2):
                        nc.tensor.matmul(s[:, c0:c0 + n_c], qabs[:, ct, n, :, :].rearrange("p h q -> p (h q)"), keys[ct],
                                         start=(ct == 0), stop=False)
                    ins = nc.tensor.matmul(s[:, c0:c0 + n_c], qT_s[NOPE:QK, n].rearrange("p h q -> p (h q)"), keys[2], start=False, stop=True)
            else:
                k = n % 2
                own = slice(SEQ + n * Q_DEC, SEQ + (n + 1) * Q_DEC)
                for kv in range(KVH):
                    r = slice(64 * kv, 64 * kv + 64)
                    q = qsT_s[r, n].rearrange("p g q -> p (g q)")
                    nc.tensor.matmul(s[r, 0:WINDOW], q, ck_sT[r, k, :], start=True, stop=True)
                    ins = nc.tensor.matmul(s[r, WINDOW:WINDOW + Q_DEC], q, ksT[r, own], start=True, stop=True)
            ins.then_inc(S["scored"], 1)

        def flip(i):
            kind, n, hh = items[i]
            pe.wait_ge(S["normed"], i + 1)
            if i >= 1:
                pe.wait_ge(S["pT_ready"], i)
            tb = ps[:, 4:6, :].rearrange("p a b -> p (a b)")
            full = full_tiles(i)
            for k in range(full):
                ins = turn(tb[:, k * P:(k + 1) * P], probs[:, i % 2, k * P:(k + 1) * P])
            if kind.endswith("_s"):
                ins = turn(tb[0:Q_DEC, full * P:(full + 1) * P], probs[:, i % 2, full * P:full * P + Q_DEC])
            ins.then_inc(S["flipped"], 1)

        def weigh(i):
            kind, n, hh = items[i]
            pe.wait_ge(S["pT_ready"], i + 1)
            if i >= 1:
                pe.wait_ge(S["o_ready"], i)
            ob, full, pt = ps[:, 6, :], full_tiles(i), pT[:, i % 2, :]
            if kind in ("mla", "swa"):
                r = slice(64 * (hh % 2), 64 * (hh % 2) + 64)
                for k in range(full):
                    vals = v_p[:, k, hh * VD:(hh + 1) * VD] if kind == "mla" else \
                        v_swa[:, k, (hh // GRP) * HD:(hh // GRP + 1) * HD]
                    ins = nc.tensor.matmul(ob[r, 0:P], vals, pt[:, k * P:(k + 1) * P], start=(k == 0), stop=(k == full - 1))
            elif kind == "mla_s":
                for ct in range(2):
                    c = slice(ct * P, (ct + 1) * P)
                    for k in range(full):
                        nc.tensor.matmul(ob[:, c], lat[:, n % 2, k, c], pt[:, k * P:(k + 1) * P], start=(k == 0), stop=False)
                    ins = nc.tensor.matmul(ob[:, c], new_lat[:, n % 2, c], pt[0:Q_DEC, full * P:(full + 1) * P],
                                           start=False, stop=True)
            else:
                for kv in range(KVH):
                    for par in range(2):
                        o = ob[64 * par:64 * par + 64, kv * 2 * Q_DEC:(kv + 1) * 2 * Q_DEC]
                        vals = slice(kv * HD, (kv + 1) * HD)
                        for k, rows in ((0, P), (1, Q_DEC)):
                            cols = pt[0:rows, k * P:(k + 1) * P].rearrange("p (k g a q) -> p k g a q", k=KVH, g=2, a=2)
                            src = cv_s[:, n % 2, vals] if k == 0 else new_v[:, n % 2, vals]
                            ins = nc.tensor.matmul(o, src, cols[:, kv, :, par, :], start=(k == 0), stop=(k == 1))
            ins.then_inc(S["pv_done"], 1)

        score(0)
        for i in range(len(items)):
            if i + 1 < len(items):
                score(i + 1)
            flip(i)
            if i % 6 == 4 and i // 6 < N_MOD - EARLY_MOD:
                if i // 6:
                    pe.wait_ge(S["mod_extra_used"], i // 6)
                mod_products(EARLY_MOD + i // 6, ps[:, 7, :], "mod_extra")
            if i >= 1:
                weigh(i - 1)
        weigh(len(items) - 1)

        pe.wait_ge(S["o_ready"], len(items))
        pe.wait_ge(S["mod_extra_used"], N_MOD - EARLY_MOD)
        out = open_job("oS")
        for hh in range(H):
            r = slice(64 * (hh % 2), 64 * (hh % 2) + 64)
            for ct in range(2):
                ins = nc.tensor.matmul(out[r, (hh // 2) * P:(hh // 2 + 1) * P], w_ukv[:, ct, hh, NOPE:NOPE + VD],
                                       qabs[:, ct, :, hh, :], start=(ct == 0), stop=(ct == 1))
        close(ins)
        emptied(pe, "oS")
        for j in range(4):
            unit_here(pe, ("out", j))
            w = unit(("out", j)).rearrange("p (k n) -> p k n", k=KT)
            for t in range(NT):
                out = open_job("o", j, t)
                for kt in range(KT):
                    ins = nc.tensor.matmul(out[:, 0:OUT_COLS], mixT[:, kt, t * P:(t + 1) * P], w[:, kt, :],
                                           start=(kt == 0), stop=(kt == KT - 1))
                close(ins)
        pe.wait_ge(S["parts_ready"], N_MOD)
        for k in range(2):
            for f in range(2):
                spread(("fgate", k, f), 10 + f, k)
        for k in range(2):
            for f in range(2):
                spread(("fscale", k, f), 8 + f, k)
                spread(("fshift", k, f), 6 + f, k)
        for t in range(NT):
            for g in range(2):
                emptied(pe, "fshift", t // 2, g)
                out = open_job("fT", t, g)
                for k in range(4):
                    kt = 4 * g + k
                    ins = turn(out[:, k * P:(k + 1) * P], h[:, t, kt * P:(kt + 1) * P])
                close(ins)
        for t in range(NT):
            emptied(pe, "fT", t, 1)
            out = open_job("logit", t)
            for kt in range(KT):
                ins = nc.tensor.matmul(out[:, 0:NE], hT[:, kt, t * P:(t + 1) * P], w_rt[:, kt, :],
                                       start=(kt == 0), stop=(kt == KT - 1))
            close(ins)
        chosen = hq[:, 2048:2048 + NT * NE // 2].bitcast(BF16).rearrange("p (t e) -> p t e", t=NT)
        pe.wait_ge(S["logits_exp"], 1)
        for t in range(NT):
            out = open_job("rank", t)
            for s in range(t + 1):
                ins = nc.tensor.matmul(out[:, 0:NE], before[:, 1 if s < t else 0, :], chosen[:, s, :], start=(s == 0),
                                       stop=(s == t))
            close(ins)
        out = open_job("count")
        for s in range(NT):
            ins = nc.tensor.matmul(out[:, 0:NE], before[:, 1, :], chosen[:, s, :], start=(s == 0), stop=(s == NT - 1))
        close(ins)

        pe.wait_ge(S["v_emptied"], n_all["v"])
        pe.wait_ge(S["a_emptied"], n_all["a"])
        pe.wait_ge(S["bias_ready"], 1)
        t_bank = [ps[:, 6, :], ps[:, 7, :]]

        def turn_x(r, bk):
            for k in range(4):
                kt = 4 * r + k
                ins = turn(t_bank[bk][:, k * P:(k + 1) * P], x_slots[:, kt * P:(kt + 1) * P])
            ins.then_inc(S["xT_filled"], 1)

        pe.wait_ge(S["gathered"], 16)
        turn_x(0, 0)
        turn_x(1, 1)

        def expert_block(i):
            pe.wait_ge(S["sel_ready"], i + 1)
            pe.wait_ge(S["xT_ready"], i * 2 + 2)
            for f in range(2):
                pe.wait_ge(S["gu_emptied"], i * 2 + f + 1)
                for s in range(2):
                    nc.tensor.matmul(ps[:, 2 * f + s, :], sel_e[:, :],
                                     bias_parts[:, s * D + f * 512:s * D + (f + 1) * 512], start=True, stop=False)
                for j in range(4):
                    n = 4 * f + j
                    pe.wait_ge(slot_sem[moe_slot(n)], moe_full(i, n))
                    w = ring[:, moe_slot(n), :].rearrange("p (k s n) -> p k s n", k=2, s=2)
                    for k in range(2):
                        for s in range(2):
                            ins = nc.tensor.matmul(ps[:, 2 * f + s, :], x_slotsT[:, 2 * j + k, :], w[:, k, s, :],
                                                   start=False, stop=(j == 3 and k == 1))
                    ins.then_inc(S["unit_used"], 1)

            def turn_act(f, bk):
                pe.wait_ge(S["act_ready"], i * 2 + f + 3)
                for k in range(4):
                    ins = turn(t_bank[bk][:, k * P:(k + 1) * P], act[:, f, k * P:(k + 1) * P])
                ins.then_inc(S["actT_filled"], 1)

            def down(f):
                pe.wait_ge(S["actT_ready"], i * 2 + f + 1)
                for j in range(2):
                    n = 8 + 2 * f + j
                    pe.wait_ge(slot_sem[moe_slot(n)], moe_full(i, n))
                    w = ring[:, moe_slot(n), :].rearrange("p (k s n) -> p k s n", k=2, s=2)
                    for k in range(2):
                        for s in range(2):
                            ins = nc.tensor.matmul(ps[:, 4 + s, :], actT[:, 4 * f + 2 * j + k, :], w[:, k, s, :],
                                                   start=False, stop=(f == 1 and j == 1 and k == 1))
                    ins.then_inc(S["unit_used"], 1)

            turn_act(0, 0)
            pe.wait_ge(S["gathered"], i * 16 + 32)
            turn_x(0, 1)
            pe.wait_ge(S["actT_ready"], i * 2 + 1)
            turn_x(1, 0)
            pe.wait_ge(S["y_copied"], i + 1)
            for s in range(2):
                ins = nc.tensor.matmul(ps[:, 4 + s, :], sel_e[:, :], bias_parts[:, 2 * D + s * 512:2 * D + (s + 1) * 512],
                                       start=True, stop=False)
            ins.then_inc(S["bias_done"], 1)
            down(0)
            pe.wait_ge(S["xT_ready"], i * 2 + 3)
            turn_act(1, 1)
            down(1)

        with pe.Fori(0, NE) as i:
            expert_block(i)
        pe.wait_ge(S["table_ready"], 1)
        n_ovf = pe.value_load(ovf_table[0:1, NOVF:NOVF + 1], min_val=0, max_val=NOVF)
        with pe.If(n_ovf > 0):
            with pe.Fori(NE, n_ovf + NE) as i:
                expert_block(i)

    stack.close()


def layouts(i):
    def c(a):
        return np.ascontiguousarray(a)

    def rows(a, n):
        return np.broadcast_to(a, (n,) + a.shape)

    k = shape_constants()
    x = np.concatenate([i["x_prompt"].reshape(NP_T, P, D), i["x_sample"].reshape(1, P, D)])
    cond = np.concatenate([i["c_prompt"], i["c_sample"]])
    ada = i["w_ada"][0].reshape(2, 4, P, N_MOD, 512).transpose(3, 0, 2, 1, 4)
    g2 = np.zeros((N_MOD, 512), np.float32)
    g2[2:4], g2[8:10] = i["g_attn_norm"][0].reshape(2, 512), i["g_ffn_norm"][0].reshape(2, 512)
    ada_rows = np.stack([i["b_ada"][0].reshape(N_MOD, 512), g2], axis=1)
    gu = i["w_gate_up"][0].reshape(NE, 4, 2, P, 2, 2, 512).transpose(0, 5, 1, 3, 2, 4, 6)
    dn = i["w_down"][0].reshape(NE, 4, 2, P, D).transpose(0, 1, 3, 2, 4)
    moe = np.concatenate([gu.reshape(NE, 8, P, UNIT), dn.reshape(NE, 4, P, UNIT)], axis=1)
    sk = i["swa_sinks"][0]
    w_in = i["w_in"][0]
    w_qs = w_in[:, O_QS:O_KS].reshape(D, KVH, GRP, HD).transpose(0, 2, 1, 3).reshape(D, H * HD)
    w_in = np.concatenate([w_in[:, :O_QS], w_qs, w_in[:, O_KS:]], axis=1)
    return {
        "x_in": c(x),
        "c_t": c(cond.T.reshape(KT, P, 9).transpose(1, 0, 2)),
        "cache_lat": c(i["cache_mla_latent"][0].reshape(NB_DEC, PAST // P, P, KVL).transpose(0, 2, 1, 3)),
        "cache_lat_t": c(i["cache_mla_latent"][0].reshape(NB_DEC, PAST, 2, P).transpose(0, 3, 2, 1)),
        "cache_kr_t": c(i["cache_mla_krope"][0].transpose(0, 2, 1)),
        "cache_k_t": c(i["cache_swa_k"][0].reshape(NB_DEC, WINDOW, KVH * HD).transpose(0, 2, 1)),
        "cache_v": c(i["cache_swa_v"][0].reshape(NB_DEC, WINDOW, KVH * HD)),
        "cache_k_rows": c(i["cache_swa_k"][0].reshape(NB_DEC, WINDOW, KVH * HD)),
        "ada_w": c(ada.reshape(N_MOD, 2, P, UNIT)),
        "ada_rows": c(np.broadcast_to(ada_rows[:, None], (N_MOD, 9, 2, 512))),
        "in_w": c(w_in.reshape(KT, P, 6, IN_COLS).transpose(2, 1, 0, 3).reshape(6, P, KT * IN_COLS)),
        "uq_w": c(i["w_uq"][0].reshape(3, P, H * QK).transpose(1, 0, 2)),
        "ukv_w": c(i["w_ukv"][0].reshape(2, P, H, NOPE + VD).transpose(1, 0, 2, 3)),
        "uk_t": c(i["w_ukv"][0][:, :, 0:NOPE].transpose(2, 1, 0)),
        "out_w": c(i["w_out"][0].reshape(KT, P, 4, OUT_COLS).transpose(2, 1, 0, 3).reshape(4, P, KT * OUT_COLS)),
        "rows_q_kv": c(rows(np.concatenate([i["g_q_norm"][0], i["g_kv_norm"][0]]), P)),
        "sink_cols": c(np.concatenate([rows(sk, P), np.repeat(sk, Q_DEC)[:, None]], axis=1)),
        "router_w": c(i["w_router"][0].reshape(KT, P, NE).transpose(1, 0, 2)),
        "router_b": c(rows(i["b_router"][0], P)),
        "moe_w": c(moe),
        "moe_b": c(np.concatenate([i["b_gate_up"][0], i["b_down"][0]], axis=1)),
        "g_final": c(rows(i["g_final"], P)),
        "c_ident": k["ident"], "c_rope": k["rope"], "c_causal": k["causal"], "c_dist": k["dist"],
        "c_alibi": k["alibi"], "c_kind": k["kind_sel"].reshape(96, 2 * P), "c_before": k["before"].reshape(P, 2 * P),
        "c_eid": k["expert_id"], "c_rowe": k["row_expert"], "c_blk": k["block_id"].reshape(P, NOVF, NE),
        "c_tok": k["token_id"],
    }


def kernel(**inputs):
    import concourse.bacc as _bacc
    from concourse.bass_utils import run_bass_kernel_spmd as _run

    nc = _bacc.Bacc("TRN2", target_bir_lowering=False, num_devices=1)
    arrays, ins, outs = {}, [], []
    for name, a in layouts({k: np.asarray(v) for k, v in inputs.items()}).items():
        arrays[f"in_{name}"] = a
        ins.append(nc.dram_tensor(f"in_{name}", a.shape, mybir.dt.from_np(a.dtype), kind="ExternalInput").ap())
    for n, shape in enumerate(OUT_SHAPES):
        outs.append(nc.dram_tensor(f"out_{n}", shape, F32, kind="ExternalOutput").ap())
    build(nc, ins, outs)
    r = _run(nc, [arrays], core_ids=[0])
    return tuple(r.results[0][f"out_{n}"] for n in range(len(OUT_SHAPES)))
```

```python
from contextlib import ExitStack

import numpy as np

import concourse.bass as bass
from concourse import mybir

F32 = mybir.dt.float32
F32R = mybir.dt.float32r
BF16 = mybir.dt.bfloat16
I32 = mybir.dt.int32
U32 = mybir.dt.uint32
ALU = mybir.AluOpType
ACT = mybir.ActivationFunctionType
AX = mybir.AxisListType.X

P = 128
D = 1024
KT = D // P
SEQ, NB_DEC, Q_DEC, PAST = 256, 8, 16, 512
NT = 3
NP_T = 2
CHUNK, WINDOW = 64, 128
H, NOPE, ROPE, VD = 8, 64, 32, 64
QK = NOPE + ROPE
QL, KVL = 384, 256
KVH, GRP, HD = 2, 4, 64
IN_W = QL + KVL + ROPE + H * HD + 2 * KVH * HD
O_KV, O_KPE, O_QS = QL, QL + KVL, QL + KVL + ROPE
O_KS = O_QS + H * HD
O_VS = O_KS + KVH * HD
MLA_SCALE = float(QK) ** -0.5
SWA_SCALE = float(HD) ** -0.5
NE, TOPK = 32, 4
DFF = D
EPS = 1e-6
BIG = 1e30

UNIT = 2048
SLOTS = 6
IN_COLS = IN_W // 6
OUT_COLS = 256
N_MOD = 6 * D // 512
EARLY_MOD = 6
SPLIT = 4
PIECES = 6
PIECE_AT = (0, 2, 3, 5)
PIECE_N = (2, 1, 2, 1)
MOE_UNITS = 12
NOVF = NT * P * TOPK // (P + 1)
NBLK = NE + NOVF + 1

QUERY_ORDER = (("q", 0), ("q", 1), ("qT", 0), ("q", 2), ("qT", 1), ("qT", 2))

OUT_SHAPES = [
    (1, SEQ, D), (NB_DEC, Q_DEC, D),
    (1, 1, SEQ, KVL), (1, 1, SEQ, ROPE), (1, 1, WINDOW, KVH, HD), (1, 1, WINDOW, KVH, HD),
    (1, NB_DEC, Q_DEC, KVL), (1, NB_DEC, Q_DEC, ROPE),
    (1, NB_DEC, WINDOW, KVH, HD), (1, NB_DEC, WINDOW, KVH, HD),
]


def shape_constants():
    c = {}
    c["ident"] = np.eye(P, dtype=np.float32)
    pos = np.concatenate([np.arange(SEQ), np.tile(PAST + np.arange(Q_DEC), NB_DEC)]).astype(np.float32)
    inv = np.float32(10000.0) ** (-np.arange(ROPE // 2, dtype=np.float32) * np.float32(2.0) / np.float32(ROPE))
    ang = (pos[:, None] * inv[None, :]).astype(np.float32)
    cs = np.concatenate([np.cos(ang), np.sin(ang)], axis=1).astype(np.float32)
    c["rope"] = np.ascontiguousarray(cs.reshape(NT, P, ROPE).transpose(1, 0, 2))
    q = np.arange(SEQ)
    qc, kc = q[:, None] // CHUNK, q[None, :] // CHUNK
    mask = np.where(kc <= qc, 0.0, -BIG).astype(np.float32)
    c["causal"] = np.ascontiguousarray(mask.reshape(NP_T, P, SEQ).transpose(1, 0, 2))
    seen = (kc <= qc) & (kc >= qc - WINDOW // CHUNK)
    dist = np.where(seen, np.abs(q[:, None] - q[None, :]), BIG * 1e4).astype(np.float32)
    c["dist"] = np.ascontiguousarray(dist.reshape(NP_T, P, SEQ).transpose(1, 0, 2))
    slope = 2.0 ** (-8.0 * np.arange(1, H + 1) / H)
    rel = np.abs(np.arange(Q_DEC)[:, None] + WINDOW - np.arange(WINDOW + Q_DEC)[None, :])
    c["alibi"] = (-slope[:, None, None] * rel[None] / SWA_SCALE).reshape(P, WINDOW + Q_DEC).astype(np.float32)
    sel = np.zeros((96, 2, P), np.float32)
    for part in range(3):
        sel[32 * part, 0, :] = 1.0
        for t in range(P):
            sel[32 * part + 1 + t // Q_DEC, 1, t] = 1.0
    c["kind_sel"] = sel
    tri = np.zeros((P, 2, P), np.float32)
    tri[:, 0, :] = np.triu(np.ones((P, P)), 1)
    tri[:, 1, :] = 1.0
    c["before"] = tri
    c["expert_id"] = np.tile(np.arange(NE, dtype=np.float32), (P, 1))
    c["row_expert"] = np.tile((np.arange(96) % 32).astype(np.float32)[:, None], (1, P))
    c["block_id"] = np.tile(np.arange(NOVF, dtype=np.float32)[:, None], (1, NE)).reshape(1, -1).repeat(P, 0)
    c["token_id"] = (np.arange(NT)[None, :] * P + np.arange(P)[:, None]).astype(np.float32)
    c["slot_id"] = np.tile(np.arange(P, dtype=np.float32), (P, 1))
    return c


def psum_jobs():
    early = [(("mod", n), "v") for n in range(4)]
    early += [(("mod", 4), "v")]
    early += [(("b" + w, k, f), "v") for k in range(2) for f in range(2) for w in ("scale", "shift")]
    early += [(("mod", 5), "v")]
    early += [(("hT", t, g), "a") for t in range(NT) for g in range(2)]
    early += [(("u", j, t), "a") for j in range(6) for t in range(NT)]
    early += [(("qlT", t), "a") for t in range(NT)]
    early += [(("ckT", t), "a") for t in range(NT)]
    early += [(("qsT", t), "a") for t in range(NT)] + [(("ksT",), "a")]
    early += [(("gate", k, f), "a") for k in range(2) for f in range(2)]
    early += [(("v", t), "a") for t in range(NP_T)]
    early += [((w, t, f), "v" if w == "q" else "a") for w, t in QUERY_ORDER for f in range(2)]
    early += [(("qabs", p), "a") for p in range(4)] + [(("kT", p), "a") for p in range(4)]
    late = [(("oS",), "a")]
    late += [(("o", j, t), "v") for j in range(4) for t in range(NT)]
    late += [(("fgate", k, f), "a") for k in range(2) for f in range(2)]
    late += [(("f" + w, k, f), "v") for k in range(2) for f in range(2) for w in ("scale", "shift")]
    late += [(("fT", t, g), "a") for t in range(NT) for g in range(2)]
    late += [(("logit", t), "v") for t in range(NT)]
    late += [(("rank", t), "v") for t in range(NT)] + [(("count",), "v"), (("table",), "v")]
    return early, late


def attention_items():
    items = []
    for b in range(NB_DEC):
        for j in (2 * b, 2 * b + 1):
            items += [("mla", j // H, j % H), ("swa", j // H, j % H)]
        items += [("mla_s", b, 0), ("swa_s", b, 0)]
    return items



def build(nc, ins, outs):
    (x_in, c_t, cache_lat, cache_lat_t, cache_kr_t, cache_k_t, cache_v, cache_k_rows, ada_w, ada_rows,
     in_w, uq_w, ukv_w, uk_t, out_w, rows_q_kv, sink_cols, router_w, router_b, moe_w, moe_b, g_final,
     c_ident, c_rope, c_causal, c_dist, c_alibi, c_kind, c_before, c_eid, c_rowe, c_blk, c_tok, c_slot) = ins
    (o_yp, o_ys, o_latp, o_krp, o_kp, o_vp, o_lats, o_krs, o_ks, o_vs) = outs
    stack = ExitStack()

    def sb(name, shape, dt=F32, scope=stack):
        return scope.enter_context(nc.sbuf_tensor(name, shape, dt))

    def sem(name):
        return stack.enter_context(nc.semaphore(name))

    h_rows = nc.dram_tensor("h_rows", [NT * P, D], F32, kind="Internal").ap()
    y_rows = nc.dram_tensor("y_rows", [(NBLK - 1) * P, D], F32, kind="Internal").ap()

    ps = stack.enter_context(nc.psum_tensor("ps", [P, 8, 512], F32))

    ring = sb("ring", [P, SLOTS, UNIT])
    x = sb("x", [P, NT, D])
    mod_parts = sb("mod_parts", [96, 6 * D], BF16)
    gates = sb("gates", [P, 2, D])
    ident = sb("ident", [P, P])
    kind_sel = sb("kind_sel", [96, 2, P], BF16)
    before = sb("before", [P, 2, P], BF16)
    expert_id = sb("expert_id", [P, NE])
    row_expert = sb("row_expert", [96, P])
    block_id = sb("block_id", [P, NOVF, NE])
    token_id = sb("token_id", [P, NT])
    slot_id = sb("slot_id", [P, P])
    gate_w = sb("gate_w", [P, NT, TOPK])
    y_row_idx = sb("y_row_idx", [P, NT * TOPK], I32)
    slot_tok = sb("slot_tok", [P, NBLK], I32)
    block_expert = sb("block_expert", [P, NBLK])
    ovf_table = sb("ovf_table", [1, NOVF + 1], I32)
    stat = sb("stat", [P, 64])

    pre = ExitStack()

    def pb(name, shape, dt=F32):
        return sb(name, shape, dt, pre)

    hm = pb("hm", [P, KT, NT * P])
    hq = pb("hq", [P, NT * D])
    qabs = pb("qabs", [P, 2, NB_DEC, H, Q_DEC])
    kT = pb("kT", [QK, H, SEQ])
    w_ukv = pb("w_ukv", [P, 2, H, NOPE + VD])
    v_p = pb("v_p", [P, NP_T, H * VD])
    v_swa = pb("v_swa", [P, NT, KVH * HD])
    qsT = pb("qsT", [P, NP_T, GRP, P])
    qsT_s = pb("qsT_s", [P, NB_DEC, GRP, Q_DEC])
    ksT = pb("ksT", [P, NT * P])
    ckT = pb("ckT", [P, 2, NT * P])
    kpT = pb("kpT", [QK, NT * P])
    q_tok = pb("q_tok", [P, H, QK])
    rope = pb("rope", [P, NT, ROPE])
    rt = pb("rt", [P, 4, 96])
    causal = pb("causal", [P, NP_T, SEQ])
    dist = pb("dist", [P, NP_T, SEQ])
    alibi = pb("alibi", [P, WINDOW + Q_DEC])
    g_qkv = pb("g_qkv", [P, QL + KVL])
    sinks = pb("sinks", [P, H + 1])
    sinks_s = pb("sinks_s", [P, H + 1])
    w_rt = pb("w_rt", [P, KT, NE])
    b_rt = pb("b_rt", [P, NE])
    cT = pb("cT", [P, KT, 9])
    cs = pb("cs", [P, KT, 9])
    mod_rows = pb("mod_rows", [9, 2, 512])
    mod_row = pb("mod_row", [9, 512])
    mod_res = pb("mod_res", [9, 512])
    mod_p2 = pb("mod_p2", [9, 512], BF16)
    row_max = pb("row_max", [P, 48])
    neg_max = pb("neg_max", [P, 48])
    row_sum = pb("row_sum", [P, 48])
    sink_e = pb("sink_e", [P, 48])
    row_inv = pb("row_inv", [P, 48])
    rtr = pb("rtr", [P, 12, NE])
    h = hq[:, :].rearrange("p (t d) -> p t d", t=NT)
    qT = hq[0:QK, 0:NP_T * H * P].rearrange("p (t h n) -> p t h n", t=NP_T, h=H)
    qT_s = hq[0:QK, NP_T * H * P:].rearrange("p (b h q) -> p b h q", b=NB_DEC, h=H)
    hT = hm
    mixT = hm
    w_uq = hm[:, :, :].rearrange("p k t -> p (k t)")[:, 0:3 * H * QK].rearrange("p (k n) -> p k n", k=3)
    qlT = qabs[:, :, :, :, :].rearrange("p a b h q -> p (a b h q)")[:, 0:3 * NT * P].rearrange(
        "p (k t) -> p k t", k=3)
    wukT = kT[0:NOPE, :, :]
    q_flat = q_tok[:, :, :].rearrange("p h d -> p (h d)")
    cv_s = q_flat[:, 0:2 * P].rearrange("p (b n) -> p b n", b=2)
    new_v = q_flat[0:Q_DEC, 2 * P:4 * P].rearrange("p (b n) -> p b n", b=2)
    tail_base = nc.sbuf_base

    su = ExitStack()
    u = sb("u", [P, NT, IN_W], F32, su)
    su.close()

    st = ExitStack()
    early_rows = sb("early_rows", [9, EARLY_MOD, 2, 512], F32, st)
    st.close()

    att = ExitStack()
    latT = sb("latT", [P, 2, 2, PAST], F32, att)
    lat = sb("lat", [P, 2, PAST // P, KVL], F32, att)
    krT = sb("krT", [QK, 2, PAST], F32, att)
    ck_sT = sb("ck_sT", [P, 2, WINDOW], F32, att)
    new_lat = sb("new_lat", [Q_DEC, 2, KVL], F32, att)
    probs = sb("probs", [P, 2, PAST + Q_DEC], F32, att)
    pT = sb("pT", [P, 2, 5 * P], F32, att)
    att.close()

    late = ExitStack()
    bias_parts = sb("bias_parts", [96, 3 * D], BF16, late)
    bias_src = sb("bias_src", [NE, 3 * D], F32, late)
    bias_p2 = sb("bias_p2", [NE, 3 * D], BF16, late)
    late.close()
    pre.close()

    moe = ExitStack()
    x_slots = sb("x_slots", [P, D], F32, moe)
    xT_hi = sb("xT_hi", [P, PIECES, P], F32R, moe)
    xT_lo = sb("xT_lo", [P, PIECES, P], F32R, moe)
    xT_raw = sb("xT_raw", [P, 2, P], F32, moe)
    aT_hi = sb("aT_hi", [P, PIECES, P], F32R, moe)
    aT_lo = sb("aT_lo", [P, PIECES, P], F32R, moe)
    aT_raw = sb("aT_raw", [P, 2, P], F32, moe)
    y_blk = sb("y_blk", [P, D], F32, moe)
    glu = sb("glu", [P, 2, 512], F32, moe)
    w_hi = sb("w_hi", [P, PIECES, UNIT // 2], F32R, moe)
    w_lo = sb("w_lo", [P, PIECES, UNIT // 2], F32R, moe)
    sig = sb("sig", [P, 2, 512], F32, moe)
    lin = sb("lin", [P, 2, 512], F32, moe)
    sel_e = sb("sel_e", [96, P], BF16, moe)
    cur_idx = sb("cur_idx", [P, 1], I32, moe)
    assert nc.sbuf_base <= tail_base, (nc.sbuf_base, tail_base)
    moe.close()
    y_got = ring[:, 2:4, :].rearrange("p s (b n) -> p (s b) n", b=2)
    y_acc = lin[:, :, :].rearrange("p a b -> p (a b)")
    gfin = sig[:, :, :].rearrange("p a b -> p (a b)")

    S = {}
    for name in (
            "loaded_c loaded_tables loaded_x loaded_small loaded_uq loaded_rows loaded_bias loaded_gfin "
            "psum_filled v_emptied a_emptied unit_used v_step a_step p_step zeroed consts_cast "
            "sig_ready silu_ready ss_ready ms_ready root_ready parts_ready h_done ql_ready ck_ready u_stats "
            "lat_stored out_stored rows_zeroed v_swa_ready "
            "scored maxed exped normed flipped pT_ready pv_done o_ready mod_extra mod_extra_used caches_ready "
            "x1_ready h_ready bias_ready logits_exp gates_exped probs_top placed h_stored table_ready "
            "sel_ready bias_done gu_emptied glu_ready sig_done act_ready hi_ready lo_ready xT_hi_ready aT_hi_ready actT_filled actT_ready "
            "xT_filled xT_ready gathered idx_ready y_copied y_stored x_flip "
            "got0 got1 got2 got3 acc_done fin_ss fin_root fin_ready fin_ms fin_stored gsg_ready pool_gate").split():
        S[name] = sem(name)
    slot_sem = [sem(f"slot_full{s}") for s in range(SLOTS)]
    cache_sem = [sem(f"cache_full{s}") for s in range(2)]
    (x_sem, ) = (S["loaded_x"], )

    early, late_jobs = psum_jobs()
    jobs = early + late_jobs
    number = {key: i for i, (key, _) in enumerate(jobs)}
    engine_of = dict(jobs)
    ordinal, seen = {}, {"v": 0, "a": 0}
    for key, who in jobs:
        seen[who] += 1
        ordinal[key] = seen[who]

    def bank(*key):
        return ps[:, number[key] % 8, :]

    def filled(eng, *key):
        eng.wait_ge(S["psum_filled"], number[key] + 1)

    def emptied(eng, *key):
        eng.wait_ge(S["v_emptied"] if engine_of[key] == "v" else S["a_emptied"], ordinal[key])

    n_early = {w: sum(1 for _, e in early if e == w) for w in "va"}
    n_all = {w: sum(1 for _, e in jobs if e == w) for w in "va"}

    units = [("ada", n, f) for n in range(EARLY_MOD) for f in range(2)]
    units += [("in", j) for j in range(6)]
    units += [("ada", n, f) for n in range(EARLY_MOD, N_MOD) for f in range(2)]
    units += [("out", j) for j in range(4)]
    unit_no = {k: i for i, k in enumerate(units)}
    N_PRE = len(units)
    N_TABLES = 15
    HALVES = N_MOD

    def unit(key):
        return ring[:, unit_no[key] % SLOTS, :]

    def unit_here(eng, key):
        n = unit_no[key]
        eng.wait_ge(slot_sem[n % SLOTS], 16 * (n // SLOTS + 1))

    def used_up(eng, key):
        if key[0] == "ada" and key[2] == 0:
            eng.wait_ge(S["unit_used"], key[1] + 1)
        elif key[0] == "ada" and key[1] < EARLY_MOD:
            filled(eng, "mod", key[1])
        elif key[0] == "ada":
            eng.wait_ge(S["mod_extra"], key[1] - EARLY_MOD + 1)
        else:
            filled(eng, "u" if key[0] == "in" else "o", key[1], NT - 1)

    def moe_slot(j):
        return (N_PRE + j) % SLOTS

    assert all(moe_slot(j) not in (2, 3) for j in range(SPLIT))

    def moe_full(i, j):
        return ((N_PRE + j) // SLOTS + 1) * 16 + i * (16 * MOE_UNITS // SLOTS)

    def moe_used(i, j):
        return i * MOE_UNITS + (HALVES + j + 1)

    def piece(w, n):
        return w[:, PIECE_AT[n % 4]:PIECE_AT[n % 4] + PIECE_N[n % 4], :].rearrange("p k n -> p (k n)")

    def piece_src(n):
        return ring[:, moe_slot(n), 0:PIECE_N[n % 4] * UNIT // 2]

    items = attention_items()
    t_bank = [ps[:, 6, :], ps[:, 7, :]]

    def width(i):
        kind, n, _ = items[i]
        return {"mla": P * (n + 1), "swa": P * (n + 1), "mla_s": PAST + Q_DEC, "swa_s": WINDOW + Q_DEC}[kind]

    def full_tiles(i):
        kind, n, _ = items[i]
        return {"mla": n + 1, "swa": n + 1, "mla_s": PAST // P, "swa_s": 1}[kind]

    score_bank = (3, 0, 2, 3, 0, 2)

    def scores(i):
        b = score_bank[i % 6]
        return ps[:, b:b + (2 if items[i][0] == "mla_s" else 1), :].rearrange("p a b -> p (a b)")

    def place_where():
        flat = hm[:, :, :].rearrange("p k t -> p (k t)")
        n_place = NT * TOPK * P
        return (flat[:, 0:n_place].rearrange("p (n s) -> p n s", s=P),
                flat[:, n_place:n_place + NT * TOPK * NBLK].rearrange("p (n b) -> p n b", b=NBLK))

    block = stack.enter_context(nc.Block())

    @block.sync
    def _(sp):
        for n, key in enumerate(units):
            if n >= SLOTS:
                used_up(sp, units[n - SLOTS])
            if key[0] == "ada":
                src, dst = ada_w[key[1], key[2]], ring[:, n % SLOTS, :]
            elif key[0] == "in":
                src, dst = in_w[key[1]], ring[:, n % SLOTS, 0:KT * IN_COLS]
            else:
                src, dst = out_w[key[1]], ring[:, n % SLOTS, :]
            nc.sync.dma_start(dst, src).then_inc(slot_sem[n % SLOTS], 16)

        def stream(i, expert):
            for j in range(MOE_UNITS):
                if PIECE_N[j % 4] == 2:
                    sp.wait_ge(S["lo_ready"], i * MOE_UNITS + (j + 1))
                else:
                    sp.wait_ge(S["unit_used"], moe_used(i, j - SLOTS))
                src = moe_w[bass.ds(expert, 1), j].rearrange("e p n -> (e p) n")
                nc.sync.dma_start(ring[:, moe_slot(j), :], src).then_inc(slot_sem[moe_slot(j)], 16)

        used_up(sp, units[-1])
        with sp.Fori(0, NE) as i:
            stream(i, i)
        sp.wait_ge(S["table_ready"], 1)
        n_ovf = sp.value_load(ovf_table[0:1, NOVF:NOVF + 1], min_val=0, max_val=NOVF)
        with sp.If(n_ovf > 0):
            with sp.Fori(NE, n_ovf + NE) as i:
                expert = sp.value_load(ovf_table[0:1, bass.ds(i - NE, 1)], min_val=0, max_val=NE - 1)
                stream(i, expert)
        for j in range(SPLIT):
            if PIECE_N[j % 4] == 2:
                sp.wait_ge(S["lo_ready"], (n_ovf + NE) * MOE_UNITS + (j + 1))
            else:
                sp.wait_ge(S["unit_used"], moe_used(n_ovf + NE, j - SLOTS))
            nc.sync.dma_start(ring[:, moe_slot(j), :], moe_w[0, j]).then_inc(slot_sem[moe_slot(j)], 16)

    @block.gpsimd
    def _(pool):
        nc.gpsimd.dma_start(early_rows[:, :, :, :], ada_rows[0:EARLY_MOD].rearrange("n r a c -> r n a c")).then_inc(
            S["loaded_rows"], 16)
        pool.wait_ge(S["loaded_small"], 16 * 3)
        qf = q_tok[:, :, :].rearrange("p h d -> p (h d)")
        nc.gpsimd.tensor_copy(kind_sel[:, :, :].rearrange("p a b -> p (a b)"), qf[0:96, 0:2 * P]).then_inc(S["consts_cast"], 1)
        nc.gpsimd.tensor_copy(before[:, :, :].rearrange("p a b -> p (a b)"), qf[:, 2 * P:4 * P]).then_inc(S["consts_cast"], 1)

        zeros = qabs[:, :, :, :, :].rearrange("p a b h q -> p (a b h q)")[:, 0:D]
        nc.gpsimd.memset(zeros, 0.0).then_inc(S["zeroed"], 1)
        pool.wait_ge(S["zeroed"], 1)
        filled(pool, "u", 0, 0)
        for n in range(NE, NBLK - 1):
            nc.gpsimd.dma_start(y_rows[n * P:(n + 1) * P, :], zeros).then_inc(S["rows_zeroed"], 16)
        nc.gpsimd.dma_start(o_ks[0, :, 0:WINDOW - Q_DEC].rearrange("b t k d -> b t (k d)"),
                            cache_k_rows[:, Q_DEC:WINDOW]).then_inc(S["out_stored"], 16)
        nc.gpsimd.dma_start(o_vs[0, :, 0:WINDOW - Q_DEC].rearrange("b t k d -> b t (k d)"),
                            cache_v[:, Q_DEC:WINDOW]).then_inc(S["out_stored"], 16)

        filled(pool, "u", 5, NT - 1)
        nc.gpsimd.dma_start(w_uq, uq_w).then_inc(S["loaded_uq"], 16)

        pool.wait_ge(S["ck_ready"], 1)
        for t in range(NP_T):
            nc.gpsimd.dma_start(o_latp[0, 0, t * P:(t + 1) * P], u[:, t, O_KV:O_KPE]).then_inc(S["out_stored"], 16)
            nc.gpsimd.dma_start(o_krp[0, 0, t * P:(t + 1) * P], u[:, t, O_KPE:O_QS]).then_inc(S["out_stored"], 16)
        nc.gpsimd.dma_start(o_kp[0, 0].rearrange("t k d -> t (k d)"), u[:, 1, O_KS:O_VS]).then_inc(S["out_stored"], 16)
        nc.gpsimd.dma_start(o_vp[0, 0].rearrange("t k d -> t (k d)"), u[:, 1, O_VS:IN_W]).then_inc(S["out_stored"], 16)
        nc.gpsimd.dma_start(o_krs[0].rearrange("b q c -> (b q) c"), u[:, 2, O_KPE:O_QS]).then_inc(S["out_stored"], 16)
        nc.gpsimd.dma_start(o_lats[0].rearrange("b q c -> (b q) c"), u[:, 2, O_KV:O_KPE]).then_inc(S["lat_stored"], 16)
        for b in range(NB_DEC):
            rows = slice(b * Q_DEC, (b + 1) * Q_DEC)
            nc.gpsimd.dma_start(o_ks[0, b, WINDOW - Q_DEC:WINDOW].rearrange("t k d -> t (k d)"),
                                u[rows, 2, O_KS:O_VS]).then_inc(S["out_stored"], 16)
            nc.gpsimd.dma_start(o_vs[0, b, WINDOW - Q_DEC:WINDOW].rearrange("t k d -> t (k d)"),
                                u[rows, 2, O_VS:IN_W]).then_inc(S["lat_stored"], 16)
        n_out = 2 + 2 * NP_T + 3 + NB_DEC

        pool.wait_ge(S["out_stored"], 16 * n_out)
        pool.wait_ge(S["lat_stored"], 16 * (1 + NB_DEC))
        pool.wait_ge(S["v_swa_ready"], 1)
        filled(pool, "ksT")
        filled(pool, "ckT", NT - 1)
        filled(pool, "qlT", NT - 1)
        filled(pool, "qsT", NT - 1)
        filled(pool, "qT", NT - 1, 1)
        for b in range(NB_DEC):
            if b >= 2:
                pool.wait_ge(S["pv_done"], 6 * (b - 1))
            k = b % 2
            for dst, src in ((latT[:, k], cache_lat_t[b]), (lat[:, k], cache_lat[b]),
                             (krT[NOPE:QK, k], cache_kr_t[b]), (ck_sT[:, k], cache_k_t[b]), (cv_s[:, k], cache_v[b]),
                             (new_lat[:, k], o_lats[0, b]),
                             (new_v[:, k], o_vs[0, b, WINDOW - Q_DEC:WINDOW].rearrange("t k d -> t (k d)"))):
                nc.gpsimd.dma_start(dst, src).then_inc(cache_sem[k], 16)
            if b < N_MOD - EARLY_MOD:
                pool.wait_ge(S["parts_ready"], EARLY_MOD + b)
                nc.gpsimd.dma_start(mod_rows[:, :, :], ada_rows[EARLY_MOD + b]).then_inc(S["loaded_rows"], 16)

        pool.wait_ge(S["o_ready"], len(items))
        nc.gpsimd.dma_start(bias_src[:, :], moe_b).then_inc(S["loaded_bias"], 16)
        pool.wait_ge(S["loaded_bias"], 16)
        steps = [0]

        def step(ins):
            steps[0] += 1
            ins.then_inc(S["p_step"], 1)
            pool.wait_ge(S["p_step"], steps[0])

        step(nc.gpsimd.tensor_copy(bias_parts[0:NE, :], bias_src[:, :]))
        step(nc.gpsimd.tensor_tensor(bias_src[:, :], bias_src[:, :], bias_parts[0:NE, :], ALU.subtract))
        step(nc.gpsimd.tensor_copy(bias_p2[:, :], bias_src[:, :]))
        step(nc.gpsimd.tensor_tensor(bias_src[:, :], bias_src[:, :], bias_p2[:, :], ALU.subtract))
        step(nc.gpsimd.tensor_copy(bias_parts[NE:2 * NE, :], bias_p2[:, :]))
        nc.gpsimd.tensor_copy(bias_parts[2 * NE:3 * NE, :], bias_src[:, :]).then_inc(S["bias_ready"], 1)
        pool.wait_ge(S["bias_ready"], 1)

        emptied(pool, "table")
        pool.wait_ge(S["h_stored"], 16 * NT)

        def gather(i, first=False):
            if not first:
                pool.wait_ge(S["gathered"], i * 16)
                pool.wait_ge(S["xT_filled"], i * 2)
            col = slot_tok[:, 0:1] if first else slot_tok[:, bass.ds(i, 1)]
            nc.gpsimd.tensor_copy(cur_idx[:, :], col).then_inc(S["idx_ready"], 1)
            pool.wait_ge(S["idx_ready"], 1 if first else i + 1)
            if not first:
                pool.sem_inc(S["pool_gate"], 1)
            nc.gpsimd.indirect_dma_start(
                out=x_slots[:, :], out_offset=None, in_=h_rows,
                in_offset=bass.IndirectOffsetOnAxis(ap=cur_idx[:, 0:1], axis=0)).then_inc(S["gathered"], 16)

        gather(0, first=True)
        with pool.Fori(0, NE) as i:
            gather(i + 1)
        n_ovf = pool.value_load(ovf_table[0:1, NOVF:NOVF + 1], min_val=0, max_val=NOVF)
        with pool.If(n_ovf > 0):
            with pool.Fori(NE, n_ovf + NE) as i:
                gather(i + 1)

        pool.wait_ge(S["y_stored"], (n_ovf + NE) * 16 + 16)
        pool.sem_inc(S["pool_gate"], 1)
        for n in range(NT * TOPK):
            k = n % TOPK
            if n >= TOPK:
                pool.wait_ge(S["acc_done"], n - TOPK + 1)
            nc.gpsimd.indirect_dma_start(
                out=y_got[:, k, :], out_offset=None, in_=y_rows,
                in_offset=bass.IndirectOffsetOnAxis(ap=y_row_idx[:, n:n + 1], axis=0)).then_inc(S[f"got{k}"], 16)
        pool.wait_ge(S["out_stored"], 16 * n_out)
        pool.wait_ge(S["gathered"], (n_ovf + NE + 1) * 16)

    @block.scalar
    def _(a):
        qf = q_tok[:, :, :].rearrange("p h d -> p (h d)")
        nc.scalar.dma_start(cT[:, :, :], c_t).then_inc(S["loaded_c"], 16)
        nc.scalar.dma_start(qf[0:96, 0:2 * P], c_kind).then_inc(S["loaded_small"], 16)
        nc.scalar.dma_start(qf[:, 2 * P:4 * P], c_before).then_inc(S["loaded_small"], 16)
        for t in range(NT):
            nc.scalar.dma_start(x[:, t, :], x_in[t]).then_inc(S["loaded_x"], 16)
        nc.scalar.dma_start(ident[:, :], c_ident).then_inc(S["loaded_small"], 16)

        a.wait_ge(S["loaded_c"], 16)
        csig = rtr[:, :, :].rearrange("p a b -> p (a b)")[:, 0:KT * 9]
        nc.scalar.activation(csig, cT[:, :, :].rearrange("p k n -> p (k n)"), ACT.Sigmoid).then_inc(S["sig_ready"], 1)

        def x_stats(n0):
            for t in range(NT):
                nc.scalar.activation(hq[:, 0:D] if n0 == 0 else hm[:, :, :].rearrange("p k t -> p (k t)")[:, 0:D],
                                     x[:, t, :], ACT.Square, accum_out=stat[:, n0 + t:n0 + t + 1]).then_inc(S["ss_ready"], 1)
                a.wait_ge(S["ss_ready"], (0 if n0 == 0 else NT) + t + 1)
            a.wait_ge(S["ms_ready"], 1 if n0 == 0 else 3)
            nc.scalar.activation(stat[:, n0 + 3:n0 + 6], stat[:, n0 + 6:n0 + 9], ACT.Sqrt).then_inc(S["root_ready"], 1)

        a.wait_ge(S["loaded_x"], 16 * NT)
        x_stats(0)
        rest = ((kT[0:NOPE, :, :], uk_t), (w_ukv[:, :, :, :], ukv_w), (rope[:, :, :], c_rope),
                (causal[:, :, :], c_causal), (dist[:, :, :], c_dist), (alibi[:, :], c_alibi), (g_qkv[:, :], rows_q_kv),
                (sinks[:, :], sink_cols), (w_rt[:, :, :], router_w), (b_rt[:, :], router_b), (expert_id[:, :], c_eid),
                (row_expert[:, :], c_rowe), (block_id[:, :, :], c_blk), (token_id[:, :], c_tok), (slot_id[:, :], c_slot))
        assert len(rest) == N_TABLES
        for dst, src in rest:
            nc.scalar.dma_start(dst, src).then_inc(S["loaded_tables"], 16)

        def empty(key, dst, src, last=True):
            ins = nc.scalar.copy(dst, src)
            if last:
                ins.then_inc(S["a_emptied"], 1)

        for t in range(NT):
            for g in range(2):
                filled(a, "hT", t, g)
                empty(("hT", t, g), hT[:, 4 * g:4 * g + 4, t * P:(t + 1) * P],
                      bank("hT", t, g).rearrange("p (k n) -> p k n", k=4))
        for j in range(6):
            for t in range(NT):
                filled(a, "u", j, t)
                if (j, t) == (0, 0):
                    a.wait_ge(S["parts_ready"], EARLY_MOD)
                empty(("u", j, t), u[:, t, j * IN_COLS:(j + 1) * IN_COLS], bank("u", j, t)[:, 0:IN_COLS])
        a.wait_ge(S["a_emptied"], ordinal[("u", 5, NT - 1)])
        a.wait_ge(S["consts_cast"], 2)
        for t in range(NT):
            for c0, n, o in ((0, QL, 16 + t), (O_KV, KVL, 19 + t)):
                nc.scalar.activation(qf[:, 0:n], u[:, t, c0:c0 + n], ACT.Square, scale=float(n) ** -0.5,
                                     accum_out=stat[:, o:o + 1]).then_inc(S["u_stats"], 1)
                a.wait_ge(S["u_stats"], 2 * t + (2 if c0 else 1))
        a.wait_ge(S["ms_ready"], 2)
        nc.scalar.activation(stat[:, 28:34], stat[:, 22:28], ACT.Sqrt).then_inc(S["root_ready"], 1)
        a.wait_ge(S["rows_zeroed"], 16 * NOVF)
        for t in range(NT):
            filled(a, "qlT", t)
            empty(("qlT", t), qlT[:, :, t * P:(t + 1) * P], bank("qlT", t)[:, 0:3 * P].rearrange("p (k n) -> p k n", k=3))
        for t in range(NT):
            filled(a, "ckT", t)
            nc.scalar.copy(kpT[NOPE:QK, t * P:(t + 1) * P], bank("ckT", t)[0:ROPE, 2 * P:3 * P])
            empty(("ckT", t), ckT[:, :, t * P:(t + 1) * P], bank("ckT", t)[:, 0:2 * P].rearrange("p (k n) -> p k n", k=2))
        for t in range(NT):
            filled(a, "qsT", t)
            if t < NP_T:
                empty(("qsT", t), qsT[:, t, :, :], bank("qsT", t).rearrange("p (k n) -> p k n", k=GRP))
            else:
                empty(("qsT", t), qsT_s[:, :, :, :].rearrange("p b g q -> p g b q"),
                      bank("qsT", t).rearrange("p (g b q) -> p g b q", g=GRP, b=NB_DEC))
        filled(a, "ksT")
        empty(("ksT",), ksT[:, :], bank("ksT")[:, 0:NT * P])
        for k in range(2):
            for f in range(2):
                filled(a, "gate", k, f)
                empty(("gate", k, f), gates[:, k, f * 512:(f + 1) * 512], bank("gate", k, f))
        for t in range(NP_T):
            filled(a, "v", t)
            empty(("v", t), v_p[:, t, :], bank("v", t))
        for t in range(NT):
            for f in range(2):
                filled(a, "qT", t, f)
                if t < NP_T:
                    empty(("qT", t, f), qT[:, t, 4 * f:4 * f + 4, :],
                          bank("qT", t, f)[0:QK].rearrange("p (h n) -> p h n", h=4))
                else:
                    empty(("qT", t, f), qT_s[:, :, 4 * f:4 * f + 4, :].rearrange("p b h q -> p h b q"),
                          bank("qT", t, f)[0:QK].rearrange("p (h b q) -> p h b q", h=4, b=NB_DEC))
        for p in range(4):
            filled(a, "qabs", p)
            for hh in range(2):
                for ct in range(2):
                    o = (hh * 2 + ct) * P
                    empty(("qabs", p), qabs[:, ct, :, 2 * p + hh, :],
                          bank("qabs", p)[:, o:o + P].rearrange("p (b q) -> p b q", b=NB_DEC), last=(hh + ct == 2))
        for p in range(4):
            filled(a, "kT", p)
            empty(("kT", p), kT[0:NOPE, 2 * p:2 * p + 2, :], bank("kT", p)[0:NOPE].rearrange("p (h n) -> p h n", h=2),
                  last=False)
            for hh in range(2):
                empty(("kT", p), kT[NOPE:QK, 2 * p + hh, :], kpT[NOPE:QK, 0:SEQ], last=(hh == 1))

        a.wait_ge(S["loaded_tables"], 16 * N_TABLES)

        def a_exp(i):
            kind, n, hh = items[i]
            a.wait_ge(S["maxed"], i + 1)
            if i >= 2:
                a.wait_ge(S["flipped"], i - 1)
            scale = MLA_SCALE if kind.startswith("mla") else SWA_SCALE
            nk = width(i)
            ins = nc.scalar.activation(probs[:, i % 2, 0:nk], scores(i)[:, 0:nk], ACT.Exp, bias=neg_max[:, i:i + 1],
                                       scale=scale, accum_out=row_sum[:, i:i + 1])
            if kind.startswith("swa"):
                col = sinks[:, hh:hh + 1] if kind == "swa" else sinks[:, H:H + 1]
                ins = nc.scalar.activation(sink_e[:, i:i + 1], col, ACT.Exp, bias=neg_max[:, i:i + 1])
            ins.then_inc(S["exped"], 1)

        def a_flip(i):
            kind, n, hh = items[i]
            a.wait_ge(S["flipped"], i + 1)
            if i >= 2:
                a.wait_ge(S["pv_done"], i - 1)
            full = full_tiles(i)
            tb = ps[:, 4:6, :].rearrange("p a b -> p (a b)")
            last = nc.scalar.copy(pT[:, i % 2, 0:full * P], tb[:, 0:full * P])
            if kind.endswith("_s"):
                last = nc.scalar.copy(pT[0:Q_DEC, i % 2, full * P:(full + 1) * P], tb[0:Q_DEC, full * P:(full + 1) * P])
            last.then_inc(S["pT_ready"], 1)

        def a_out(i):
            kind, n, hh = items[i]
            a.wait_ge(S["pv_done"], i + 1)
            ob = ps[:, 6, :]
            if kind in ("mla", "swa"):
                r = slice(64 * (hh % 2), 64 * (hh % 2) + 64)
                last = nc.scalar.copy(mixT[r, (4 if kind == "swa" else 0) + hh // 2, n * P:(n + 1) * P], ob[r, 0:P])
            elif kind == "mla_s":
                last = nc.scalar.copy(qabs[:, :, n, :, :].rearrange("p a h q -> p a (h q)"),
                                      ob[:, 0:2 * P].rearrange("p (a n) -> p a n", a=2))
            else:
                c0 = SEQ + n * Q_DEC
                last = nc.scalar.copy(mixT[:, 4:8, c0:c0 + Q_DEC], ob[:, 0:4 * Q_DEC].rearrange("p (a q) -> p a q", a=4))
            last.then_inc(S["o_ready"], 1)

        a_exp(0)
        for i in range(len(items)):
            if i + 1 < len(items):
                a_exp(i + 1)
            a_flip(i)
            if i >= 1:
                a_out(i - 1)
        a_out(len(items) - 1)
        filled(a, "oS")
        empty(("oS",), mixT[:, 0:4, SEQ:SEQ + P], bank("oS").rearrange("p (k n) -> p k n", k=4))
        a.wait_ge(S["x1_ready"], 12)
        for k in range(2):
            for f in range(2):
                filled(a, "fgate", k, f)
                empty(("fgate", k, f), gates[:, k, f * 512:(f + 1) * 512], bank("fgate", k, f))
        x_stats(36)
        emptied(a, "fshift", 1, 1)
        for t in range(NT):
            nc.scalar.dma_start(h_rows[t * P:(t + 1) * P, :], h[:, t, :]).then_inc(S["h_stored"], 16)
        for t in range(NT):
            for g in range(2):
                filled(a, "fT", t, g)
                empty(("fT", t, g), hT[:, 4 * g:4 * g + 4, t * P:(t + 1) * P],
                      bank("fT", t, g).rearrange("p (k n) -> p k n", k=4))

        def round_unit(i, n):
            a.wait_ge(slot_sem[moe_slot(n)], moe_full(i, n))
            a.wait_ge(S["unit_used"], moe_used(i, n - SPLIT))
            nc.scalar.copy(piece(w_hi, n), piece_src(n)).then_inc(S["hi_ready"], 1)

        for n in range(SPLIT):
            round_unit(0, n)
        for t in range(NT):
            a.wait_ge(S["probs_top"], t + 1)
            nc.scalar.activation(gate_w[:, t, :], gate_w[:, t, :], ACT.Exp, bias=stat[:, 50 + t:51 + t],
                                 accum_out=stat[:, 53 + t:54 + t]).then_inc(S["gates_exped"], 1)

        a.wait_ge(S["gates_exped"], NT)
        a.wait_ge(S["table_ready"], 1)

        def turned(sem_in, count, hi, raw, r, bk, sem_out):
            a.wait_ge(S[sem_in], count)
            src = t_bank[bk].rearrange("p (k n) -> p k n", k=4)
            nc.scalar.copy(hi[:, 3 * r:3 * r + 3, :], src[:, 0:3])
            nc.scalar.copy(raw[:, r, :], src[:, 3]).then_inc(S[sem_out], 1)

        turned("xT_filled", 1, xT_hi, xT_raw, 0, 1, "xT_hi_ready")
        turned("xT_filled", 2, xT_hi, xT_raw, 1, 1, "xT_hi_ready")

        def swish(i, f):
            a.wait_ge(S["glu_ready"], i * 2 + f + 1)
            nc.scalar.activation(sig[:, f, :], glu[:, f, :], ACT.Sigmoid, scale=1.702).then_inc(S["sig_done"], 1)

        def expert_block(i):
            for n in (4, 5, 6, 7):
                round_unit(i, n)
            swish(i, 0)
            for n in (8, 9):
                round_unit(i, n)
            turned("actT_filled", i * 2 + 1, aT_hi, aT_raw, 0, 0, "aT_hi_ready")
            round_unit(i, 10)
            swish(i, 1)
            round_unit(i, 11)
            turned("xT_filled", i * 2 + 3, xT_hi, xT_raw, 0, 1, "xT_hi_ready")
            turned("actT_filled", i * 2 + 2, aT_hi, aT_raw, 1, 0, "aT_hi_ready")
            for n in (0, 1, 2):
                round_unit(i + 1, n)
            turned("xT_filled", i * 2 + 4, xT_hi, xT_raw, 1, 1, "xT_hi_ready")
            round_unit(i + 1, 3)
            a.wait_ge(S["unit_used"], moe_used(i, MOE_UNITS - 1))
            a.wait_ge(S["y_stored"], i * 16 + 16)
            nc.scalar.copy(y_blk[:, :], ps[:, 4:6, :].rearrange("p a b -> p (a b)")).then_inc(S["y_copied"], 1)
            a.wait_ge(S["y_copied"], i + 2)
            nc.scalar.dma_start(y_rows[bass.ds(i * P, P), :], y_blk[:, :]).then_inc(S["y_stored"], 16)

        a.sem_inc(S["y_copied"], 1)
        a.sem_inc(S["y_stored"], 16)
        with a.Fori(0, NE) as i:
            expert_block(i)
        n_ovf = a.value_load(ovf_table[0:1, NOVF:NOVF + 1], min_val=0, max_val=NOVF)
        with a.If(n_ovf > 0):
            with a.Fori(NE, n_ovf + NE) as i:
                expert_block(i)
        a.wait_ge(S["y_copied"], n_ovf + (NE + 1))
        nc.scalar.dma_start(gfin, g_final).then_inc(S["loaded_gfin"], 16)

        for t in range(NT):
            a.wait_ge(S["fin_ready"], 3 * t + 1)
            nc.scalar.activation(glu[:, :, :].rearrange("p a b -> p (a b)"), x[:, t, :], ACT.Square, scale=float(D) ** -0.5,
                                 accum_out=stat[:, 56 + t:57 + t]).then_inc(S["fin_ss"], 1)
            a.wait_ge(S["fin_ready"], 3 * t + 2)
            nc.scalar.activation(stat[:, 59 + t:60 + t], stat[:, 56 + t:57 + t], ACT.Sqrt).then_inc(S["fin_root"], 1)
            a.wait_ge(S["fin_ready"], 3 * t + 3)
            dst = o_yp[0, t * P:(t + 1) * P, :] if t < NP_T else o_ys.rearrange("b q d -> (b q) d")
            nc.scalar.dma_start(dst, x[:, t, :]).then_inc(S["fin_stored"], 16)
        a.wait_ge(S["fin_stored"], 16 * NT)

    @block.vector
    def _(v):
        steps = [0]

        def step(ins):
            steps[0] += 1
            ins.then_inc(S["v_step"], 1)
            v.wait_ge(S["v_step"], steps[0])

        csig = rtr[:, :, :].rearrange("p a b -> p (a b)")[:, 0:KT * 9]
        step(nc.vector.memset(mod_parts[:, :], 0.0))
        v.wait_ge(S["sig_ready"], 1)
        nc.vector.tensor_tensor(cs[:, :, :].rearrange("p k n -> p (k n)"), cT[:, :, :].rearrange("p k n -> p (k n)"),
                                csig, ALU.mult).then_inc(S["silu_ready"], 1)

        def rms_of_x(n0, ss, ms, root):
            v.wait_ge(S["ss_ready"], ss)
            nc.vector.tensor_scalar(stat[:, n0 + 6:n0 + 9], stat[:, n0:n0 + 3], 1.0 / D, EPS, ALU.mult, ALU.add).then_inc(
                S["ms_ready"], 1)
            v.wait_ge(S["root_ready"], root)
            step(nc.vector.reciprocal(stat[:, n0 + 9:n0 + 12], stat[:, n0 + 3:n0 + 6]))

        rms_of_x(0, NT, 1, 1)

        def mod_take(n, src, done):
            rows = early_rows[:, n] if n < EARLY_MOD else mod_rows
            v.wait_ge(S["loaded_rows"], 16 if n < EARLY_MOD else 16 * (n - EARLY_MOD + 2))
            nc.vector.tensor_tensor(mod_row[:, :], src[0:9], rows[:, 0, :], ALU.add).then_inc(S[done], 1)
            v.wait_ge(S[done], ordinal[("mod", n)] if n < EARLY_MOD else n - EARLY_MOD + 1)

        def mod_split(n):
            cols = slice(n * 512, (n + 1) * 512)
            rows = early_rows[:, n] if n < EARLY_MOD else mod_rows
            if n // 2 in (1, 4):
                step(nc.vector.scalar_tensor_tensor(mod_row[:, :], mod_row[:, :], 1.0, rows[:, 1, :], ALU.add, ALU.mult))
            step(nc.vector.tensor_copy(mod_parts[0:9, cols], mod_row[:, :]))
            step(nc.vector.tensor_tensor(mod_res[:, :], mod_row[:, :], mod_parts[0:9, cols], ALU.subtract))
            step(nc.vector.tensor_copy(mod_p2[:, :], mod_res[:, :]))
            step(nc.vector.tensor_tensor(mod_res[:, :], mod_res[:, :], mod_p2[:, :], ALU.subtract))
            step(nc.vector.tensor_copy(mod_parts[32:41, cols], mod_p2[:, :]))
            nc.vector.tensor_copy(mod_parts[64:73, cols], mod_res[:, :]).then_inc(S["parts_ready"], 1)
            v.wait_ge(S["parts_ready"], n + 1)

        for n in range(4):
            filled(v, "mod", n)
            mod_take(n, bank("mod", n), "v_emptied")
            mod_split(n)
        filled(v, "mod", 4)
        mod_take(4, bank("mod", 4), "v_emptied")

        def modulated(pre_, inv0):
            for k in range(2):
                tiles = (0, 1) if k == 0 else (2,)
                for f in range(2):
                    cols = slice(f * 512, (f + 1) * 512)
                    filled(v, pre_ + "scale", k, f)
                    for t in tiles:
                        last = nc.vector.scalar_tensor_tensor(h[:, t, cols], x[:, t, cols], stat[:, inv0 + t:inv0 + t + 1],
                                                              bank(pre_ + "scale", k, f), ALU.mult, ALU.mult)
                    last.then_inc(S["v_emptied"], 1)
                    v.wait_ge(S["v_emptied"], ordinal[(pre_ + "scale", k, f)])
                    filled(v, pre_ + "shift", k, f)
                    for t in tiles:
                        last = nc.vector.tensor_tensor(h[:, t, cols], h[:, t, cols], bank(pre_ + "shift", k, f), ALU.add)
                    last.then_inc(S["v_emptied"], 1)

        modulated("b", 9)
        mod_split(4)
        filled(v, "mod", 5)
        mod_take(5, bank("mod", 5), "v_emptied")
        mod_split(5)

        def rope_into(dst, x1, x2, cos, sin, tmp):
            nc.vector.tensor_tensor(tmp[0], x1, cos, ALU.mult)
            nc.vector.tensor_tensor(tmp[1], x2, sin, ALU.mult)
            nc.vector.tensor_tensor(tmp[2], x2, cos, ALU.mult)
            step(nc.vector.tensor_tensor(tmp[3], x1, sin, ALU.mult))
            nc.vector.tensor_tensor(dst[0], tmp[0], tmp[1], ALU.subtract)
            return nc.vector.tensor_tensor(dst[1], tmp[2], tmp[3], ALU.add)

        v.wait_ge(S["loaded_tables"], 16 * N_TABLES)
        step(nc.vector.tensor_scalar(sinks_s[:, :], sinks[:, :], 1.0 / SWA_SCALE, None, ALU.mult))
        v.wait_ge(S["u_stats"], 2 * NT)
        step(nc.vector.tensor_scalar(stat[:, 22:28], stat[:, 16:22], EPS, None, ALU.add))
        v.sem_inc(S["ms_ready"], 1)
        v.wait_ge(S["root_ready"], 2)
        step(nc.vector.reciprocal(stat[:, 34:36], stat[:, 28:30]))
        step(nc.vector.reciprocal(stat[:, 12:16], stat[:, 30:34]))
        q_inv = (stat[:, 34:35], stat[:, 35:36], stat[:, 12:13])
        for t in range(NT):
            last = nc.vector.scalar_tensor_tensor(u[:, t, 0:QL], u[:, t, 0:QL], q_inv[t], g_qkv[:, 0:QL], ALU.mult, ALU.mult)
        last.then_inc(S["ql_ready"], 1)
        for t in range(NT):
            nc.vector.scalar_tensor_tensor(u[:, t, O_KV:O_KPE], u[:, t, O_KV:O_KPE], stat[:, 13 + t:14 + t],
                                           g_qkv[:, QL:QL + KVL], ALU.mult, ALU.mult)
        half = ROPE // 2
        tmp = [rt[:, n, 0:NT * half].rearrange("p (t d) -> p t d", t=NT) for n in range(4)]
        rope_into((u[:, :, O_KPE:O_KPE + half], u[:, :, O_KPE + half:O_QS]), u[:, :, O_KPE:O_KPE + half],
                  u[:, :, O_KPE + half:O_QS], rope[:, :, 0:half], rope[:, :, half:ROPE], tmp).then_inc(S["ck_ready"], 1)
        nc.vector.tensor_copy(v_swa[:, :, :], u[:, :, O_VS:IN_W]).then_inc(S["v_swa_ready"], 1)

        for t in range(NT):
            for f in range(2):
                filled(v, "q", t, f)
                if t:
                    filled(v, "qT", t - 1, f)
                src = bank("q", t, f)[:, 0:4 * QK].rearrange("p (h d) -> p h d", h=4)
                hs = slice(4 * f, 4 * f + 4)
                cos = rope[:, t:t + 1, 0:half].to_broadcast([P, 4, half])
                sin = rope[:, t:t + 1, half:ROPE].to_broadcast([P, 4, half])
                nc.vector.tensor_copy(q_tok[:, hs, 0:NOPE], src[:, :, 0:NOPE])
                tmp = [rt[:, n, 0:4 * half].rearrange("p (t d) -> p t d", t=4) for n in range(4)]
                rope_into((q_tok[:, hs, NOPE:NOPE + half], q_tok[:, hs, NOPE + half:QK]),
                          src[:, :, NOPE:NOPE + half], src[:, :, NOPE + half:QK], cos, sin, tmp).then_inc(S["v_emptied"], 1)
                emptied(v, "q", t, f)

        mod_next = [EARLY_MOD]

        def v_max(i):
            kind, n, hh = items[i]
            s, nk = scores(i), width(i)
            v.wait_ge(S["scored"], i + 1)
            if kind == "mla":
                step(nc.vector.tensor_tensor(s[:, 0:nk], s[:, 0:nk], causal[:, n, 0:nk], ALU.add))
            elif kind == "swa":
                slope = 2.0 ** (-8.0 * (hh + 1) / H)
                step(nc.vector.scalar_tensor_tensor(s[:, 0:nk], dist[:, n, 0:nk], -slope / SWA_SCALE, s[:, 0:nk],
                                                    ALU.mult, ALU.add))
            elif kind == "swa_s":
                step(nc.vector.tensor_tensor(s[:, 0:nk], s[:, 0:nk], alibi[:, 0:nk], ALU.add))
            step(nc.vector.tensor_reduce(row_max[:, i:i + 1], s[:, 0:nk], AX, ALU.max))
            if kind.startswith("swa"):
                col = sinks_s[:, hh:hh + 1] if kind == "swa" else sinks_s[:, H:H + 1]
                nc.vector.tensor_scalar(neg_max[:, i:i + 1], row_max[:, i:i + 1], col, -SWA_SCALE, ALU.max,
                                        ALU.mult).then_inc(S["maxed"], 1)
            else:
                nc.vector.tensor_scalar(neg_max[:, i:i + 1], row_max[:, i:i + 1], -MLA_SCALE, None, ALU.mult).then_inc(
                    S["maxed"], 1)

        def v_norm(i):
            kind, n, hh = items[i]
            v.wait_ge(S["exped"], i + 1)
            if kind.startswith("swa"):
                step(nc.vector.tensor_tensor(row_sum[:, i:i + 1], row_sum[:, i:i + 1], sink_e[:, i:i + 1], ALU.add))
            step(nc.vector.reciprocal(row_inv[:, i:i + 1], row_sum[:, i:i + 1]))
            nk = width(i)
            nc.vector.tensor_scalar(probs[:, i % 2, 0:nk], probs[:, i % 2, 0:nk], row_inv[:, i:i + 1], None,
                                    ALU.mult).then_inc(S["normed"], 1)

        v_max(0)
        for i in range(len(items)):
            if i + 1 < len(items):
                v_max(i + 1)
            v_norm(i)
            if i % 6 == 5 and i // 6 < N_MOD - EARLY_MOD:
                v.wait_ge(S["mod_extra"], i // 6 + 1)
                mod_take(EARLY_MOD + i // 6, ps[:, 7, :], "mod_extra_used")
                mod_split(EARLY_MOD + i // 6)

        for j in range(4):
            cols = slice(j * OUT_COLS, (j + 1) * OUT_COLS)
            for t in range(NT):
                filled(v, "o", j, t)
                emptied(v, "gate", 1, 1)
                if j:
                    v.wait_ge(S["x1_ready"], NT * (j - 1) + t + 1)
                tmp = hq[:, (t % 3) * OUT_COLS:(t % 3 + 1) * OUT_COLS]
                nc.vector.tensor_tensor(tmp, bank("o", j, t)[:, 0:OUT_COLS], gates[:, t // 2, cols], ALU.mult).then_inc(
                    S["v_emptied"], 1)
                v.wait_ge(S["v_emptied"], ordinal[("o", j, t)])
                nc.vector.tensor_tensor(x[:, t, cols], x[:, t, cols], tmp, ALU.add).then_inc(S["x1_ready"], 1)
        rms_of_x(36, 2 * NT, 3, 3)
        modulated("f", 45)

        def remainder(i, n):
            v.wait_ge(S["hi_ready"], i * MOE_UNITS + (n + 1))
            nc.vector.tensor_tensor(piece(w_lo, n), piece_src(n), piece(w_hi, n).bitcast(F32), ALU.subtract).then_inc(
                S["lo_ready"], 1)

        v.sem_inc(S["lo_ready"], SLOTS)

        v.wait_ge(S["v_emptied"], ordinal[("fshift", 1, 1)])
        top = rtr[:, 0, :]
        idx_u = rtr[:, 1, 0:24].bitcast(U32)
        idx_f = rtr[:, 2, 0:12]
        logit = rtr[:, 4:7, :]
        for t in range(NT):
            filled(v, "logit", t)
            nc.vector.tensor_tensor(logit[:, t, :], bank("logit", t)[:, 0:NE], b_rt[:, :], ALU.add).then_inc(S["v_emptied"], 1)
            v.wait_ge(S["v_emptied"], ordinal[("logit", t)])
            step(nc.vector.max(top[:, 8 * t:8 * t + 8], logit[:, t, :]))
            nc.vector.max_index(idx_u[:, 8 * t:8 * t + 8], top[:, 8 * t:8 * t + 8], logit[:, t, :])
            nc.vector.tensor_scalar(stat[:, 50 + t:51 + t], top[:, 8 * t:8 * t + 1], -1.0, None, ALU.mult)
            nc.vector.tensor_copy(gate_w[:, t, :], top[:, 8 * t:8 * t + TOPK]).then_inc(S["probs_top"], 1)
        v.wait_ge(S["probs_top"], NT)
        step(nc.vector.tensor_copy(idx_f.rearrange("p (t k) -> p t k", t=NT),
                                   idx_u.rearrange("p (t k) -> p t k", t=NT)[:, :, 0:TOPK]))
        hot = hq[:, 0:NT * TOPK * NE].rearrange("p (n e) -> p n e", e=NE)
        prod = hq[:, 512:512 + NT * TOPK * NE].rearrange("p (n e) -> p n e", e=NE)
        fld = [hq[:, 1024 + 128 * n:1024 + 128 * n + NT * NE].rearrange("p (t e) -> p t e", t=NT) for n in range(7)]
        chosen = hq[:, 2048:2048 + NT * NE // 2].bitcast(BF16).rearrange("p (t e) -> p t e", t=NT)
        emptied(v, "fT", NT - 1, 1)
        v.wait_ge(S["h_stored"], 16 * NT)
        step(nc.vector.tensor_tensor(hot, expert_id[:, :].unsqueeze(1).to_broadcast([P, NT * TOPK, NE]),
                                     idx_f.unsqueeze(2).to_broadcast([P, NT * TOPK, NE]), ALU.is_equal))
        step(nc.vector.tensor_reduce(fld[0], hot.rearrange("p (t k) e -> p t e k", t=NT), AX, ALU.add))
        nc.vector.tensor_copy(chosen, fld[0]).then_inc(S["logits_exp"], 1)
        rank, big1, big2, blk, pos, f1, f2 = fld
        for t in range(NT):
            filled(v, "rank", t)
            nc.vector.tensor_copy(rank[:, t, :], bank("rank", t)[:, 0:NE]).then_inc(S["v_emptied"], 1)
        filled(v, "count")
        cnt = rtr[:, 7, :]
        nc.vector.tensor_copy(cnt, bank("count")[:, 0:NE]).then_inc(S["v_emptied"], 1)
        v.wait_ge(S["v_emptied"], ordinal[("count",)])
        cum, alt = rtr[:, 8, :], rtr[:, 9, :]
        step(nc.vector.tensor_scalar(alt, cnt, 2.0 * P, None, ALU.is_gt))
        step(nc.vector.scalar_tensor_tensor(cum, cnt, 1.0 * P, alt, ALU.is_gt, ALU.add))
        n_own = rtr[:, 10, :]
        step(nc.vector.tensor_copy(n_own, cum))
        d = 1
        while d < NE:
            nc.vector.tensor_copy(alt[:, 0:d], cum[:, 0:d])
            step(nc.vector.tensor_tensor(alt[:, d:NE], cum[:, d:NE], cum[:, 0:NE - d], ALU.add))
            cum, alt, d = alt, cum, 2 * d
        ovf = prod.rearrange("p n e -> p (n e)")[:, 0:NOVF * NE].rearrange("p (n e) -> p n e", e=NE)
        step(nc.vector.tensor_tensor(ovf, cum.unsqueeze(1).to_broadcast([P, NOVF, NE]), block_id[:, :, :], ALU.is_le))
        nc.vector.memset(block_expert[:, NBLK - 1:NBLK], 0.0)
        nc.vector.tensor_copy(block_expert[:, 0:NE], expert_id[:, :])
        step(nc.vector.tensor_reduce(block_expert[:, NE:NE + NOVF], ovf, AX, ALU.add))
        nc.vector.tensor_copy(ovf_table[0:1, 0:NOVF], block_expert[0:1, NE:NE + NOVF])
        nc.vector.tensor_copy(ovf_table[0:1, NOVF:NOVF + 1], cum[0:1, NE - 1:NE]).then_inc(S["table_ready"], 1)
        first = alt
        step(nc.vector.tensor_tensor(first, cum, n_own, ALU.subtract))
        step(nc.vector.tensor_scalar(first, first, float(NE), None, ALU.add))
        step(nc.vector.tensor_tensor(first, first, expert_id[:, :], ALU.subtract))
        first3 = first.unsqueeze(1).to_broadcast([P, NT, NE])
        eid3 = expert_id[:, :].unsqueeze(1).to_broadcast([P, NT, NE])
        nc.vector.tensor_scalar(big1, rank, float(P), None, ALU.is_ge)
        step(nc.vector.tensor_scalar(big2, rank, 2.0 * P, None, ALU.is_ge))
        step(nc.vector.tensor_tensor(blk, big1, first3, ALU.mult))
        step(nc.vector.tensor_tensor(blk, blk, eid3, ALU.add))
        step(nc.vector.tensor_tensor(blk, blk, big2, ALU.add))
        step(nc.vector.tensor_tensor(big1, big1, big2, ALU.add))
        step(nc.vector.scalar_tensor_tensor(pos, big1, -float(P), rank, ALU.mult, ALU.add))
        blk_of, pos_of = rtr[:, 11, 0:NT * TOPK], rtr[:, 11, NT * TOPK:2 * NT * TOPK]
        for fsrc, dst in ((pos, pos_of), (blk, blk_of)):
            for t in range(NT):
                last = nc.vector.tensor_tensor(prod[:, t * TOPK:(t + 1) * TOPK, :], hot[:, t * TOPK:(t + 1) * TOPK, :],
                                               fsrc[:, t:t + 1, :].to_broadcast([P, TOPK, NE]), ALU.mult)
            step(last)
            step(nc.vector.tensor_reduce(dst, prod, AX, ALU.add))
        place, where = place_where()
        nc.vector.tensor_tensor(place, slot_id[:, :].unsqueeze(1).to_broadcast([P, NT * TOPK, P]),
                                pos_of.unsqueeze(2).to_broadcast([P, NT * TOPK, P]), ALU.is_equal)
        step(nc.vector.tensor_tensor(where, slot_id[:, 0:NBLK].unsqueeze(1).to_broadcast([P, NT * TOPK, NBLK]),
                                     blk_of.unsqueeze(2).to_broadcast([P, NT * TOPK, NBLK]), ALU.is_equal))
        for t in range(NT):
            ks = slice(t * TOPK, (t + 1) * TOPK)
            last = nc.vector.tensor_scalar(where[:, ks, :], where[:, ks, :], token_id[:, t:t + 1], None, ALU.mult)
        last.then_inc(S["placed"], 1)
        step(nc.vector.scalar_tensor_tensor(pos_of, blk_of, float(P), pos_of, ALU.mult, ALU.add))
        step(nc.vector.tensor_copy(y_row_idx[:, :], pos_of))
        filled(v, "table")
        nc.vector.tensor_copy(slot_tok[:, :], bank("table")[:, 0:NBLK]).then_inc(S["v_emptied"], 1)

        for n in range(SPLIT):
            remainder(0, n)
        v.wait_ge(S["gates_exped"], NT)
        step(nc.vector.reciprocal(stat[:, 50:53], stat[:, 53:56]))
        for t in range(NT):
            last = nc.vector.tensor_scalar(gate_w[:, t, :], gate_w[:, t, :], stat[:, 50 + t:51 + t], None, ALU.mult)
        step(last)
        nc.vector.tensor_scalar(sel_e[:, :], row_expert[:, :], block_expert[0:96, 0:1], None, ALU.is_equal).then_inc(
            S["sel_ready"], 1)

        def turned(v_hi, src_hi, dst, r, bk, sem_in, sem_out):
            v.wait_ge(S[sem_in], v_hi)
            nc.vector.tensor_tensor(dst[:, 3 * r:3 * r + 3, :], t_bank[bk].rearrange("p (k n) -> p k n", k=4)[:, 0:3],
                                    src_hi[:, 3 * r:3 * r + 3, :].bitcast(F32), ALU.subtract).then_inc(S[sem_out], 1)

        turned(1, xT_hi, xT_lo, 0, 1, "xT_hi_ready", "xT_ready")
        turned(2, xT_hi, xT_lo, 1, 1, "xT_hi_ready", "xT_ready")

        def clamp(i, f):
            v.wait_ge(S["unit_used"], moe_used(i, 4 * f + 3))
            if f == 0:
                v.wait_ge(S["act_ready"], i * 2 + 2)
            nc.vector.tensor_scalar(glu[:, f, :], ps[:, 2 * f, :], 7.0, None, ALU.min).then_inc(S["glu_ready"], 1)
            nc.vector.tensor_scalar(lin[:, f, :], ps[:, 2 * f + 1, :], -7.0, 7.0, ALU.max, ALU.min).then_inc(
                S["gu_emptied"], 1)

        def swiglu(i, f):
            v.wait_ge(S["sig_done"], i * 2 + f + 1)
            nc.vector.tensor_tensor(sig[:, f, :], glu[:, f, :], sig[:, f, :], ALU.mult).then_inc(S["gsg_ready"], 1)
            v.wait_ge(S["gu_emptied"], i * 2 + f + 3)
            v.wait_ge(S["gsg_ready"], i * 2 + f + 1)
            nc.vector.scalar_tensor_tensor(lin[:, f, :], lin[:, f, :], 1.0, sig[:, f, :], ALU.add, ALU.mult).then_inc(
                S["act_ready"], 1)

        def expert_block(i):
            for n in (4, 5, 6):
                remainder(i, n)
            clamp(i, 0)
            remainder(i, 7)
            swiglu(i, 0)
            for n in (8, 9):
                remainder(i, n)
            turned(i * 2 + 1, aT_hi, aT_lo, 0, 0, "aT_hi_ready", "actT_ready")
            remainder(i, 10)
            clamp(i, 1)
            swiglu(i, 1)
            remainder(i, 11)
            v.wait_ge(S["bias_done"], i + 1)
            v.wait_ge(S["sel_ready"], i + 1)
            nc.vector.tensor_scalar(sel_e[:, :], row_expert[:, :], block_expert[0:96, bass.ds(i + 1, 1)], None,
                                    ALU.is_equal).then_inc(S["sel_ready"], 1)
            turned(i * 2 + 3, xT_hi, xT_lo, 0, 1, "xT_hi_ready", "xT_ready")
            turned(i * 2 + 2, aT_hi, aT_lo, 1, 0, "aT_hi_ready", "actT_ready")
            for n in (0, 1, 2):
                remainder(i + 1, n)
            turned(i * 2 + 4, xT_hi, xT_lo, 1, 1, "xT_hi_ready", "xT_ready")
            remainder(i + 1, 3)

        v.sem_inc(S["gu_emptied"], 2)
        v.sem_inc(S["act_ready"], 2)
        with v.Fori(0, NE) as i:
            expert_block(i)
        n_ovf = v.value_load(ovf_table[0:1, NOVF:NOVF + 1], min_val=0, max_val=NOVF)
        with v.If(n_ovf > 0):
            with v.Fori(NE, n_ovf + NE) as i:
                expert_block(i)

        v.wait_ge(S["loaded_gfin"], 16)
        for t in range(NT):
            for k in range(TOPK):
                v.wait_ge(S[f"got{k}"], 16 * (t + 1))
                w = gate_w[:, t, k:k + 1]
                if k == 0:
                    ins = nc.vector.tensor_scalar(y_acc[:, :], y_got[:, k, :], w, None, ALU.mult)
                else:
                    ins = nc.vector.scalar_tensor_tensor(y_acc[:, :], y_got[:, k, :], w, y_acc[:, :], ALU.mult, ALU.add)
                ins.then_inc(S["acc_done"], 1)
                v.wait_ge(S["acc_done"], t * TOPK + k + 1)
            step(nc.vector.tensor_tensor(y_acc[:, :], y_acc[:, :], gates[:, t // 2, :], ALU.mult))
            nc.vector.tensor_tensor(x[:, t, :], x[:, t, :], y_acc[:, :], ALU.add).then_inc(S["fin_ready"], 1)
            v.wait_ge(S["fin_ss"], t + 1)
            nc.vector.tensor_scalar(stat[:, 56 + t:57 + t], stat[:, 56 + t:57 + t], EPS, None, ALU.add).then_inc(
                S["fin_ready"], 1)
            v.wait_ge(S["fin_root"], t + 1)
            step(nc.vector.reciprocal(stat[:, 48:49], stat[:, 59 + t:60 + t]))
            nc.vector.scalar_tensor_tensor(x[:, t, :], x[:, t, :], stat[:, 48:49], gfin[:, :], ALU.mult, ALU.mult).then_inc(
                S["fin_ready"], 1)

    @block.tensor
    def _(pe):
        def open_job(*key):
            n = number[key]
            first = 0 if n < len(early) else len(early)
            if n - 8 >= first:
                emptied(pe, *jobs[n - 8][0])
            return bank(*key)

        def close(ins):
            ins.then_inc(S["psum_filled"], 1)

        def mod_products(n, out, done):
            for f in range(2):
                unit_here(pe, ("ada", n, f))
                w = unit(("ada", n, f)).rearrange("p (k n) -> p k n", k=4)
                for k in range(4):
                    kt = 4 * f + k
                    ins = nc.tensor.matmul(out[0:9], cs[:, kt, :], w[:, k, :], start=(kt == 0), stop=(kt == KT - 1))
                ins.then_inc(S["unit_used"] if f == 0 else S[done], 1)

        def spread(key, chunk, k):
            out = open_job(*key)
            close(nc.tensor.matmul(out, kind_sel[:, k, :], mod_parts[:, chunk * 512:(chunk + 1) * 512], start=True, stop=True))

        def turn(out, src, n_rows=P):
            return nc.tensor.transpose(out, src, ident[0:n_rows, 0:n_rows])

        pe.wait_ge(S["silu_ready"], 1)
        for n in range(5):
            mod_products(n, open_job("mod", n), "psum_filled")
        pe.wait_ge(S["parts_ready"], 4)
        pe.wait_ge(S["consts_cast"], 2)
        for k in range(2):
            for f in range(2):
                spread(("bscale", k, f), 2 + f, k)
                spread(("bshift", k, f), f, k)
        mod_products(5, open_job("mod", 5), "psum_filled")
        pe.wait_ge(S["loaded_small"], 16 * 3)
        for t in range(NT):
            for g in range(2):
                emptied(pe, "bshift", t // 2, g)
                out = open_job("hT", t, g)
                for k in range(4):
                    kt = 4 * g + k
                    ins = turn(out[:, k * P:(k + 1) * P], h[:, t, kt * P:(kt + 1) * P])
                close(ins)
        emptied(pe, "hT", NT - 1, 1)
        for j in range(6):
            unit_here(pe, ("in", j))
            w = unit(("in", j))[:, 0:KT * IN_COLS].rearrange("p (k n) -> p k n", k=KT)
            for t in range(NT):
                out = open_job("u", j, t)
                for kt in range(KT):
                    ins = nc.tensor.matmul(out[:, 0:IN_COLS], hT[:, kt, t * P:(t + 1) * P], w[:, kt, :],
                                           start=(kt == 0), stop=(kt == KT - 1))
                close(ins)
        pe.wait_ge(S["ql_ready"], 1)
        for t in range(NT):
            out = open_job("qlT", t)
            for k in range(3):
                ins = turn(out[:, k * P:(k + 1) * P], u[:, t, k * P:(k + 1) * P])
            close(ins)
        pe.wait_ge(S["ck_ready"], 1)
        for t in range(NT):
            out = open_job("ckT", t)
            for k in range(2):
                turn(out[:, k * P:(k + 1) * P], u[:, t, O_KV + k * P:O_KV + (k + 1) * P])
            close(turn(out[0:ROPE, 2 * P:3 * P], u[:, t, O_KPE:O_QS]))
        for t in range(NT):
            out = open_job("qsT", t)
            qs = u[:, t, O_QS:O_KS].rearrange("p (g n) -> p g n", g=GRP)
            for g in range(GRP):
                ins = turn(out[:, g * P:(g + 1) * P], qs[:, g])
            close(ins)
        out = open_job("ksT")
        for t in range(NT):
            ins = turn(out[:, t * P:(t + 1) * P], u[:, t, O_KS:O_VS])
        close(ins)
        pe.wait_ge(S["parts_ready"], EARLY_MOD)
        for k in range(2):
            for f in range(2):
                spread(("gate", k, f), 4 + f, k)
        emptied(pe, "ckT", NT - 1)
        pe.wait_ge(S["loaded_tables"], 16 * N_TABLES)
        for t in range(NP_T):
            out = open_job("v", t)
            for ct in range(2):
                ins = nc.tensor.matmul(out, ckT[:, ct, t * P:(t + 1) * P], w_ukv[:, ct, :, NOPE:NOPE + VD],
                                       start=(ct == 0), stop=(ct == 1))
            close(ins)
        pe.wait_ge(S["loaded_uq"], 16)
        emptied(pe, "qlT", NT - 1)

        def q_products(t, f):
            out = open_job("q", t, f)
            for k in range(3):
                ins = nc.tensor.matmul(out[:, 0:4 * QK], qlT[:, k, t * P:(t + 1) * P], w_uq[:, k, f * 4 * QK:(f + 1) * 4 * QK],
                                       start=(k == 0), stop=(k == 2))
            close(ins)

        def q_turn(t, f):
            emptied(pe, "q", t, f)
            out = open_job("qT", t, f)
            for hh in range(4):
                ins = turn(out[0:QK, hh * P:(hh + 1) * P], q_tok[:, 4 * f + hh, :])
            close(ins)

        for w, t in QUERY_ORDER:
            for f in range(2):
                (q_products if w == "q" else q_turn)(t, f)
        emptied(pe, "qT", NT - 1, 1)

        for p in range(4):
            out = open_job("qabs", p)
            for hh in range(2):
                for ct in range(2):
                    ins = nc.tensor.matmul(out[:, (hh * 2 + ct) * P:(hh * 2 + ct + 1) * P],
                                           wukT[:, 2 * p + hh, ct * P:(ct + 1) * P], qT_s[0:NOPE, :, 2 * p + hh, :],
                                           start=True, stop=True)
            close(ins)
        for p in range(4):
            out = open_job("kT", p)
            for hh in range(2):
                for ct in range(2):
                    ins = nc.tensor.matmul(out[0:NOPE, hh * SEQ:(hh + 1) * SEQ], w_ukv[:, ct, 2 * p + hh, 0:NOPE],
                                           ckT[:, ct, 0:SEQ], start=(ct == 0), stop=(ct == 1))
            close(ins)

        pe.wait_ge(S["v_emptied"], n_early["v"])
        pe.wait_ge(S["a_emptied"], n_early["a"])

        def score(i):
            kind, n, hh = items[i]
            s = scores(i)
            if i >= 3:
                pe.wait_ge(S["exped"], i - 2)
            if kind == "mla":
                ins = nc.tensor.matmul(s[:, 0:width(i)], qT[:, n, hh, :], kT[:, hh, 0:width(i)], start=True, stop=True)
            elif kind == "swa":
                r = slice(64 * (hh // GRP), 64 * (hh // GRP) + 64)
                ins = nc.tensor.matmul(s[:, 0:width(i)], qsT[r, n, hh % GRP, :], ksT[r, 0:width(i)], start=True, stop=True)
            elif kind == "mla_s":
                k = n % 2
                pe.wait_ge(cache_sem[k], 16 * 7 * (n // 2 + 1))
                own = slice(SEQ + n * Q_DEC, SEQ + (n + 1) * Q_DEC)
                for c0, n_c, keys in ((0, PAST, [latT[:, k, 0, :], latT[:, k, 1, :], krT[NOPE:QK, k, :]]),
                                      (PAST, Q_DEC, [ckT[:, 0, own], ckT[:, 1, own], kpT[NOPE:QK, own]])):
                    for ct in range(2):
                        nc.tensor.matmul(s[:, c0:c0 + n_c], qabs[:, ct, n, :, :].rearrange("p h q -> p (h q)"), keys[ct],
                                         start=(ct == 0), stop=False)
                    ins = nc.tensor.matmul(s[:, c0:c0 + n_c], qT_s[NOPE:QK, n].rearrange("p h q -> p (h q)"), keys[2], start=False, stop=True)
            else:
                k = n % 2
                own = slice(SEQ + n * Q_DEC, SEQ + (n + 1) * Q_DEC)
                for kv in range(KVH):
                    r = slice(64 * kv, 64 * kv + 64)
                    q = qsT_s[r, n].rearrange("p g q -> p (g q)")
                    nc.tensor.matmul(s[r, 0:WINDOW], q, ck_sT[r, k, :], start=True, stop=True)
                    ins = nc.tensor.matmul(s[r, WINDOW:WINDOW + Q_DEC], q, ksT[r, own], start=True, stop=True)
            ins.then_inc(S["scored"], 1)

        def flip(i):
            kind, n, hh = items[i]
            pe.wait_ge(S["normed"], i + 1)
            if i >= 1:
                pe.wait_ge(S["pT_ready"], i)
            tb = ps[:, 4:6, :].rearrange("p a b -> p (a b)")
            full = full_tiles(i)
            for k in range(full):
                ins = turn(tb[:, k * P:(k + 1) * P], probs[:, i % 2, k * P:(k + 1) * P])
            if kind.endswith("_s"):
                ins = turn(tb[0:Q_DEC, full * P:(full + 1) * P], probs[:, i % 2, full * P:full * P + Q_DEC])
            ins.then_inc(S["flipped"], 1)

        def weigh(i):
            kind, n, hh = items[i]
            pe.wait_ge(S["pT_ready"], i + 1)
            if i >= 1:
                pe.wait_ge(S["o_ready"], i)
            ob, full, pt = ps[:, 6, :], full_tiles(i), pT[:, i % 2, :]
            if kind in ("mla", "swa"):
                r = slice(64 * (hh % 2), 64 * (hh % 2) + 64)
                for k in range(full):
                    vals = v_p[:, k, hh * VD:(hh + 1) * VD] if kind == "mla" else \
                        v_swa[:, k, (hh // GRP) * HD:(hh // GRP + 1) * HD]
                    ins = nc.tensor.matmul(ob[r, 0:P], vals, pt[:, k * P:(k + 1) * P], start=(k == 0), stop=(k == full - 1))
            elif kind == "mla_s":
                for ct in range(2):
                    c = slice(ct * P, (ct + 1) * P)
                    for k in range(full):
                        nc.tensor.matmul(ob[:, c], lat[:, n % 2, k, c], pt[:, k * P:(k + 1) * P], start=(k == 0), stop=False)
                    ins = nc.tensor.matmul(ob[:, c], new_lat[:, n % 2, c], pt[0:Q_DEC, full * P:(full + 1) * P],
                                           start=False, stop=True)
            else:
                for kv in range(KVH):
                    for par in range(2):
                        o = ob[64 * par:64 * par + 64, kv * 2 * Q_DEC:(kv + 1) * 2 * Q_DEC]
                        vals = slice(kv * HD, (kv + 1) * HD)
                        for k, rows in ((0, P), (1, Q_DEC)):
                            cols = pt[0:rows, k * P:(k + 1) * P].rearrange("p (k g a q) -> p k g a q", k=KVH, g=2, a=2)
                            src = cv_s[:, n % 2, vals] if k == 0 else new_v[:, n % 2, vals]
                            ins = nc.tensor.matmul(o, src, cols[:, kv, :, par, :], start=(k == 0), stop=(k == 1))
            ins.then_inc(S["pv_done"], 1)

        score(0)
        score(1)
        for i in range(len(items)):
            if i + 2 < len(items):
                score(i + 2)
            flip(i)
            if i % 6 == 4 and i // 6 < N_MOD - EARLY_MOD:
                if i // 6:
                    pe.wait_ge(S["mod_extra_used"], i // 6)
                mod_products(EARLY_MOD + i // 6, ps[:, 7, :], "mod_extra")
            if i >= 1:
                weigh(i - 1)
        weigh(len(items) - 1)

        pe.wait_ge(S["o_ready"], len(items))
        pe.wait_ge(S["mod_extra_used"], N_MOD - EARLY_MOD)
        out = open_job("oS")
        for hh in range(H):
            r = slice(64 * (hh % 2), 64 * (hh % 2) + 64)
            for ct in range(2):
                ins = nc.tensor.matmul(out[r, (hh // 2) * P:(hh // 2 + 1) * P], w_ukv[:, ct, hh, NOPE:NOPE + VD],
                                       qabs[:, ct, :, hh, :], start=(ct == 0), stop=(ct == 1))
        close(ins)
        emptied(pe, "oS")
        for j in range(4):
            unit_here(pe, ("out", j))
            w = unit(("out", j)).rearrange("p (k n) -> p k n", k=KT)
            for t in range(NT):
                out = open_job("o", j, t)
                for kt in range(KT):
                    ins = nc.tensor.matmul(out[:, 0:OUT_COLS], mixT[:, kt, t * P:(t + 1) * P], w[:, kt, :],
                                           start=(kt == 0), stop=(kt == KT - 1))
                close(ins)
        pe.wait_ge(S["parts_ready"], N_MOD)
        for k in range(2):
            for f in range(2):
                spread(("fgate", k, f), 10 + f, k)
        for k in range(2):
            for f in range(2):
                spread(("fscale", k, f), 8 + f, k)
                spread(("fshift", k, f), 6 + f, k)
        for t in range(NT):
            for g in range(2):
                emptied(pe, "fshift", t // 2, g)
                out = open_job("fT", t, g)
                for k in range(4):
                    kt = 4 * g + k
                    ins = turn(out[:, k * P:(k + 1) * P], h[:, t, kt * P:(kt + 1) * P])
                close(ins)
        for t in range(NT):
            emptied(pe, "fT", t, 1)
            out = open_job("logit", t)
            for kt in range(KT):
                ins = nc.tensor.matmul(out[:, 0:NE], hT[:, kt, t * P:(t + 1) * P], w_rt[:, kt, :],
                                       start=(kt == 0), stop=(kt == KT - 1))
            close(ins)
        chosen = hq[:, 2048:2048 + NT * NE // 2].bitcast(BF16).rearrange("p (t e) -> p t e", t=NT)
        pe.wait_ge(S["logits_exp"], 1)
        for t in range(NT):
            out = open_job("rank", t)
            for s in range(t + 1):
                ins = nc.tensor.matmul(out[:, 0:NE], before[:, 1 if s < t else 0, :], chosen[:, s, :], start=(s == 0),
                                       stop=(s == t))
            close(ins)
        out = open_job("count")
        for s in range(NT):
            ins = nc.tensor.matmul(out[:, 0:NE], before[:, 1, :], chosen[:, s, :], start=(s == 0), stop=(s == NT - 1))
        close(ins)
        pe.wait_ge(S["placed"], 1)
        place, where = place_where()
        out = open_job("table")
        for n in range(NT * TOPK):
            ins = nc.tensor.matmul(out[:, 0:NBLK], place[:, n, :], where[:, n, :], start=(n == 0), stop=(n == NT * TOPK - 1))
        close(ins)

        pe.wait_ge(S["v_emptied"], n_all["v"])
        pe.wait_ge(S["a_emptied"], n_all["a"])
        pe.wait_ge(S["bias_ready"], 1)
        def turn_x(r, bk):
            for k in range(4):
                kt = 4 * r + k
                ins = turn(t_bank[bk][:, k * P:(k + 1) * P], x_slots[:, kt * P:(kt + 1) * P])
            ins.then_inc(S["xT_filled"], 1)

        pe.wait_ge(S["gathered"], 16)
        turn_x(0, 1)
        pe.wait_ge(S["xT_ready"], 1)
        turn_x(1, 1)

        def products(i, n, banks, hi, lo, raw, last):
            pe.wait_ge(S["lo_ready"], i * MOE_UNITS + (SLOTS + n + 1))
            for k in range(2):
                if k < PIECE_N[n % 4]:
                    own, w = PIECE_AT[n % 4] + k, PIECE_AT[n % 4] + k
                    passes = ((hi[:, own, :], w_hi[:, w, :]), (hi[:, own, :], w_lo[:, w, :]), (lo[:, own, :], w_hi[:, w, :]))
                else:
                    passes = ((raw[:, n % 4 // 2, :], ring[:, moe_slot(n), UNIT // 2:UNIT]), )
                for q, (x_part, w_part) in enumerate(passes):
                    for s in range(2):
                        ins = nc.tensor.matmul(banks[s], x_part, w_part[:, s * 512:(s + 1) * 512], start=False,
                                               stop=(last and k == 1 and q == len(passes) - 1))
            ins.then_inc(S["unit_used"], 1)

        def expert_block(i):
            def turn_act(f):
                pe.wait_ge(S["act_ready"], i * 2 + f + 3)
                for k in range(4):
                    ins = turn(t_bank[0][:, k * P:(k + 1) * P], lin[:, f, k * P:(k + 1) * P])
                ins.then_inc(S["actT_filled"], 1)

            pe.wait_ge(S["sel_ready"], i + 1)
            for f in range(2):
                pe.wait_ge(S["gu_emptied"], i * 2 + f + 1)
                banks = [ps[:, 2 * f + s, :] for s in range(2)]
                for s in range(2):
                    nc.tensor.matmul(banks[s], sel_e[:, :], bias_parts[:, s * D + f * 512:s * D + (f + 1) * 512],
                                     start=True, stop=False)
                for j in range(4):
                    if f == 0 and j % 2 == 0:
                        pe.wait_ge(S["xT_ready"], i * 2 + j // 2 + 1)
                    products(i, 4 * f + j, banks, xT_hi, xT_lo, xT_raw, j == 3)
                    if (f, j) == (1, 1):
                        turn_act(0)

            banks = [ps[:, 4 + s, :] for s in range(2)]
            pe.wait_ge(S["y_copied"], i + 1)
            for s in range(2):
                ins = nc.tensor.matmul(banks[s], sel_e[:, :], bias_parts[:, 2 * D + s * 512:2 * D + (s + 1) * 512],
                                       start=True, stop=False)
            ins.then_inc(S["bias_done"], 1)
            pe.wait_ge(S["actT_ready"], i * 2 + 1)
            products(i, 8, banks, aT_hi, aT_lo, aT_raw, False)
            pe.wait_ge(S["gathered"], i * 16 + 32)
            turn_x(0, 1)
            turn_act(1)
            products(i, 9, banks, aT_hi, aT_lo, aT_raw, False)
            pe.wait_ge(S["actT_ready"], i * 2 + 2)
            products(i, 10, banks, aT_hi, aT_lo, aT_raw, False)
            pe.wait_ge(S["xT_ready"], i * 2 + 3)
            turn_x(1, 1)
            products(i, 11, banks, aT_hi, aT_lo, aT_raw, True)

        with pe.Fori(0, NE) as i:
            expert_block(i)
        pe.wait_ge(S["table_ready"], 1)
        n_ovf = pe.value_load(ovf_table[0:1, NOVF:NOVF + 1], min_val=0, max_val=NOVF)
        with pe.If(n_ovf > 0):
            with pe.Fori(NE, n_ovf + NE) as i:
                expert_block(i)

    stack.close()


def layouts(i):
    def c(a):
        return np.ascontiguousarray(a)

    def rows(a, n):
        return np.broadcast_to(a, (n,) + a.shape)

    k = shape_constants()
    x = np.concatenate([i["x_prompt"].reshape(NP_T, P, D), i["x_sample"].reshape(1, P, D)])
    cond = np.concatenate([i["c_prompt"], i["c_sample"]])
    ada = i["w_ada"][0].reshape(2, 4, P, N_MOD, 512).transpose(3, 0, 2, 1, 4)
    g2 = np.zeros((N_MOD, 512), np.float32)
    g2[2:4], g2[8:10] = i["g_attn_norm"][0].reshape(2, 512), i["g_ffn_norm"][0].reshape(2, 512)
    ada_rows = np.stack([i["b_ada"][0].reshape(N_MOD, 512), g2], axis=1)
    gu = i["w_gate_up"][0].reshape(NE, 4, 2, P, 2, 2, 512).transpose(0, 5, 1, 3, 2, 4, 6)
    dn = i["w_down"][0].reshape(NE, 4, 2, P, D).transpose(0, 1, 3, 2, 4)
    moe = np.concatenate([gu.reshape(NE, 8, P, UNIT), dn.reshape(NE, 4, P, UNIT)], axis=1)
    sk = i["swa_sinks"][0]
    w_in = i["w_in"][0]
    w_qs = w_in[:, O_QS:O_KS].reshape(D, KVH, GRP, HD).transpose(0, 2, 1, 3).reshape(D, H * HD)
    w_in = np.concatenate([w_in[:, :O_QS], w_qs, w_in[:, O_KS:]], axis=1)
    return {
        "x_in": c(x),
        "c_t": c(cond.T.reshape(KT, P, 9).transpose(1, 0, 2)),
        "cache_lat": c(i["cache_mla_latent"][0].reshape(NB_DEC, PAST // P, P, KVL).transpose(0, 2, 1, 3)),
        "cache_lat_t": c(i["cache_mla_latent"][0].reshape(NB_DEC, PAST, 2, P).transpose(0, 3, 2, 1)),
        "cache_kr_t": c(i["cache_mla_krope"][0].transpose(0, 2, 1)),
        "cache_k_t": c(i["cache_swa_k"][0].reshape(NB_DEC, WINDOW, KVH * HD).transpose(0, 2, 1)),
        "cache_v": c(i["cache_swa_v"][0].reshape(NB_DEC, WINDOW, KVH * HD)),
        "cache_k_rows": c(i["cache_swa_k"][0].reshape(NB_DEC, WINDOW, KVH * HD)),
        "ada_w": c(ada.reshape(N_MOD, 2, P, UNIT)),
        "ada_rows": c(np.broadcast_to(ada_rows[:, None], (N_MOD, 9, 2, 512))),
        "in_w": c(w_in.reshape(KT, P, 6, IN_COLS).transpose(2, 1, 0, 3).reshape(6, P, KT * IN_COLS)),
        "uq_w": c(i["w_uq"][0].reshape(3, P, H * QK).transpose(1, 0, 2)),
        "ukv_w": c(i["w_ukv"][0].reshape(2, P, H, NOPE + VD).transpose(1, 0, 2, 3)),
        "uk_t": c(i["w_ukv"][0][:, :, 0:NOPE].transpose(2, 1, 0)),
        "out_w": c(i["w_out"][0].reshape(KT, P, 4, OUT_COLS).transpose(2, 1, 0, 3).reshape(4, P, KT * OUT_COLS)),
        "rows_q_kv": c(rows(np.concatenate([i["g_q_norm"][0], i["g_kv_norm"][0]]), P)),
        "sink_cols": c(np.concatenate([rows(sk, P), np.repeat(sk, Q_DEC)[:, None]], axis=1)),
        "router_w": c(i["w_router"][0].reshape(KT, P, NE).transpose(1, 0, 2)),
        "router_b": c(rows(i["b_router"][0], P)),
        "moe_w": c(moe),
        "moe_b": c(np.concatenate([i["b_gate_up"][0], i["b_down"][0]], axis=1)),
        "g_final": c(rows(i["g_final"], P)),
        "c_ident": k["ident"], "c_rope": k["rope"], "c_causal": k["causal"], "c_dist": k["dist"],
        "c_alibi": k["alibi"], "c_kind": k["kind_sel"].reshape(96, 2 * P), "c_before": k["before"].reshape(P, 2 * P),
        "c_eid": k["expert_id"], "c_rowe": k["row_expert"], "c_blk": k["block_id"].reshape(P, NOVF, NE),
        "c_tok": k["token_id"], "c_slot": k["slot_id"],
    }


def kernel(**inputs):
    import concourse.bacc as _bacc
    from concourse.bass_utils import run_bass_kernel_spmd as _run

    nc = _bacc.Bacc("TRN2", target_bir_lowering=False, num_devices=1)
    arrays, ins, outs = {}, [], []
    for name, a in layouts({k: np.asarray(v) for k, v in inputs.items()}).items():
        arrays[f"in_{name}"] = a
        ins.append(nc.dram_tensor(f"in_{name}", a.shape, mybir.dt.from_np(a.dtype), kind="ExternalInput").ap())
    for n, shape in enumerate(OUT_SHAPES):
        outs.append(nc.dram_tensor(f"out_{n}", shape, F32, kind="ExternalOutput").ap())
    build(nc, ins, outs)
    r = _run(nc, [arrays], core_ids=[0])
    return tuple(r.results[0][f"out_{n}"] for n in range(len(OUT_SHAPES)))
```

```python
from contextlib import ExitStack

import numpy as np

import concourse.bass as bass
from concourse import mybir

F32 = mybir.dt.float32
F32R = mybir.dt.float32r
BF16 = mybir.dt.bfloat16
I32 = mybir.dt.int32
U32 = mybir.dt.uint32
ALU = mybir.AluOpType
ACT = mybir.ActivationFunctionType
AX = mybir.AxisListType.X

P = 128
D = 1024
KT = D // P
SEQ, NB_DEC, Q_DEC, PAST = 256, 8, 16, 512
NT = 3
NP_T = 2
CHUNK, WINDOW = 64, 128
H, NOPE, ROPE, VD = 8, 64, 32, 64
QK = NOPE + ROPE
QL, KVL = 384, 256
KVH, GRP, HD = 2, 4, 64
IN_W = QL + KVL + ROPE + H * HD + 2 * KVH * HD
O_KV, O_KPE, O_QS = QL, QL + KVL, QL + KVL + ROPE
O_KS = O_QS + H * HD
O_VS = O_KS + KVH * HD
MLA_SCALE = float(QK) ** -0.5
SWA_SCALE = float(HD) ** -0.5
NE, TOPK = 32, 4
DFF = D
EPS = 1e-6
BIG = 1e30

UNIT = 2048
SLOTS = 6
IN_COLS = IN_W // 6
J_LATENT = (O_QS - 1) // IN_COLS
OUT_COLS = 256
N_MOD = 6 * D // 512
EARLY_MOD = 6
GATE_MOD = 10
SPLIT = 4
PIECES = 6
PIECE_AT = (0, 2, 3, 5)
PIECE_N = (2, 1, 2, 1)
MOE_UNITS = 12
NOVF = NT * P * TOPK // (P + 1)
NBLK = NE + NOVF + 1

QUERY_ORDER = (("q", 0), ("q", 1), ("qT", 0), ("q", 2), ("qT", 1), ("qT", 2))

OUT_SHAPES = [
    (1, SEQ, D), (NB_DEC, Q_DEC, D),
    (1, 1, SEQ, KVL), (1, 1, SEQ, ROPE), (1, 1, WINDOW, KVH, HD), (1, 1, WINDOW, KVH, HD),
    (1, NB_DEC, Q_DEC, KVL), (1, NB_DEC, Q_DEC, ROPE),
    (1, NB_DEC, WINDOW, KVH, HD), (1, NB_DEC, WINDOW, KVH, HD),
]


def shape_constants():
    c = {}
    c["ident"] = np.eye(P, dtype=np.float32)
    pos = np.concatenate([np.arange(SEQ), np.tile(PAST + np.arange(Q_DEC), NB_DEC)]).astype(np.float32)
    inv = np.float32(10000.0) ** (-np.arange(ROPE // 2, dtype=np.float32) * np.float32(2.0) / np.float32(ROPE))
    ang = (pos[:, None] * inv[None, :]).astype(np.float32)
    cs = np.concatenate([np.cos(ang), np.sin(ang)], axis=1).astype(np.float32)
    c["rope"] = np.ascontiguousarray(cs.reshape(NT, P, ROPE).transpose(1, 0, 2))
    q = np.arange(SEQ)
    qc, kc = q[:, None] // CHUNK, q[None, :] // CHUNK
    mask = np.where(kc <= qc, 0.0, -BIG).astype(np.float32)
    c["causal"] = np.ascontiguousarray(mask.reshape(NP_T, P, SEQ).transpose(1, 0, 2))
    seen = (kc <= qc) & (kc >= qc - WINDOW // CHUNK)
    dist = np.where(seen, np.abs(q[:, None] - q[None, :]), BIG * 1e4).astype(np.float32)
    c["dist"] = np.ascontiguousarray(dist.reshape(NP_T, P, SEQ).transpose(1, 0, 2))
    slope = 2.0 ** (-8.0 * np.arange(1, H + 1) / H)
    rel = np.abs(np.arange(Q_DEC)[:, None] + WINDOW - np.arange(WINDOW + Q_DEC)[None, :])
    c["alibi"] = (-slope[:, None, None] * rel[None] / SWA_SCALE).reshape(P, WINDOW + Q_DEC).astype(np.float32)
    sel = np.zeros((96, 2, P), np.float32)
    for part in range(3):
        sel[32 * part, 0, :] = 1.0
        for t in range(P):
            sel[32 * part + 1 + t // Q_DEC, 1, t] = 1.0
    c["kind_sel"] = sel
    tri = np.zeros((P, 2, P), np.float32)
    tri[:, 0, :] = np.triu(np.ones((P, P)), 1)
    tri[:, 1, :] = 1.0
    c["before"] = tri
    c["expert_id"] = np.tile(np.arange(NE, dtype=np.float32), (P, 1))
    c["row_expert"] = np.tile((np.arange(96) % 32).astype(np.float32)[:, None], (1, P))
    c["block_id"] = np.tile(np.arange(NOVF, dtype=np.float32)[:, None], (1, NE)).reshape(1, -1).repeat(P, 0)
    c["token_id"] = (np.arange(NT)[None, :] * P + np.arange(P)[:, None]).astype(np.float32)
    c["slot_id"] = np.tile(np.arange(P, dtype=np.float32), (P, 1))
    return c


def psum_jobs():
    early = [(("mod", n), "v") for n in range(4)]
    early += [(("mod", 4), "v")]
    early += [(("b" + w, k, f), "v") for k in range(2) for f in range(2) for w in ("scale", "shift")]
    early += [(("mod", 5), "v")]
    early += [(("hT", t, g), "a") for t in range(NT) for g in range(2)]
    early += [(("u", j, t), "a") for j in range(6) for t in range(NT)]
    early += [(("qlT", t), "a") for t in range(NT)]
    early += [(("ckT", t), "a") for t in range(NT)]
    early += [(("qsT", t), "a") for t in range(NT)] + [(("ksT",), "a")]
    early += [(("gate", k, f), "a") for k in range(2) for f in range(2)]
    early += [(("v", t), "a") for t in range(NP_T)]
    early += [((w, t, f), "v" if w == "q" else "a") for w, t in QUERY_ORDER for f in range(2)]
    early += [(("qabs", p), "a") for p in range(4)] + [(("kT", p), "a") for p in range(4)]
    late = [(("oS",), "a")]
    late += [(("o", j, t), "v") for j in range(4) for t in range(NT)]
    late += [(("f" + w, k, f), "v") for k in range(2) for f in range(2) for w in ("scale", "shift")]
    late += [(("fT", t, g), "a") for t in range(NT) for g in range(2)]
    late += [(("logit", t), "v") for t in range(NT)]
    late += [(("rank", t), "v") for t in range(NT)] + [(("count",), "v"), (("table",), "v")]
    return early, late


def attention_items():
    items = []
    for b in range(NB_DEC):
        for j in (2 * b, 2 * b + 1):
            items += [("mla", j // H, j % H), ("swa", j // H, j % H)]
        items += [("mla_s", b, 0), ("swa_s", b, 0)]
    return items



def build(nc, ins, outs):
    (x_in, c_t, cache_lat, cache_lat_t, cache_kr_t, cache_k_t, cache_v, cache_k_rows, ada_w, ada_rows,
     in_w, uq_w, ukv_w, uk_t, out_w, rows_q_kv, sink_cols, router_w, router_b, moe_w, moe_b, g_final,
     c_ident, c_rope, c_causal, c_dist, c_alibi, c_kind, c_before, c_eid, c_rowe, c_blk, c_tok, c_slot) = ins
    (o_yp, o_ys, o_latp, o_krp, o_kp, o_vp, o_lats, o_krs, o_ks, o_vs) = outs
    stack = ExitStack()

    def sb(name, shape, dt=F32, scope=stack):
        return scope.enter_context(nc.sbuf_tensor(name, shape, dt))

    def sem(name):
        return stack.enter_context(nc.semaphore(name))

    h_rows = nc.dram_tensor("h_rows", [NT * P, D], F32, kind="Internal").ap()
    y_rows = nc.dram_tensor("y_rows", [(NBLK - 1) * P, D], F32, kind="Internal").ap()

    ps = stack.enter_context(nc.psum_tensor("ps", [P, 8, 512], F32))

    ring = sb("ring", [P, SLOTS, UNIT])
    x = sb("x", [P, NT, D])
    mod_parts = sb("mod_parts", [96, 6 * D], BF16)
    gates = sb("gates", [P, 2, D])
    ident = sb("ident", [P, P])
    kind_sel = sb("kind_sel", [96, 2, P], BF16)
    before = sb("before", [P, 2, P], BF16)
    expert_id = sb("expert_id", [P, NE])
    row_expert = sb("row_expert", [96, P])
    block_id = sb("block_id", [P, NOVF, NE])
    token_id = sb("token_id", [P, NT])
    slot_id = sb("slot_id", [P, P])
    gate_w = sb("gate_w", [P, NT, TOPK])
    y_row_idx = sb("y_row_idx", [P, NT * TOPK], I32)
    slot_tok = sb("slot_tok", [P, NBLK], I32)
    block_expert = sb("block_expert", [P, NBLK])
    ovf_table = sb("ovf_table", [1, NOVF + 1], I32)
    stat = sb("stat", [P, 68])
    cs = sb("cs", [P, KT, 9])

    gfin = gates[:, 0, :]

    pre = ExitStack()

    def pb(name, shape, dt=F32):
        return sb(name, shape, dt, pre)

    pre_base = nc.sbuf_base
    hm = pb("hm", [P, KT, NT * P])
    hq = pb("hq", [P, NT * D])
    qabs = pb("qabs", [P, 2, NB_DEC, H, Q_DEC])
    kT = pb("kT", [QK, H, SEQ])
    w_ukv = pb("w_ukv", [P, 2, H, NOPE + VD])
    v_p = pb("v_p", [P, NP_T, H * VD])
    v_swa = pb("v_swa", [P, NT, KVH * HD])
    qsT = pb("qsT", [P, NP_T, GRP, P])
    qsT_s = pb("qsT_s", [P, NB_DEC, GRP, Q_DEC])
    ksT = pb("ksT", [P, NT * P])
    ckT = pb("ckT", [P, 2, NT * P])
    kpT = pb("kpT", [QK, NT * P])
    q_tok = pb("q_tok", [P, H, QK])
    rope = pb("rope", [P, NT, ROPE])
    rt = pb("rt", [P, 4, 96])
    causal = pb("causal", [P, NP_T, SEQ])
    dist = pb("dist", [P, NP_T, SEQ])
    alibi = pb("alibi", [P, WINDOW + Q_DEC])
    g_qkv = pb("g_qkv", [P, QL + KVL])
    sinks = pb("sinks", [P, H + 1])
    sinks_s = pb("sinks_s", [P, H + 1])
    w_rt = pb("w_rt", [P, KT, NE])
    b_rt = pb("b_rt", [P, NE])
    cT = pb("cT", [P, KT, 9])
    mod_rows = pb("mod_rows", [9, 2, 512])
    row_max = pb("row_max", [P, 48])
    neg_max = pb("neg_max", [P, 48])
    row_sum = pb("row_sum", [P, 48])
    sink_e = pb("sink_e", [P, 48])
    row_inv = pb("row_inv", [P, 48])
    rtr = pb("rtr", [P, 12, NE])
    mod_row_base = nc.sbuf_base
    mod_row = pb("mod_row", [9, 512])
    mod_res = pb("mod_res", [9, 512])
    mod_p2 = pb("mod_p2", [9, 512], BF16)
    h = hq[:, :].rearrange("p (t d) -> p t d", t=NT)
    qT = hq[0:QK, 0:NP_T * H * P].rearrange("p (t h n) -> p t h n", t=NP_T, h=H)
    qT_s = hq[0:QK, NP_T * H * P:].rearrange("p (b h q) -> p b h q", b=NB_DEC, h=H)
    hT = hm
    mixT = hm
    w_uq = hm[:, :, :].rearrange("p k t -> p (k t)")[:, 0:3 * H * QK].rearrange("p (k n) -> p k n", k=3)
    qlT = qabs[:, :, :, :, :].rearrange("p a b h q -> p (a b h q)")[:, 0:3 * NT * P].rearrange(
        "p (k t) -> p k t", k=3)
    wukT = kT[0:NOPE, :, :]
    q_flat = q_tok[:, :, :].rearrange("p h d -> p (h d)")
    cv_s = q_flat[:, 0:2 * P].rearrange("p (b n) -> p b n", b=2)
    new_v = q_flat[0:Q_DEC, 2 * P:4 * P].rearrange("p (b n) -> p b n", b=2)
    tail_base = nc.sbuf_base

    su = ExitStack()
    u = sb("u", [P, NT, IN_W], F32, su)
    su.close()

    st = ExitStack()
    early_rows = sb("early_rows", [9, EARLY_MOD, 2, 512], F32, st)
    st.close()

    att = ExitStack()
    latT = sb("latT", [P, 2, 2, PAST], F32, att)
    lat = sb("lat", [P, 2, PAST // P, KVL], F32, att)
    krT = sb("krT", [QK, 2, PAST], F32, att)
    ck_sT = sb("ck_sT", [P, 2, WINDOW], F32, att)
    new_lat = sb("new_lat", [Q_DEC, 2, KVL], F32, att)
    probs = sb("probs", [P, 2, PAST + Q_DEC], F32, att)
    pT = sb("pT", [P, 2, 5 * P], F32, att)
    att.close()

    late = ExitStack()
    bias_parts = sb("bias_parts", [96, 3 * D], BF16, late)
    bias_src = sb("bias_src", [NE, 3 * D], F32, late)
    bias_p2 = sb("bias_p2", [NE, 3 * D], BF16, late)
    gate_rows = sb("gate_rows", [9, N_MOD - GATE_MOD, 2, 512], F32, late)
    late.close()
    pre.close()

    tab = ExitStack()
    assert nc.sbuf_base == pre_base
    place = sb("place", [P, NT * TOPK, P], F32R, tab)
    where = sb("where", [P, NT * TOPK, NBLK], F32R, tab)
    hq_again = sb("hq_again", [P, 2 * NT * D - (NT * TOPK) * (P + NBLK)], F32, tab)
    route_hot = sb("route_hot", [P, NT * TOPK, NE], F32, tab)
    route_prod = sb("route_prod", [P, NT * TOPK, NE], F32, tab)
    route_fld = sb("route_fld", [P, 7, NT, NE], F32, tab)
    chosen = sb("chosen", [P, NT, NE], BF16, tab)
    tab_end = nc.sbuf_base
    tab.close()
    moe = ExitStack()
    x_slots = sb("x_slots", [P, D], F32, moe)
    xT_hi = sb("xT_hi", [P, PIECES, P], F32R, moe)
    xT_lo = sb("xT_lo", [P, PIECES, P], F32R, moe)
    xT_raw = sb("xT_raw", [P, 2, P], F32, moe)
    aT_hi = sb("aT_hi", [P, PIECES, P], F32R, moe)
    aT_lo = sb("aT_lo", [P, PIECES, P], F32R, moe)
    aT_raw = sb("aT_raw", [P, 2, P], F32, moe)
    y_blk = sb("y_blk", [P, D], F32, moe)
    glu = sb("glu", [P, 2, 512], F32, moe)
    sig = sb("sig", [P, 2, 512], F32, moe)
    lin = sb("lin", [P, 2, 512], F32, moe)
    sel_e = sb("sel_e", [96, P], BF16, moe)
    cur_idx = sb("cur_idx", [P, 1], I32, moe)
    assert nc.sbuf_base >= tab_end
    fin = ExitStack()
    y_got = sb("y_got", [P, NT * TOPK, D], F32, fin)
    fin.close()
    w_hi = sb("w_hi", [P, PIECES, UNIT // 2], F32R, moe)
    w_lo = sb("w_lo", [P, PIECES, UNIT // 2], F32R, moe)
    assert nc.sbuf_base <= mod_row_base, (nc.sbuf_base, mod_row_base)
    moe.close()

    S = {}
    for name in (
            "loaded_c loaded_tables loaded_x loaded_small loaded_uq loaded_rows loaded_gate_rows gates_filled "
            "loaded_bias loaded_gfin "
            "psum_filled v_emptied a_emptied unit_used raw_used v_step p_step zeroed consts_cast "
            "sig_ready silu_ready ss_ready ms_ready root_ready parts_ready ql_ready ck_ready u_stats "
            "lat_stored out_stored rows_zeroed v_swa_ready k_rope_ready "
            "scored maxed exped normed flipped pT_ready pv_done o_ready mod_extra mod_extra_used "
            "x1_ready bias_ready logits_exp gates_exped probs_top placed h_stored table_ready "
            "sel_ready bias_done gu_emptied glu_ready sig_done act_ready hi_ready lo_ready xT_hi_ready aT_hi_ready "
            "actT_filled actT_ready "
            "xT_filled xT_ready gathered idx_ready y_copied y_stored "
            "first_term x2_ready fin_ss fin_root fin_ready fin_stored gsg_ready pool_gate").split():
        S[name] = sem(name)
    slot_sem = [sem(f"slot_full{s}") for s in range(SLOTS)]
    got_sem = [sem(f"got_rows{n}") for n in range(NT * TOPK)]
    cache_sem = [sem(f"cache_full{s}") for s in range(2)]

    early, late_jobs = psum_jobs()
    jobs = early + late_jobs
    number = {key: i for i, (key, _) in enumerate(jobs)}
    engine_of = dict(jobs)
    ordinal, seen = {}, {"v": 0, "a": 0}
    for key, who in jobs:
        seen[who] += 1
        ordinal[key] = seen[who]

    def bank(*key):
        return ps[:, number[key] % 8, :]

    def filled(eng, *key):
        eng.wait_ge(S["psum_filled"], number[key] + 1)

    def emptied(eng, *key):
        eng.wait_ge(S["v_emptied"] if engine_of[key] == "v" else S["a_emptied"], ordinal[key])

    n_early = {w: sum(1 for _, e in early if e == w) for w in "va"}
    n_all = {w: sum(1 for _, e in jobs if e == w) for w in "va"}

    units = [("ada", n, f) for n in range(EARLY_MOD) for f in range(2)]
    units += [("in", j) for j in range(6)]
    units += [("ada", n, f) for n in range(EARLY_MOD, GATE_MOD) for f in range(2)]
    units += [("out", j) for j in range(4)]
    units += [("ada", n, f) for n in range(GATE_MOD, N_MOD) for f in range(2)]
    unit_no = {k: i for i, k in enumerate(units)}
    N_PRE = len(units)
    N_TABLES = 15
    HALVES = N_MOD

    def unit(key):
        return ring[:, unit_no[key] % SLOTS, :]

    def unit_here(eng, key):
        n = unit_no[key]
        eng.wait_ge(slot_sem[n % SLOTS], 16 * (n // SLOTS + 1))

    def used_up(eng, key):
        if key[0] == "ada" and key[2] == 0:
            eng.wait_ge(S["unit_used"], key[1] + 1)
        elif key[0] == "ada" and key[1] < EARLY_MOD:
            filled(eng, "mod", key[1])
        elif key[0] == "ada":
            eng.wait_ge(S["mod_extra"], key[1] - EARLY_MOD + 1)
        else:
            filled(eng, "u" if key[0] == "in" else "o", key[1], NT - 1)

    def moe_slot(j):
        return (N_PRE + j) % SLOTS

    def moe_full(i, j):
        return ((N_PRE + j) // SLOTS + 1) * 16 + i * (16 * MOE_UNITS // SLOTS)

    def moe_used(i, j):
        return i * MOE_UNITS + (HALVES + j + 1)

    def piece(w, n):
        return w[:, PIECE_AT[n % 4]:PIECE_AT[n % 4] + PIECE_N[n % 4], :].rearrange("p k n -> p (k n)")

    def piece_src(n):
        return ring[:, moe_slot(n), 0:PIECE_N[n % 4] * UNIT // 2]

    MOD_PLACES = (1, 2, 3, 5)
    items = attention_items()
    t_bank = [ps[:, 6, :], ps[:, 7, :]]

    def width(i):
        kind, n, _ = items[i]
        return {"mla": P * (n + 1), "swa": P * (n + 1), "mla_s": PAST + Q_DEC, "swa_s": WINDOW + Q_DEC}[kind]

    def full_tiles(i):
        kind, n, _ = items[i]
        return {"mla": n + 1, "swa": n + 1, "mla_s": PAST // P, "swa_s": 1}[kind]

    score_bank = (3, 0, 2, 3, 0, 2)

    def scores(i):
        b = score_bank[i % 6]
        return ps[:, b:b + (2 if items[i][0] == "mla_s" else 1), :].rearrange("p a b -> p (a b)")

    block = stack.enter_context(nc.Block())

    @block.sync
    def _(sp):
        nc.sync.dma_start(cT[:, :, :], c_t).then_inc(S["loaded_c"], 16)
        for n, key in enumerate(units):
            if n >= SLOTS:
                used_up(sp, units[n - SLOTS])
            if key[0] == "ada":
                src, dst = ada_w[key[1], key[2]], ring[:, n % SLOTS, :]
            elif key[0] == "in":
                src, dst = in_w[key[1]], ring[:, n % SLOTS, 0:KT * IN_COLS]
            else:
                src, dst = out_w[key[1]], ring[:, n % SLOTS, :]
            nc.sync.dma_start(dst, src).then_inc(slot_sem[n % SLOTS], 16)

        def stream(i, expert, first=0):
            for j in range(first, MOE_UNITS):
                if PIECE_N[j % 4] == 2:
                    sp.wait_ge(S["lo_ready"], i * MOE_UNITS + (j + 1))
                else:
                    sp.wait_ge(S["raw_used"], i * (MOE_UNITS // 2) + (j + 1) // 2)
                src = moe_w[bass.ds(expert, 1), j].rearrange("e p n -> (e p) n")
                nc.sync.dma_start(ring[:, moe_slot(j), :], src).then_inc(slot_sem[moe_slot(j)], 16)

        for j in range(SLOTS):
            used_up(sp, units[N_PRE - SLOTS + j])
            nc.sync.dma_start(ring[:, moe_slot(j), :], moe_w[0, j]).then_inc(slot_sem[moe_slot(j)], 16)
        stream(0, 0, first=SLOTS)
        with sp.Fori(1, NE) as i:
            stream(i, i)
        sp.wait_ge(S["table_ready"], 1)
        n_ovf = sp.value_load(ovf_table[0:1, NOVF:NOVF + 1], min_val=0, max_val=NOVF)
        with sp.If(n_ovf > 0):
            with sp.Fori(NE, n_ovf + NE) as i:
                expert = sp.value_load(ovf_table[0:1, bass.ds(i - NE, 1)], min_val=0, max_val=NE - 1)
                stream(i, expert)
        for j in range(SPLIT):
            if PIECE_N[j % 4] == 2:
                sp.wait_ge(S["lo_ready"], (n_ovf + NE) * MOE_UNITS + (j + 1))
            else:
                sp.wait_ge(S["raw_used"], (n_ovf + NE) * (MOE_UNITS // 2) + (j + 1) // 2)
            nc.sync.dma_start(ring[:, moe_slot(j), :], moe_w[0, j]).then_inc(slot_sem[moe_slot(j)], 16)

    @block.gpsimd
    def _(pool):
        nc.gpsimd.dma_start(early_rows[:, :, :, :], ada_rows[0:EARLY_MOD].rearrange("n r a c -> r n a c")).then_inc(
            S["loaded_rows"], 16)
        pool.wait_ge(S["loaded_small"], 16 * 3)
        qf = q_tok[:, :, :].rearrange("p h d -> p (h d)")
        nc.gpsimd.tensor_copy(kind_sel[:, :, :].rearrange("p a b -> p (a b)"), qf[0:96, 0:2 * P]).then_inc(S["consts_cast"], 1)
        nc.gpsimd.tensor_copy(before[:, :, :].rearrange("p a b -> p (a b)"), qf[:, 2 * P:4 * P]).then_inc(S["consts_cast"], 1)

        zeros = qabs[:, :, :, :, :].rearrange("p a b h q -> p (a b h q)")[:, 0:D]
        nc.gpsimd.memset(zeros, 0.0).then_inc(S["zeroed"], 1)
        pool.wait_ge(S["zeroed"], 1)
        filled(pool, "u", 0, 0)
        for n in range(NE, NBLK - 1):
            nc.gpsimd.dma_start(y_rows[n * P:(n + 1) * P, :], zeros).then_inc(S["rows_zeroed"], 16)
        nc.gpsimd.dma_start(o_ks[0, :, 0:WINDOW - Q_DEC].rearrange("b t k d -> b t (k d)"),
                            cache_k_rows[:, Q_DEC:WINDOW]).then_inc(S["out_stored"], 16)
        nc.gpsimd.dma_start(o_vs[0, :, 0:WINDOW - Q_DEC].rearrange("b t k d -> b t (k d)"),
                            cache_v[:, Q_DEC:WINDOW]).then_inc(S["out_stored"], 16)

        filled(pool, "u", 5, NT - 1)
        nc.gpsimd.dma_start(w_uq, uq_w).then_inc(S["loaded_uq"], 16)

        pool.wait_ge(S["ck_ready"], 1)
        emptied(pool, "u", 5, NT - 1)
        for t in range(NP_T):
            nc.gpsimd.dma_start(o_latp[0, 0, t * P:(t + 1) * P], u[:, t, O_KV:O_KPE]).then_inc(S["out_stored"], 16)
            nc.gpsimd.dma_start(o_krp[0, 0, t * P:(t + 1) * P], u[:, t, O_KPE:O_QS]).then_inc(S["out_stored"], 16)
        nc.gpsimd.dma_start(o_kp[0, 0].rearrange("t k d -> t (k d)"), u[:, 1, O_KS:O_VS]).then_inc(S["out_stored"], 16)
        nc.gpsimd.dma_start(o_vp[0, 0].rearrange("t k d -> t (k d)"), u[:, 1, O_VS:IN_W]).then_inc(S["out_stored"], 16)
        nc.gpsimd.dma_start(o_krs[0].rearrange("b q c -> (b q) c"), u[:, 2, O_KPE:O_QS]).then_inc(S["out_stored"], 16)
        nc.gpsimd.dma_start(o_lats[0].rearrange("b q c -> (b q) c"), u[:, 2, O_KV:O_KPE]).then_inc(S["lat_stored"], 16)
        for b in range(NB_DEC):
            rows = slice(b * Q_DEC, (b + 1) * Q_DEC)
            nc.gpsimd.dma_start(o_ks[0, b, WINDOW - Q_DEC:WINDOW].rearrange("t k d -> t (k d)"),
                                u[rows, 2, O_KS:O_VS]).then_inc(S["out_stored"], 16)
            nc.gpsimd.dma_start(o_vs[0, b, WINDOW - Q_DEC:WINDOW].rearrange("t k d -> t (k d)"),
                                u[rows, 2, O_VS:IN_W]).then_inc(S["lat_stored"], 16)
        n_out = 2 + 2 * NP_T + 3 + NB_DEC

        pool.wait_ge(S["out_stored"], 16 * n_out)
        pool.wait_ge(S["lat_stored"], 16 * (1 + NB_DEC))
        pool.wait_ge(S["v_swa_ready"], 1)
        filled(pool, "ksT")
        filled(pool, "ckT", NT - 1)
        filled(pool, "qlT", NT - 1)
        filled(pool, "qsT", NT - 1)
        filled(pool, "qT", NT - 1, 1)
        for b in range(NB_DEC):
            if b >= 2:
                pool.wait_ge(S["pv_done"], 6 * (b - 1))
            k = b % 2
            for dst, src in ((latT[:, k], cache_lat_t[b]), (lat[:, k], cache_lat[b]),
                             (krT[NOPE:QK, k], cache_kr_t[b]), (ck_sT[:, k], cache_k_t[b]), (cv_s[:, k], cache_v[b]),
                             (new_lat[:, k], o_lats[0, b]),
                             (new_v[:, k], o_vs[0, b, WINDOW - Q_DEC:WINDOW].rearrange("t k d -> t (k d)"))):
                nc.gpsimd.dma_start(dst, src).then_inc(cache_sem[k], 16)
            if b < GATE_MOD - EARLY_MOD:
                pool.wait_ge(S["parts_ready"], EARLY_MOD + b)
                nc.gpsimd.dma_start(mod_rows[:, :, :], ada_rows[EARLY_MOD + b]).then_inc(S["loaded_rows"], 16)

        pool.wait_ge(S["o_ready"], len(items))
        nc.gpsimd.dma_start(bias_src[:, :], moe_b).then_inc(S["loaded_bias"], 16)
        nc.gpsimd.dma_start(gate_rows[:, :, :, :], ada_rows[GATE_MOD:N_MOD].rearrange("n r a c -> r n a c")).then_inc(
            S["loaded_gate_rows"], 16)
        pool.wait_ge(S["loaded_bias"], 16)
        steps = [0]

        def step(ins):
            steps[0] += 1
            ins.then_inc(S["p_step"], 1)
            pool.wait_ge(S["p_step"], steps[0])

        step(nc.gpsimd.tensor_copy(bias_parts[0:NE, :], bias_src[:, :]))
        step(nc.gpsimd.tensor_tensor(bias_src[:, :], bias_src[:, :], bias_parts[0:NE, :], ALU.subtract))
        step(nc.gpsimd.tensor_copy(bias_p2[:, :], bias_src[:, :]))
        step(nc.gpsimd.tensor_tensor(bias_src[:, :], bias_src[:, :], bias_p2[:, :], ALU.subtract))
        step(nc.gpsimd.tensor_copy(bias_parts[NE:2 * NE, :], bias_p2[:, :]))
        nc.gpsimd.tensor_copy(bias_parts[2 * NE:3 * NE, :], bias_src[:, :]).then_inc(S["bias_ready"], 1)
        pool.wait_ge(S["bias_ready"], 1)

        emptied(pool, "table")
        pool.wait_ge(S["h_stored"], 16 * NT)

        def gather(i, first=False):
            if not first:
                pool.wait_ge(S["gathered"], i * 16)
                pool.wait_ge(S["xT_filled"], i * 2)
            col = slot_tok[:, 0:1] if first else slot_tok[:, bass.ds(i, 1)]
            nc.gpsimd.tensor_copy(cur_idx[:, :], col).then_inc(S["idx_ready"], 1)
            pool.wait_ge(S["idx_ready"], 1 if first else i + 1)
            if not first:
                pool.sem_inc(S["pool_gate"], 1)
            nc.gpsimd.indirect_dma_start(
                out=x_slots[:, :], out_offset=None, in_=h_rows,
                in_offset=bass.IndirectOffsetOnAxis(ap=cur_idx[:, 0:1], axis=0)).then_inc(S["gathered"], 16)

        gather(0, first=True)
        with pool.Fori(0, NE) as i:
            gather(i + 1)
        n_ovf = pool.value_load(ovf_table[0:1, NOVF:NOVF + 1], min_val=0, max_val=NOVF)
        with pool.If(n_ovf > 0):
            with pool.Fori(NE, n_ovf + NE) as i:
                gather(i + 1)

        pool.wait_ge(S["lo_ready"], (n_ovf + NE) * MOE_UNITS + (SLOTS + SPLIT))
        pool.wait_ge(S["y_stored"], (n_ovf + NE) * 16 + 16)
        pool.sem_inc(S["pool_gate"], 1)
        for n in range(NT * TOPK):
            nc.gpsimd.indirect_dma_start(
                out=y_got[:, n, :], out_offset=None, in_=y_rows,
                in_offset=bass.IndirectOffsetOnAxis(ap=y_row_idx[:, n:n + 1], axis=0)).then_inc(got_sem[n], 16)
        pool.wait_ge(S["out_stored"], 16 * n_out)
        pool.wait_ge(S["gathered"], (n_ovf + NE + 1) * 16)

    @block.scalar
    def _(a):
        qf = q_tok[:, :, :].rearrange("p h d -> p (h d)")
        nc.scalar.dma_start(qf[0:96, 0:2 * P], c_kind).then_inc(S["loaded_small"], 16)
        nc.scalar.dma_start(qf[:, 2 * P:4 * P], c_before).then_inc(S["loaded_small"], 16)
        for t in range(NT):
            nc.scalar.dma_start(x[:, t, :], x_in[t]).then_inc(S["loaded_x"], 16)
        nc.scalar.dma_start(ident[:, :], c_ident).then_inc(S["loaded_small"], 16)

        a.wait_ge(S["loaded_c"], 16)
        csig = rtr[:, :, :].rearrange("p a b -> p (a b)")[:, 0:KT * 9]
        nc.scalar.activation(csig, cT[:, :, :].rearrange("p k n -> p (k n)"), ACT.Sigmoid).then_inc(S["sig_ready"], 1)

        def x_squares(dst, cols, n0, done):
            for t in range(NT):
                nc.scalar.activation(dst[:, 0:cols.stop - cols.start], x[:, t, cols], ACT.Square,
                                     accum_out=stat[:, n0 + t:n0 + t + 1]).then_inc(S["ss_ready"], 1)
                a.wait_ge(S["ss_ready"], done + t + 1)

        def x_root(n0, ms):
            a.wait_ge(S["ms_ready"], ms)
            nc.scalar.activation(stat[:, n0 + 3:n0 + 6], stat[:, n0 + 6:n0 + 9], ACT.Sqrt).then_inc(S["root_ready"], 1)

        a.wait_ge(S["loaded_x"], 16 * NT)
        x_squares(hq, slice(0, D), 0, 0)
        x_root(0, 1)
        rest = ((kT[0:NOPE, :, :], uk_t), (w_ukv[:, :, :, :], ukv_w), (rope[:, :, :], c_rope),
                (causal[:, :, :], c_causal), (dist[:, :, :], c_dist), (alibi[:, :], c_alibi), (g_qkv[:, :], rows_q_kv),
                (sinks[:, :], sink_cols), (w_rt[:, :, :], router_w), (b_rt[:, :], router_b), (expert_id[:, :], c_eid),
                (row_expert[:, :], c_rowe), (block_id[:, :, :], c_blk), (token_id[:, :], c_tok), (slot_id[:, :], c_slot))
        assert len(rest) == N_TABLES
        for dst, src in rest:
            nc.scalar.dma_start(dst, src).then_inc(S["loaded_tables"], 16)

        def empty(key, dst, src, last=True):
            ins = nc.scalar.copy(dst, src)
            if last:
                ins.then_inc(S["a_emptied"], 1)

        for t in range(NT):
            for g in range(2):
                filled(a, "hT", t, g)
                empty(("hT", t, g), hT[:, 4 * g:4 * g + 4, t * P:(t + 1) * P],
                      bank("hT", t, g).rearrange("p (k n) -> p k n", k=4))
        def latent_stats():
            a.wait_ge(S["a_emptied"], ordinal[("u", J_LATENT, NT - 1)])
            a.wait_ge(S["consts_cast"], 2)
            for t in range(NT):
                for c0, n, o in ((0, QL, 16 + t), (O_KV, KVL, 19 + t)):
                    nc.scalar.activation(qf[:, 0:n], u[:, t, c0:c0 + n], ACT.Square, scale=float(n) ** -0.5,
                                         accum_out=stat[:, o:o + 1]).then_inc(S["u_stats"], 1)
                    a.wait_ge(S["u_stats"], 2 * t + (2 if c0 else 1))
            a.wait_ge(S["ms_ready"], 2)
            nc.scalar.activation(stat[:, 28:34], stat[:, 22:28], ACT.Sqrt).then_inc(S["root_ready"], 1)

        for j in range(6):
            for t in range(NT):
                filled(a, "u", j, t)
                if (j, t) == (0, 0):
                    a.wait_ge(S["parts_ready"], EARLY_MOD)
                empty(("u", j, t), u[:, t, j * IN_COLS:(j + 1) * IN_COLS], bank("u", j, t)[:, 0:IN_COLS])
            if j == J_LATENT:
                latent_stats()
        a.wait_ge(S["rows_zeroed"], 16 * NOVF)
        for t in range(NT):
            filled(a, "qlT", t)
            empty(("qlT", t), qlT[:, :, t * P:(t + 1) * P], bank("qlT", t)[:, 0:3 * P].rearrange("p (k n) -> p k n", k=3))
        for t in range(NT):
            filled(a, "ckT", t)
            nc.scalar.copy(kpT[NOPE:QK, t * P:(t + 1) * P], bank("ckT", t)[0:ROPE, 2 * P:3 * P])
            empty(("ckT", t), ckT[:, :, t * P:(t + 1) * P], bank("ckT", t)[:, 0:2 * P].rearrange("p (k n) -> p k n", k=2))
        for t in range(NT):
            filled(a, "qsT", t)
            if t < NP_T:
                empty(("qsT", t), qsT[:, t, :, :], bank("qsT", t).rearrange("p (k n) -> p k n", k=GRP))
            else:
                empty(("qsT", t), qsT_s[:, :, :, :].rearrange("p b g q -> p g b q"),
                      bank("qsT", t).rearrange("p (g b q) -> p g b q", g=GRP, b=NB_DEC))
        filled(a, "ksT")
        empty(("ksT",), ksT[:, :], bank("ksT")[:, 0:NT * P])
        for k in range(2):
            for f in range(2):
                filled(a, "gate", k, f)
                empty(("gate", k, f), gates[:, k, f * 512:(f + 1) * 512], bank("gate", k, f))
        for t in range(NP_T):
            filled(a, "v", t)
            empty(("v", t), v_p[:, t, :], bank("v", t))
        for t in range(NT):
            for f in range(2):
                filled(a, "qT", t, f)
                if t < NP_T:
                    empty(("qT", t, f), qT[:, t, 4 * f:4 * f + 4, :],
                          bank("qT", t, f)[0:QK].rearrange("p (h n) -> p h n", h=4))
                else:
                    empty(("qT", t, f), qT_s[:, :, 4 * f:4 * f + 4, :].rearrange("p b h q -> p h b q"),
                          bank("qT", t, f)[0:QK].rearrange("p (h b q) -> p h b q", h=4, b=NB_DEC))
        for p in range(4):
            filled(a, "qabs", p)
            for hh in range(2):
                for ct in range(2):
                    o = (hh * 2 + ct) * P
                    empty(("qabs", p), qabs[:, ct, :, 2 * p + hh, :],
                          bank("qabs", p)[:, o:o + P].rearrange("p (b q) -> p b q", b=NB_DEC), last=(hh + ct == 2))
        for p in range(4):
            filled(a, "kT", p)
            empty(("kT", p), kT[0:NOPE, 2 * p:2 * p + 2, :], bank("kT", p)[0:NOPE].rearrange("p (h n) -> p h n", h=2))

        a.wait_ge(S["loaded_tables"], 16 * N_TABLES)

        def a_exp(i):
            kind, n, hh = items[i]
            a.wait_ge(S["maxed"], i + 1)
            if i >= 2:
                a.wait_ge(S["flipped"], i - 1)
            scale = MLA_SCALE if kind.startswith("mla") else SWA_SCALE
            nk = width(i)
            ins = nc.scalar.activation(probs[:, i % 2, 0:nk], scores(i)[:, 0:nk], ACT.Exp, bias=neg_max[:, i:i + 1],
                                       scale=scale, accum_out=row_sum[:, i:i + 1])
            if kind.startswith("swa"):
                col = sinks[:, hh:hh + 1] if kind == "swa" else sinks[:, H:H + 1]
                ins = nc.scalar.activation(sink_e[:, i:i + 1], col, ACT.Exp, bias=neg_max[:, i:i + 1])
            ins.then_inc(S["exped"], 1)

        def a_flip(i):
            kind, n, hh = items[i]
            a.wait_ge(S["flipped"], i + 1)
            if i >= 2:
                a.wait_ge(S["pv_done"], i - 1)
            full = full_tiles(i)
            tb = ps[:, 4:6, :].rearrange("p a b -> p (a b)")
            last = nc.scalar.copy(pT[:, i % 2, 0:full * P], tb[:, 0:full * P])
            if kind.endswith("_s"):
                last = nc.scalar.copy(pT[0:Q_DEC, i % 2, full * P:(full + 1) * P], tb[0:Q_DEC, full * P:(full + 1) * P])
            last.then_inc(S["pT_ready"], 1)

        def a_out(i):
            kind, n, hh = items[i]
            a.wait_ge(S["pv_done"], i + 1)
            ob = ps[:, 6, :]
            if kind in ("mla", "swa"):
                r = slice(64 * (hh % 2), 64 * (hh % 2) + 64)
                last = nc.scalar.copy(mixT[r, (4 if kind == "swa" else 0) + hh // 2, n * P:(n + 1) * P], ob[r, 0:P])
            elif kind == "mla_s":
                last = nc.scalar.copy(qabs[:, :, n, :, :].rearrange("p a h q -> p a (h q)"),
                                      ob[:, 0:2 * P].rearrange("p (a n) -> p a n", a=2))
            else:
                c0 = SEQ + n * Q_DEC
                last = nc.scalar.copy(mixT[:, 4:8, c0:c0 + Q_DEC], ob[:, 0:4 * Q_DEC].rearrange("p (a q) -> p a q", a=4))
            last.then_inc(S["o_ready"], 1)

        a_exp(0)
        for i in range(len(items)):
            if i + 1 < len(items):
                a_exp(i + 1)
            a_flip(i)
            if i >= 1:
                a_out(i - 1)
        a_out(len(items) - 1)
        filled(a, "oS")
        empty(("oS",), mixT[:, 0:4, SEQ:SEQ + P], bank("oS").rearrange("p (k n) -> p k n", k=4))
        square_out = hq[:, NT * OUT_COLS:NT * OUT_COLS + 3 * OUT_COLS]
        a.wait_ge(S["x1_ready"], 3 * NT)
        x_squares(square_out, slice(0, 3 * OUT_COLS), 36, NT)
        a.wait_ge(S["x1_ready"], 4 * NT)
        x_squares(square_out, slice(3 * OUT_COLS, D), 64, 2 * NT)
        x_root(36, 3)
        for t in range(NT):
            for g in range(2):
                filled(a, "fT", t, g)
                empty(("fT", t, g), hT[:, 4 * g:4 * g + 4, t * P:(t + 1) * P],
                      bank("fT", t, g).rearrange("p (k n) -> p k n", k=4))

        emptied(a, "fshift", 1, 1)
        for t in range(NT):
            nc.scalar.dma_start(h_rows[t * P:(t + 1) * P, :], h[:, t, :]).then_inc(S["h_stored"], 16)

        def round_unit(i, n):
            a.wait_ge(slot_sem[moe_slot(n)], moe_full(i, n))
            a.wait_ge(S["unit_used"], moe_used(i, n - SPLIT))
            nc.scalar.copy(piece(w_hi, n), piece_src(n)).then_inc(S["hi_ready"], 1)

        for n in range(SPLIT):
            round_unit(0, n)
        for t in range(NT):
            a.wait_ge(S["probs_top"], t + 1)
            nc.scalar.activation(gate_w[:, t, :], gate_w[:, t, :], ACT.Exp, bias=stat[:, 50 + t:51 + t],
                                 accum_out=stat[:, 53 + t:54 + t]).then_inc(S["gates_exped"], 1)

        nc.scalar.dma_start(gfin, g_final).then_inc(S["loaded_gfin"], 16)
        a.wait_ge(S["gates_exped"], NT)
        a.wait_ge(S["table_ready"], 1)

        def turned(sem_in, count, hi, raw, r, bk, sem_out):
            a.wait_ge(S[sem_in], count)
            src = t_bank[bk].rearrange("p (k n) -> p k n", k=4)
            nc.scalar.copy(hi[:, 3 * r:3 * r + 3, :], src[:, 0:3])
            nc.scalar.copy(raw[:, r, :], src[:, 3]).then_inc(S[sem_out], 1)

        turned("xT_filled", 1, xT_hi, xT_raw, 0, 1, "xT_hi_ready")
        turned("xT_filled", 2, xT_hi, xT_raw, 1, 1, "xT_hi_ready")

        def swish(i, f):
            a.wait_ge(S["glu_ready"], i * 2 + f + 1)
            nc.scalar.activation(sig[:, f, :], glu[:, f, :], ACT.Sigmoid, scale=1.702).then_inc(S["sig_done"], 1)

        def expert_block(i):
            for n in (4, 5, 6, 7):
                round_unit(i, n)
            swish(i, 0)
            for n in (8, 9):
                round_unit(i, n)
            turned("actT_filled", i * 2 + 1, aT_hi, aT_raw, 0, 0, "aT_hi_ready")
            round_unit(i, 10)
            swish(i, 1)
            round_unit(i, 11)
            turned("xT_filled", i * 2 + 3, xT_hi, xT_raw, 0, 1, "xT_hi_ready")
            turned("actT_filled", i * 2 + 2, aT_hi, aT_raw, 1, 0, "aT_hi_ready")
            for n in (0, 1, 2):
                round_unit(i + 1, n)
            turned("xT_filled", i * 2 + 4, xT_hi, xT_raw, 1, 1, "xT_hi_ready")
            round_unit(i + 1, 3)
            a.wait_ge(S["unit_used"], moe_used(i, MOE_UNITS - 1))
            a.wait_ge(S["y_stored"], i * 16 + 16)
            nc.scalar.copy(y_blk[:, :], ps[:, 4:6, :].rearrange("p a b -> p (a b)")).then_inc(S["y_copied"], 1)
            a.wait_ge(S["y_copied"], i + 2)
            nc.scalar.dma_start(y_rows[bass.ds(i * P, P), :], y_blk[:, :]).then_inc(S["y_stored"], 16)

        a.sem_inc(S["y_copied"], 1)
        a.sem_inc(S["y_stored"], 16)
        with a.Fori(0, NE) as i:
            expert_block(i)
        n_ovf = a.value_load(ovf_table[0:1, NOVF:NOVF + 1], min_val=0, max_val=NOVF)
        with a.If(n_ovf > 0):
            with a.Fori(NE, n_ovf + NE) as i:
                expert_block(i)
        a.wait_ge(S["y_copied"], n_ovf + (NE + 1))

        def first_term(t):
            rows = y_got[:, t * TOPK, :]
            a.wait_ge(got_sem[t * TOPK], 16)
            nc.scalar.activation(rows, rows, ACT.Copy, scale=gate_w[:, t, 0:1]).then_inc(S["first_term"], 1)

        first_term(0)
        first_term(1)
        for t in range(NT):
            a.wait_ge(S["x2_ready"], t + 1)
            nc.scalar.activation(glu[:, :, :].rearrange("p a b -> p (a b)"), x[:, t, :], ACT.Square, scale=float(D) ** -0.5,
                                 accum_out=stat[:, 56 + t:57 + t]).then_inc(S["fin_ss"], 1)
            if t + 2 < NT:
                first_term(t + 2)
            a.wait_ge(S["fin_ready"], 2 * t + 1)
            nc.scalar.activation(stat[:, 59 + t:60 + t], stat[:, 56 + t:57 + t], ACT.Sqrt).then_inc(S["fin_root"], 1)
            a.wait_ge(S["fin_ready"], 2 * t + 2)
            dst = o_yp[0, t * P:(t + 1) * P, :] if t < NP_T else o_ys.rearrange("b q d -> (b q) d")
            nc.scalar.dma_start(dst, x[:, t, :]).then_inc(S["fin_stored"], 16)
        a.wait_ge(S["fin_stored"], 16 * NT)

    @block.vector
    def _(v):
        steps = [0]

        def step(ins):
            steps[0] += 1
            ins.then_inc(S["v_step"], 1)
            v.wait_ge(S["v_step"], steps[0])

        csig = rtr[:, :, :].rearrange("p a b -> p (a b)")[:, 0:KT * 9]
        step(nc.vector.memset(mod_parts[:, :], 0.0))
        v.wait_ge(S["sig_ready"], 1)
        nc.vector.tensor_tensor(cs[:, :, :].rearrange("p k n -> p (k n)"), cT[:, :, :].rearrange("p k n -> p (k n)"),
                                csig, ALU.mult).then_inc(S["silu_ready"], 1)

        def rms_of_x(n0, ss, root, second=None):
            v.wait_ge(S["ss_ready"], ss)
            if second:
                step(nc.vector.tensor_tensor(stat[:, n0:n0 + 3], stat[:, n0:n0 + 3], stat[:, second:second + 3], ALU.add))
            nc.vector.tensor_scalar(stat[:, n0 + 6:n0 + 9], stat[:, n0:n0 + 3], 1.0 / D, EPS, ALU.mult, ALU.add).then_inc(
                S["ms_ready"], 1)
            v.wait_ge(S["root_ready"], root)
            step(nc.vector.reciprocal(stat[:, n0 + 9:n0 + 12], stat[:, n0 + 3:n0 + 6]))

        def mod_source(n):
            return early_rows[:, n] if n < EARLY_MOD else mod_rows if n < GATE_MOD else gate_rows[:, n - GATE_MOD]

        def mod_take(n, src, done):
            rows = mod_source(n)
            if n >= GATE_MOD:
                v.wait_ge(S["loaded_gate_rows"], 16)
            else:
                v.wait_ge(S["loaded_rows"], 16 if n < EARLY_MOD else 16 * (n - EARLY_MOD + 2))
            nc.vector.tensor_tensor(mod_row[:, :], src[0:9], rows[:, 0, :], ALU.add).then_inc(S[done], 1)
            v.wait_ge(S[done], ordinal[("mod", n)] if n < EARLY_MOD else n - EARLY_MOD + 1)

        def mod_split(n, parts=(0, 1, 2, 3)):
            cols = slice(n * 512, (n + 1) * 512)
            rows = mod_source(n)
            if 0 in parts and n // 2 in (1, 4):
                step(nc.vector.scalar_tensor_tensor(mod_row[:, :], mod_row[:, :], 1.0, rows[:, 1, :], ALU.add, ALU.mult))
            if 1 in parts:
                step(nc.vector.tensor_copy(mod_parts[0:9, cols], mod_row[:, :]))
                step(nc.vector.tensor_tensor(mod_res[:, :], mod_row[:, :], mod_parts[0:9, cols], ALU.subtract))
            if 2 in parts:
                step(nc.vector.tensor_copy(mod_p2[:, :], mod_res[:, :]))
                step(nc.vector.tensor_tensor(mod_res[:, :], mod_res[:, :], mod_p2[:, :], ALU.subtract))
            if 3 in parts:
                step(nc.vector.tensor_copy(mod_parts[32:41, cols], mod_p2[:, :]))
                nc.vector.tensor_copy(mod_parts[64:73, cols], mod_res[:, :]).then_inc(S["parts_ready"], 1)
                v.wait_ge(S["parts_ready"], n + 1)

        for n in range(4):
            filled(v, "mod", n)
            mod_take(n, bank("mod", n), "v_emptied")
            mod_split(n)
            if n == 1:
                rms_of_x(0, NT, 1)
        filled(v, "mod", 4)
        mod_take(4, bank("mod", 4), "v_emptied")

        def modulated(pre_, inv0):
            for k in range(2):
                tiles = (0, 1) if k == 0 else (2,)
                for f in range(2):
                    cols = slice(f * 512, (f + 1) * 512)
                    filled(v, pre_ + "scale", k, f)
                    for t in tiles:
                        last = nc.vector.scalar_tensor_tensor(h[:, t, cols], x[:, t, cols], stat[:, inv0 + t:inv0 + t + 1],
                                                              bank(pre_ + "scale", k, f), ALU.mult, ALU.mult)
                    last.then_inc(S["v_emptied"], 1)
                    v.wait_ge(S["v_emptied"], ordinal[(pre_ + "scale", k, f)])
                    filled(v, pre_ + "shift", k, f)
                    for t in tiles:
                        last = nc.vector.tensor_tensor(h[:, t, cols], h[:, t, cols], bank(pre_ + "shift", k, f), ALU.add)
                    last.then_inc(S["v_emptied"], 1)

        modulated("b", 9)
        mod_split(4)
        filled(v, "mod", 5)
        mod_take(5, bank("mod", 5), "v_emptied")
        mod_split(5)

        def rope_into(dst, x1, x2, cos, sin, tmp):
            nc.vector.tensor_tensor(tmp[0], x1, cos, ALU.mult)
            nc.vector.tensor_tensor(tmp[1], x2, sin, ALU.mult)
            nc.vector.tensor_tensor(tmp[2], x2, cos, ALU.mult)
            step(nc.vector.tensor_tensor(tmp[3], x1, sin, ALU.mult))
            nc.vector.tensor_tensor(dst[0], tmp[0], tmp[1], ALU.subtract)
            return nc.vector.tensor_tensor(dst[1], tmp[2], tmp[3], ALU.add)

        v.wait_ge(S["loaded_tables"], 16 * N_TABLES)
        step(nc.vector.tensor_scalar(sinks_s[:, :], sinks[:, :], 1.0 / SWA_SCALE, None, ALU.mult))
        v.wait_ge(S["u_stats"], 2 * NT)
        step(nc.vector.tensor_scalar(stat[:, 22:28], stat[:, 16:22], EPS, None, ALU.add))
        v.sem_inc(S["ms_ready"], 1)
        v.wait_ge(S["root_ready"], 2)
        step(nc.vector.reciprocal(stat[:, 34:36], stat[:, 28:30]))
        step(nc.vector.reciprocal(stat[:, 12:16], stat[:, 30:34]))
        q_inv = (stat[:, 34:35], stat[:, 35:36], stat[:, 12:13])
        for t in range(NT):
            last = nc.vector.scalar_tensor_tensor(u[:, t, 0:QL], u[:, t, 0:QL], q_inv[t], g_qkv[:, 0:QL], ALU.mult, ALU.mult)
        last.then_inc(S["ql_ready"], 1)
        for t in range(NT):
            nc.vector.scalar_tensor_tensor(u[:, t, O_KV:O_KPE], u[:, t, O_KV:O_KPE], stat[:, 13 + t:14 + t],
                                           g_qkv[:, QL:QL + KVL], ALU.mult, ALU.mult)
        half = ROPE // 2
        tmp = [rt[:, n, 0:NT * half].rearrange("p (t d) -> p t d", t=NT) for n in range(4)]
        rope_into((u[:, :, O_KPE:O_KPE + half], u[:, :, O_KPE + half:O_QS]), u[:, :, O_KPE:O_KPE + half],
                  u[:, :, O_KPE + half:O_QS], rope[:, :, 0:half], rope[:, :, half:ROPE], tmp).then_inc(S["ck_ready"], 1)
        emptied(v, "u", 5, NT - 1)
        nc.vector.tensor_copy(v_swa[:, :, :], u[:, :, O_VS:IN_W]).then_inc(S["v_swa_ready"], 1)
        emptied(v, "ckT", NT - 1)
        nc.vector.tensor_copy(kT[NOPE:QK, :, :], kpT[NOPE:QK, 0:SEQ].unsqueeze(1).to_broadcast([ROPE, H, SEQ])).then_inc(
            S["k_rope_ready"], 1)

        for t in range(NT):
            for f in range(2):
                filled(v, "q", t, f)
                if t:
                    filled(v, "qT", t - 1, f)
                src = bank("q", t, f)[:, 0:4 * QK].rearrange("p (h d) -> p h d", h=4)
                hs = slice(4 * f, 4 * f + 4)
                cos = rope[:, t:t + 1, 0:half].to_broadcast([P, 4, half])
                sin = rope[:, t:t + 1, half:ROPE].to_broadcast([P, 4, half])
                nc.vector.tensor_copy(q_tok[:, hs, 0:NOPE], src[:, :, 0:NOPE])
                tmp = [rt[:, n, 0:4 * half].rearrange("p (t d) -> p t d", t=4) for n in range(4)]
                rope_into((q_tok[:, hs, NOPE:NOPE + half], q_tok[:, hs, NOPE + half:QK]),
                          src[:, :, NOPE:NOPE + half], src[:, :, NOPE + half:QK], cos, sin, tmp).then_inc(S["v_emptied"], 1)
                emptied(v, "q", t, f)

        mod_next = [EARLY_MOD]

        def v_max(i):
            kind, n, hh = items[i]
            s, nk = scores(i), width(i)
            v.wait_ge(S["scored"], i + 1)
            if kind == "mla":
                step(nc.vector.tensor_tensor(s[:, 0:nk], s[:, 0:nk], causal[:, n, 0:nk], ALU.add))
            elif kind == "swa":
                slope = 2.0 ** (-8.0 * (hh + 1) / H)
                step(nc.vector.scalar_tensor_tensor(s[:, 0:nk], dist[:, n, 0:nk], -slope / SWA_SCALE, s[:, 0:nk],
                                                    ALU.mult, ALU.add))
            elif kind == "swa_s":
                step(nc.vector.tensor_tensor(s[:, 0:nk], s[:, 0:nk], alibi[:, 0:nk], ALU.add))
            step(nc.vector.tensor_reduce(row_max[:, i:i + 1], s[:, 0:nk], AX, ALU.max))
            if kind.startswith("swa"):
                col = sinks_s[:, hh:hh + 1] if kind == "swa" else sinks_s[:, H:H + 1]
                nc.vector.tensor_scalar(neg_max[:, i:i + 1], row_max[:, i:i + 1], col, -SWA_SCALE, ALU.max,
                                        ALU.mult).then_inc(S["maxed"], 1)
            else:
                nc.vector.tensor_scalar(neg_max[:, i:i + 1], row_max[:, i:i + 1], -MLA_SCALE, None, ALU.mult).then_inc(
                    S["maxed"], 1)

        def v_norm(i):
            kind, n, hh = items[i]
            v.wait_ge(S["exped"], i + 1)
            if kind.startswith("swa"):
                step(nc.vector.tensor_tensor(row_sum[:, i:i + 1], row_sum[:, i:i + 1], sink_e[:, i:i + 1], ALU.add))
            step(nc.vector.reciprocal(row_inv[:, i:i + 1], row_sum[:, i:i + 1]))
            nk = width(i)
            nc.vector.tensor_scalar(probs[:, i % 2, 0:nk], probs[:, i % 2, 0:nk], row_inv[:, i:i + 1], None,
                                    ALU.mult).then_inc(S["normed"], 1)

        v_max(0)
        for i in range(len(items)):
            if i + 1 < len(items):
                v_max(i + 1)
            v_norm(i)
            c = i // 6 - 1
            if 0 <= c < GATE_MOD - EARLY_MOD:
                if i % 6 == 0:
                    v.wait_ge(S["mod_extra"], c + 1)
                    mod_take(EARLY_MOD + c, ps[:, 7, :], "mod_extra_used")
                elif i % 6 <= 4:
                    mod_split(EARLY_MOD + c, (i % 6 - 1, ))

        for j in range(4):
            cols = slice(j * OUT_COLS, (j + 1) * OUT_COLS)
            for t in range(NT):
                filled(v, "o", j, t)
                emptied(v, "gate", 1, 1)
                if j:
                    v.wait_ge(S["x1_ready"], NT * (j - 1) + t + 1)
                tmp = hq[:, (t % 3) * OUT_COLS:(t % 3 + 1) * OUT_COLS]
                nc.vector.tensor_tensor(tmp, bank("o", j, t)[:, 0:OUT_COLS], gates[:, t // 2, cols], ALU.mult).then_inc(
                    S["v_emptied"], 1)
                v.wait_ge(S["v_emptied"], ordinal[("o", j, t)])
                nc.vector.tensor_tensor(x[:, t, cols], x[:, t, cols], tmp, ALU.add).then_inc(S["x1_ready"], 1)
        rms_of_x(36, 3 * NT, 3, second=64)
        modulated("f", 45)

        def remainder(i, n):
            v.wait_ge(S["hi_ready"], i * MOE_UNITS + (n + 1))
            nc.vector.tensor_tensor(piece(w_lo, n), piece_src(n), piece(w_hi, n).bitcast(F32), ALU.subtract).then_inc(
                S["lo_ready"], 1)

        v.sem_inc(S["lo_ready"], SLOTS)

        v.wait_ge(S["v_emptied"], ordinal[("fshift", 1, 1)])
        top = rtr[:, 0, :]
        idx_u = rtr[:, 1, 0:24].bitcast(U32)
        idx_f = rtr[:, 2, 0:12]
        logit = rtr[:, 4:7, :]
        for t in range(NT):
            filled(v, "logit", t)
            nc.vector.tensor_tensor(logit[:, t, :], bank("logit", t)[:, 0:NE], b_rt[:, :], ALU.add).then_inc(S["v_emptied"], 1)
            v.wait_ge(S["v_emptied"], ordinal[("logit", t)])
            step(nc.vector.max(top[:, 8 * t:8 * t + 8], logit[:, t, :]))
            nc.vector.max_index(idx_u[:, 8 * t:8 * t + 8], top[:, 8 * t:8 * t + 8], logit[:, t, :])
            nc.vector.tensor_scalar(stat[:, 50 + t:51 + t], top[:, 8 * t:8 * t + 1], -1.0, None, ALU.mult)
            nc.vector.tensor_copy(gate_w[:, t, :], top[:, 8 * t:8 * t + TOPK]).then_inc(S["probs_top"], 1)
            if t < NT - 1:
                remainder(0, t)
        v.wait_ge(S["probs_top"], NT)
        step(nc.vector.tensor_copy(idx_f.rearrange("p (t k) -> p t k", t=NT),
                                   idx_u.rearrange("p (t k) -> p t k", t=NT)[:, :, 0:TOPK]))
        hot = route_hot[:, :, :]
        prod = route_prod[:, :, :]
        fld = [route_fld[:, n] for n in range(7)]
        step(nc.vector.tensor_tensor(hot, expert_id[:, :].unsqueeze(1).to_broadcast([P, NT * TOPK, NE]),
                                     idx_f.unsqueeze(2).to_broadcast([P, NT * TOPK, NE]), ALU.is_equal))
        step(nc.vector.tensor_reduce(fld[0], hot.rearrange("p (t k) e -> p t e k", t=NT), AX, ALU.add))
        nc.vector.tensor_copy(chosen[:, :, :], fld[0]).then_inc(S["logits_exp"], 1)
        rank, big1, big2, blk, pos, f1, f2 = fld
        for t in range(NT):
            filled(v, "rank", t)
            nc.vector.tensor_copy(rank[:, t, :], bank("rank", t)[:, 0:NE]).then_inc(S["v_emptied"], 1)
        filled(v, "count")
        cnt = rtr[:, 7, :]
        nc.vector.tensor_copy(cnt, bank("count")[:, 0:NE]).then_inc(S["v_emptied"], 1)
        v.wait_ge(S["v_emptied"], ordinal[("count",)])
        cum, alt = rtr[:, 8, :], rtr[:, 9, :]
        step(nc.vector.tensor_scalar(alt, cnt, 2.0 * P, None, ALU.is_gt))
        step(nc.vector.scalar_tensor_tensor(cum, cnt, 1.0 * P, alt, ALU.is_gt, ALU.add))
        n_own = rtr[:, 10, :]
        step(nc.vector.tensor_copy(n_own, cum))
        d = 1
        while d < NE:
            nc.vector.tensor_copy(alt[:, 0:d], cum[:, 0:d])
            step(nc.vector.tensor_tensor(alt[:, d:NE], cum[:, d:NE], cum[:, 0:NE - d], ALU.add))
            cum, alt, d = alt, cum, 2 * d
        ovf = prod.rearrange("p n e -> p (n e)")[:, 0:NOVF * NE].rearrange("p (n e) -> p n e", e=NE)
        step(nc.vector.tensor_tensor(ovf, cum.unsqueeze(1).to_broadcast([P, NOVF, NE]), block_id[:, :, :], ALU.is_le))
        nc.vector.memset(block_expert[:, NBLK - 1:NBLK], 0.0)
        nc.vector.tensor_copy(block_expert[:, 0:NE], expert_id[:, :])
        step(nc.vector.tensor_reduce(block_expert[:, NE:NE + NOVF], ovf, AX, ALU.add))
        nc.vector.tensor_copy(ovf_table[0:1, 0:NOVF], block_expert[0:1, NE:NE + NOVF])
        nc.vector.tensor_copy(ovf_table[0:1, NOVF:NOVF + 1], cum[0:1, NE - 1:NE]).then_inc(S["table_ready"], 1)
        first = alt
        step(nc.vector.tensor_tensor(first, cum, n_own, ALU.subtract))
        step(nc.vector.tensor_scalar(first, first, float(NE), None, ALU.add))
        step(nc.vector.tensor_tensor(first, first, expert_id[:, :], ALU.subtract))
        first3 = first.unsqueeze(1).to_broadcast([P, NT, NE])
        eid3 = expert_id[:, :].unsqueeze(1).to_broadcast([P, NT, NE])
        nc.vector.tensor_scalar(big1, rank, float(P), None, ALU.is_ge)
        step(nc.vector.tensor_scalar(big2, rank, 2.0 * P, None, ALU.is_ge))
        step(nc.vector.tensor_tensor(blk, big1, first3, ALU.mult))
        step(nc.vector.tensor_tensor(blk, blk, eid3, ALU.add))
        step(nc.vector.tensor_tensor(blk, blk, big2, ALU.add))
        step(nc.vector.tensor_tensor(big1, big1, big2, ALU.add))
        step(nc.vector.scalar_tensor_tensor(pos, big1, -float(P), rank, ALU.mult, ALU.add))
        blk_of, pos_of = rtr[:, 11, 0:NT * TOPK], rtr[:, 11, NT * TOPK:2 * NT * TOPK]
        for fsrc, dst in ((pos, pos_of), (blk, blk_of)):
            for t in range(NT):
                last = nc.vector.tensor_tensor(prod[:, t * TOPK:(t + 1) * TOPK, :], hot[:, t * TOPK:(t + 1) * TOPK, :],
                                               fsrc[:, t:t + 1, :].to_broadcast([P, TOPK, NE]), ALU.mult)
            step(last)
            step(nc.vector.tensor_reduce(dst, prod, AX, ALU.add))
        nc.vector.tensor_tensor(place[:, :, :], slot_id[:, :].unsqueeze(1).to_broadcast([P, NT * TOPK, P]),
                                pos_of.unsqueeze(2).to_broadcast([P, NT * TOPK, P]), ALU.is_equal)
        step(nc.vector.tensor_tensor(where[:, :, :], slot_id[:, 0:NBLK].unsqueeze(1).to_broadcast([P, NT * TOPK, NBLK]),
                                     blk_of.unsqueeze(2).to_broadcast([P, NT * TOPK, NBLK]), ALU.is_equal))
        for t in range(NT):
            ks = slice(t * TOPK, (t + 1) * TOPK)
            last = nc.vector.tensor_scalar(where[:, ks, :], where[:, ks, :].bitcast(F32), token_id[:, t:t + 1], None, ALU.mult)
        last.then_inc(S["placed"], 1)
        step(nc.vector.scalar_tensor_tensor(pos_of, blk_of, float(P), pos_of, ALU.mult, ALU.add))
        step(nc.vector.tensor_copy(y_row_idx[:, :], pos_of))
        remainder(0, 2)
        filled(v, "table")
        nc.vector.tensor_copy(slot_tok[:, :], bank("table")[:, 0:NBLK]).then_inc(S["v_emptied"], 1)
        remainder(0, 3)
        v.wait_ge(S["gates_exped"], NT)
        step(nc.vector.reciprocal(stat[:, 50:53], stat[:, 53:56]))
        for t in range(NT):
            last = nc.vector.tensor_scalar(gate_w[:, t, :], gate_w[:, t, :], stat[:, 50 + t:51 + t], None, ALU.mult)
        step(last)
        nc.vector.tensor_scalar(sel_e[:, :], row_expert[:, :], block_expert[0:96, 0:1], None, ALU.is_equal).then_inc(
            S["sel_ready"], 1)

        def turned(v_hi, src_hi, dst, r, bk, sem_in, sem_out):
            v.wait_ge(S[sem_in], v_hi)
            nc.vector.tensor_tensor(dst[:, 3 * r:3 * r + 3, :], t_bank[bk].rearrange("p (k n) -> p k n", k=4)[:, 0:3],
                                    src_hi[:, 3 * r:3 * r + 3, :].bitcast(F32), ALU.subtract).then_inc(S[sem_out], 1)

        def gate_chunk(c):
            n = GATE_MOD + c
            v.wait_ge(S["mod_extra"], n - EARLY_MOD + 1)
            mod_take(n, bank("logit", c), "mod_extra_used")
            mod_split(n)

        v.sem_inc(S["gu_emptied"], 2)
        v.sem_inc(S["act_ready"], 2)
        gate_chunk(0)
        turned(1, xT_hi, xT_lo, 0, 1, "xT_hi_ready", "xT_ready")
        turned(2, xT_hi, xT_lo, 1, 1, "xT_hi_ready", "xT_ready")
        gate_chunk(1)

        def clamp(i, f):
            v.wait_ge(S["unit_used"], moe_used(i, 4 * f + 3))
            if f == 0:
                v.wait_ge(S["act_ready"], i * 2 + 2)
            nc.vector.tensor_scalar(glu[:, f, :], ps[:, 2 * f, :], 7.0, None, ALU.min).then_inc(S["glu_ready"], 1)
            nc.vector.tensor_scalar(lin[:, f, :], ps[:, 2 * f + 1, :], -7.0, 7.0, ALU.max, ALU.min).then_inc(
                S["gu_emptied"], 1)

        def swiglu(i, f):
            v.wait_ge(S["sig_done"], i * 2 + f + 1)
            nc.vector.tensor_tensor(sig[:, f, :], glu[:, f, :], sig[:, f, :], ALU.mult).then_inc(S["gsg_ready"], 1)
            v.wait_ge(S["gu_emptied"], i * 2 + f + 3)
            v.wait_ge(S["gsg_ready"], i * 2 + f + 1)
            nc.vector.scalar_tensor_tensor(lin[:, f, :], lin[:, f, :], 1.0, sig[:, f, :], ALU.add, ALU.mult).then_inc(
                S["act_ready"], 1)

        def expert_block(i):
            for n in (4, 5, 6):
                remainder(i, n)
            clamp(i, 0)
            remainder(i, 7)
            swiglu(i, 0)
            for n in (8, 9):
                remainder(i, n)
            turned(i * 2 + 1, aT_hi, aT_lo, 0, 0, "aT_hi_ready", "actT_ready")
            remainder(i, 10)
            clamp(i, 1)
            swiglu(i, 1)
            remainder(i, 11)
            v.wait_ge(S["bias_done"], i + 1)
            v.wait_ge(S["sel_ready"], i + 1)
            nc.vector.tensor_scalar(sel_e[:, :], row_expert[:, :], block_expert[0:96, bass.ds(i + 1, 1)], None,
                                    ALU.is_equal).then_inc(S["sel_ready"], 1)
            turned(i * 2 + 3, xT_hi, xT_lo, 0, 1, "xT_hi_ready", "xT_ready")
            turned(i * 2 + 2, aT_hi, aT_lo, 1, 0, "aT_hi_ready", "actT_ready")
            for n in (0, 1, 2):
                remainder(i + 1, n)
            turned(i * 2 + 4, xT_hi, xT_lo, 1, 1, "xT_hi_ready", "xT_ready")
            remainder(i + 1, 3)

        with v.Fori(0, NE) as i:
            expert_block(i)
        n_ovf = v.value_load(ovf_table[0:1, NOVF:NOVF + 1], min_val=0, max_val=NOVF)
        with v.If(n_ovf > 0):
            with v.Fori(NE, n_ovf + NE) as i:
                expert_block(i)

        def combine(t):
            y_acc = y_got[:, t * TOPK, :]
            v.wait_ge(S["first_term"], t + 1)
            for k in range(1, TOPK):
                v.wait_ge(got_sem[t * TOPK + k], 16)
                step(nc.vector.scalar_tensor_tensor(y_acc, y_got[:, t * TOPK + k, :], gate_w[:, t, k:k + 1], y_acc,
                                                    ALU.mult, ALU.add))
            if t == 0:
                v.wait_ge(S["gates_filled"], 1)
            k = 2 * (t // 2)
            step(nc.vector.tensor_tensor(y_acc, y_acc, ps[:, k:k + 2, :].rearrange("p a b -> p (a b)"), ALU.mult))
            nc.vector.tensor_tensor(x[:, t, :], x[:, t, :], y_acc, ALU.add).then_inc(S["x2_ready"], 1)

        def final_norm(t):
            v.wait_ge(S["x2_ready"], t + 1)
            v.wait_ge(S["fin_root"], t + 1)
            step(nc.vector.reciprocal(stat[:, 48:49], stat[:, 59 + t:60 + t]))
            nc.vector.scalar_tensor_tensor(x[:, t, :], x[:, t, :], stat[:, 48:49], gfin, ALU.mult, ALU.mult).then_inc(
                S["fin_ready"], 1)

        def add_eps(t):
            v.wait_ge(S["fin_ss"], t + 1)
            nc.vector.tensor_scalar(stat[:, 56 + t:57 + t], stat[:, 56 + t:57 + t], EPS, None, ALU.add).then_inc(
                S["fin_ready"], 1)

        v.wait_ge(S["loaded_gfin"], 16)
        combine(0)
        for t in range(NT):
            if t + 1 < NT:
                combine(t + 1)
            add_eps(t)
            final_norm(t)

    @block.tensor
    def _(pe):
        def open_job(*key):
            n = number[key]
            first = 0 if n < len(early) else len(early)
            if n - 8 >= first:
                emptied(pe, *jobs[n - 8][0])
            return bank(*key)

        def close(ins):
            ins.then_inc(S["psum_filled"], 1)

        def mod_products(n, out, done):
            for f in range(2):
                unit_here(pe, ("ada", n, f))
                w = unit(("ada", n, f)).rearrange("p (k n) -> p k n", k=4)
                for k in range(4):
                    kt = 4 * f + k
                    ins = nc.tensor.matmul(out[0:9], cs[:, kt, :], w[:, k, :], start=(kt == 0), stop=(kt == KT - 1))
                ins.then_inc(S["unit_used"] if f == 0 else S[done], 1)

        def spread(key, chunk, k):
            out = open_job(*key)
            close(nc.tensor.matmul(out, kind_sel[:, k, :], mod_parts[:, chunk * 512:(chunk + 1) * 512], start=True, stop=True))

        def turn(out, src, n_rows=P):
            return nc.tensor.transpose(out, src, ident[0:n_rows, 0:n_rows])

        pe.sem_inc(S["raw_used"], SLOTS // 2)
        pe.wait_ge(S["silu_ready"], 1)
        for n in range(5):
            mod_products(n, open_job("mod", n), "psum_filled")
        pe.wait_ge(S["parts_ready"], 4)
        pe.wait_ge(S["consts_cast"], 2)
        for k in range(2):
            for f in range(2):
                spread(("bscale", k, f), 2 + f, k)
                spread(("bshift", k, f), f, k)
        mod_products(5, open_job("mod", 5), "psum_filled")
        pe.wait_ge(S["loaded_small"], 16 * 3)
        for t in range(NT):
            for g in range(2):
                emptied(pe, "bshift", t // 2, g)
                out = open_job("hT", t, g)
                for k in range(4):
                    kt = 4 * g + k
                    ins = turn(out[:, k * P:(k + 1) * P], h[:, t, kt * P:(kt + 1) * P])
                close(ins)
        emptied(pe, "hT", NT - 1, 1)
        for j in range(6):
            unit_here(pe, ("in", j))
            w = unit(("in", j))[:, 0:KT * IN_COLS].rearrange("p (k n) -> p k n", k=KT)
            for t in range(NT):
                out = open_job("u", j, t)
                for kt in range(KT):
                    ins = nc.tensor.matmul(out[:, 0:IN_COLS], hT[:, kt, t * P:(t + 1) * P], w[:, kt, :],
                                           start=(kt == 0), stop=(kt == KT - 1))
                close(ins)
        pe.wait_ge(S["ql_ready"], 1)
        for t in range(NT):
            out = open_job("qlT", t)
            for k in range(3):
                ins = turn(out[:, k * P:(k + 1) * P], u[:, t, k * P:(k + 1) * P])
            close(ins)
        pe.wait_ge(S["ck_ready"], 1)
        for t in range(NT):
            out = open_job("ckT", t)
            for k in range(2):
                turn(out[:, k * P:(k + 1) * P], u[:, t, O_KV + k * P:O_KV + (k + 1) * P])
            close(turn(out[0:ROPE, 2 * P:3 * P], u[:, t, O_KPE:O_QS]))
        emptied(pe, "u", 5, NT - 1)
        for t in range(NT):
            out = open_job("qsT", t)
            qs = u[:, t, O_QS:O_KS].rearrange("p (g n) -> p g n", g=GRP)
            for g in range(GRP):
                ins = turn(out[:, g * P:(g + 1) * P], qs[:, g])
            close(ins)
        out = open_job("ksT")
        for t in range(NT):
            ins = turn(out[:, t * P:(t + 1) * P], u[:, t, O_KS:O_VS])
        close(ins)
        pe.wait_ge(S["parts_ready"], EARLY_MOD)
        for k in range(2):
            for f in range(2):
                spread(("gate", k, f), 4 + f, k)
        emptied(pe, "ckT", NT - 1)
        pe.wait_ge(S["loaded_tables"], 16 * N_TABLES)
        for t in range(NP_T):
            out = open_job("v", t)
            for ct in range(2):
                ins = nc.tensor.matmul(out, ckT[:, ct, t * P:(t + 1) * P], w_ukv[:, ct, :, NOPE:NOPE + VD],
                                       start=(ct == 0), stop=(ct == 1))
            close(ins)
        pe.wait_ge(S["loaded_uq"], 16)
        emptied(pe, "qlT", NT - 1)

        def q_products(t, f):
            out = open_job("q", t, f)
            for k in range(3):
                ins = nc.tensor.matmul(out[:, 0:4 * QK], qlT[:, k, t * P:(t + 1) * P], w_uq[:, k, f * 4 * QK:(f + 1) * 4 * QK],
                                       start=(k == 0), stop=(k == 2))
            close(ins)

        def q_turn(t, f):
            emptied(pe, "q", t, f)
            out = open_job("qT", t, f)
            for hh in range(4):
                ins = turn(out[0:QK, hh * P:(hh + 1) * P], q_tok[:, 4 * f + hh, :])
            close(ins)

        for w, t in QUERY_ORDER:
            for f in range(2):
                (q_products if w == "q" else q_turn)(t, f)
        emptied(pe, "qT", NT - 1, 1)

        for p in range(4):
            out = open_job("qabs", p)
            for hh in range(2):
                for ct in range(2):
                    ins = nc.tensor.matmul(out[:, (hh * 2 + ct) * P:(hh * 2 + ct + 1) * P],
                                           wukT[:, 2 * p + hh, ct * P:(ct + 1) * P], qT_s[0:NOPE, :, 2 * p + hh, :],
                                           start=True, stop=True)
            close(ins)
        for p in range(4):
            out = open_job("kT", p)
            for hh in range(2):
                for ct in range(2):
                    ins = nc.tensor.matmul(out[0:NOPE, hh * SEQ:(hh + 1) * SEQ], w_ukv[:, ct, 2 * p + hh, 0:NOPE],
                                           ckT[:, ct, 0:SEQ], start=(ct == 0), stop=(ct == 1))
            close(ins)

        pe.wait_ge(S["k_rope_ready"], 1)
        pe.wait_ge(S["v_emptied"], n_early["v"])
        pe.wait_ge(S["a_emptied"], n_early["a"])

        def score(i):
            kind, n, hh = items[i]
            s = scores(i)
            if i >= 3:
                pe.wait_ge(S["exped"], i - 2)
            if kind == "mla":
                ins = nc.tensor.matmul(s[:, 0:width(i)], qT[:, n, hh, :], kT[:, hh, 0:width(i)], start=True, stop=True)
            elif kind == "swa":
                r = slice(64 * (hh // GRP), 64 * (hh // GRP) + 64)
                ins = nc.tensor.matmul(s[:, 0:width(i)], qsT[r, n, hh % GRP, :], ksT[r, 0:width(i)], start=True, stop=True)
            elif kind == "mla_s":
                k = n % 2
                pe.wait_ge(cache_sem[k], 16 * 7 * (n // 2 + 1))
                own = slice(SEQ + n * Q_DEC, SEQ + (n + 1) * Q_DEC)
                for c0, n_c, keys in ((0, PAST, [latT[:, k, 0, :], latT[:, k, 1, :], krT[NOPE:QK, k, :]]),
                                      (PAST, Q_DEC, [ckT[:, 0, own], ckT[:, 1, own], kpT[NOPE:QK, own]])):
                    for ct in range(2):
                        nc.tensor.matmul(s[:, c0:c0 + n_c], qabs[:, ct, n, :, :].rearrange("p h q -> p (h q)"), keys[ct],
                                         start=(ct == 0), stop=False)
                    ins = nc.tensor.matmul(s[:, c0:c0 + n_c], qT_s[NOPE:QK, n].rearrange("p h q -> p (h q)"), keys[2], start=False, stop=True)
            else:
                k = n % 2
                own = slice(SEQ + n * Q_DEC, SEQ + (n + 1) * Q_DEC)
                for kv in range(KVH):
                    r = slice(64 * kv, 64 * kv + 64)
                    q = qsT_s[r, n].rearrange("p g q -> p (g q)")
                    nc.tensor.matmul(s[r, 0:WINDOW], q, ck_sT[r, k, :], start=True, stop=True)
                    ins = nc.tensor.matmul(s[r, WINDOW:WINDOW + Q_DEC], q, ksT[r, own], start=True, stop=True)
            ins.then_inc(S["scored"], 1)

        def flip(i):
            kind, n, hh = items[i]
            pe.wait_ge(S["normed"], i + 1)
            if i >= 1:
                pe.wait_ge(S["pT_ready"], i)
            tb = ps[:, 4:6, :].rearrange("p a b -> p (a b)")
            full = full_tiles(i)
            for k in range(full):
                ins = turn(tb[:, k * P:(k + 1) * P], probs[:, i % 2, k * P:(k + 1) * P])
            if kind.endswith("_s"):
                ins = turn(tb[0:Q_DEC, full * P:(full + 1) * P], probs[:, i % 2, full * P:full * P + Q_DEC])
            ins.then_inc(S["flipped"], 1)

        def mod_part(c, place):
            if place not in MOD_PLACES:
                return
            if c and place == MOD_PLACES[0]:
                pe.wait_ge(S["mod_extra_used"], c)
            for kt in (2 * MOD_PLACES.index(place), 2 * MOD_PLACES.index(place) + 1):
                f, k = kt // 4, kt % 4
                if k == 0:
                    unit_here(pe, ("ada", EARLY_MOD + c, f))
                w = unit(("ada", EARLY_MOD + c, f)).rearrange("p (k n) -> p k n", k=4)
                ins = nc.tensor.matmul(ps[0:9, 7, :], cs[:, kt, :], w[:, k, :], start=(kt == 0), stop=(kt == KT - 1))
                if k == 3:
                    ins.then_inc(S["unit_used"] if f == 0 else S["mod_extra"], 1)

        def weigh(i):
            kind, n, hh = items[i]
            pe.wait_ge(S["pT_ready"], i + 1)
            if i >= 1:
                pe.wait_ge(S["o_ready"], i)
            ob, full, pt = ps[:, 6, :], full_tiles(i), pT[:, i % 2, :]
            if kind in ("mla", "swa"):
                r = slice(64 * (hh % 2), 64 * (hh % 2) + 64)
                for k in range(full):
                    vals = v_p[:, k, hh * VD:(hh + 1) * VD] if kind == "mla" else \
                        v_swa[:, k, (hh // GRP) * HD:(hh // GRP + 1) * HD]
                    ins = nc.tensor.matmul(ob[r, 0:P], vals, pt[:, k * P:(k + 1) * P], start=(k == 0), stop=(k == full - 1))
            elif kind == "mla_s":
                for ct in range(2):
                    c = slice(ct * P, (ct + 1) * P)
                    for k in range(full):
                        nc.tensor.matmul(ob[:, c], lat[:, n % 2, k, c], pt[:, k * P:(k + 1) * P], start=(k == 0), stop=False)
                    ins = nc.tensor.matmul(ob[:, c], new_lat[:, n % 2, c], pt[0:Q_DEC, full * P:(full + 1) * P],
                                           start=False, stop=True)
            else:
                for kv in range(KVH):
                    for par in range(2):
                        o = ob[64 * par:64 * par + 64, kv * 2 * Q_DEC:(kv + 1) * 2 * Q_DEC]
                        vals = slice(kv * HD, (kv + 1) * HD)
                        for k, rows in ((0, P), (1, Q_DEC)):
                            cols = pt[0:rows, k * P:(k + 1) * P].rearrange("p (k g a q) -> p k g a q", k=KVH, g=2, a=2)
                            src = cv_s[:, n % 2, vals] if k == 0 else new_v[:, n % 2, vals]
                            ins = nc.tensor.matmul(o, src, cols[:, kv, :, par, :], start=(k == 0), stop=(k == 1))
            ins.then_inc(S["pv_done"], 1)

        score(0)
        score(1)
        for i in range(len(items)):
            if i + 2 < len(items):
                score(i + 2)
            flip(i)
            if i // 6 < GATE_MOD - EARLY_MOD:
                mod_part(i // 6, i % 6)
            if i >= 1:
                weigh(i - 1)
        weigh(len(items) - 1)

        pe.wait_ge(S["o_ready"], len(items))
        pe.wait_ge(S["mod_extra_used"], GATE_MOD - EARLY_MOD)
        out = open_job("oS")
        for hh in range(H):
            r = slice(64 * (hh % 2), 64 * (hh % 2) + 64)
            for ct in range(2):
                ins = nc.tensor.matmul(out[r, (hh // 2) * P:(hh // 2 + 1) * P], w_ukv[:, ct, hh, NOPE:NOPE + VD],
                                       qabs[:, ct, :, hh, :], start=(ct == 0), stop=(ct == 1))
        close(ins)
        emptied(pe, "oS")
        for j in range(4):
            unit_here(pe, ("out", j))
            w = unit(("out", j)).rearrange("p (k n) -> p k n", k=KT)
            for t in range(NT):
                out = open_job("o", j, t)
                for kt in range(KT):
                    ins = nc.tensor.matmul(out[:, 0:OUT_COLS], mixT[:, kt, t * P:(t + 1) * P], w[:, kt, :],
                                           start=(kt == 0), stop=(kt == KT - 1))
                close(ins)
        pe.wait_ge(S["parts_ready"], GATE_MOD)
        for k in range(2):
            for f in range(2):
                spread(("fscale", k, f), 8 + f, k)
                spread(("fshift", k, f), 6 + f, k)
        for t in range(NT):
            for g in range(2):
                emptied(pe, "fshift", t // 2, g)
                out = open_job("fT", t, g)
                for k in range(4):
                    kt = 4 * g + k
                    ins = turn(out[:, k * P:(k + 1) * P], h[:, t, kt * P:(kt + 1) * P])
                close(ins)
        for t in range(NT):
            emptied(pe, "fT", t, 1)
            out = open_job("logit", t)
            for kt in range(KT):
                ins = nc.tensor.matmul(out[:, 0:NE], hT[:, kt, t * P:(t + 1) * P], w_rt[:, kt, :],
                                       start=(kt == 0), stop=(kt == KT - 1))
            close(ins)
        def gate_part(c, kts):
            out = bank("logit", c)
            n = GATE_MOD + c
            if kts[0] == 0:
                emptied(pe, "logit", c)
            for kt in kts:
                f, k = kt // 4, kt % 4
                if k == 0:
                    unit_here(pe, ("ada", n, f))
                w = unit(("ada", n, f)).rearrange("p (k n) -> p k n", k=4)
                ins = nc.tensor.matmul(out[0:9], cs[:, kt, :], w[:, k, :], start=(kt == 0), stop=(kt == KT - 1))
                if k == 3:
                    ins.then_inc(S["unit_used"] if f == 0 else S["mod_extra"], 1)

        gate_part(0, (0, 1))
        pe.wait_ge(S["logits_exp"], 1)
        for t in range(NT):
            out = open_job("rank", t)
            for s in range(t + 1):
                ins = nc.tensor.matmul(out[:, 0:NE], before[:, 1 if s < t else 0, :], chosen[:, s, :], start=(s == 0),
                                       stop=(s == t))
            close(ins)
        out = open_job("count")
        for s in range(NT):
            ins = nc.tensor.matmul(out[:, 0:NE], before[:, 1, :], chosen[:, s, :], start=(s == 0), stop=(s == NT - 1))
        close(ins)
        gate_part(0, range(2, KT))
        gate_part(1, range(0, 4))
        pe.wait_ge(S["placed"], 1)
        out = open_job("table")
        for n in range(NT * TOPK):
            ins = nc.tensor.matmul(out[:, 0:NBLK], place[:, n, :], where[:, n, :], start=(n == 0), stop=(n == NT * TOPK - 1))
        close(ins)

        gate_part(1, range(4, KT))
        pe.wait_ge(S["mod_extra_used"], GATE_MOD - EARLY_MOD + 1)
        pe.wait_ge(S["v_emptied"], n_all["v"])
        pe.wait_ge(S["a_emptied"], n_all["a"])
        pe.wait_ge(S["bias_ready"], 1)
        def turn_x(r, bk):
            for k in range(4):
                kt = 4 * r + k
                ins = turn(t_bank[bk][:, k * P:(k + 1) * P], x_slots[:, kt * P:(kt + 1) * P])
            ins.then_inc(S["xT_filled"], 1)

        pe.wait_ge(S["gathered"], 16)
        turn_x(0, 1)
        pe.wait_ge(S["xT_ready"], 1)
        turn_x(1, 1)

        def products(i, n, banks, hi, lo, raw, last):
            pe.wait_ge(S["lo_ready"], i * MOE_UNITS + (SLOTS + n + 1))
            order = (0, 1) if PIECE_N[n % 4] == 2 else (1, 0)
            for k in order:
                if k < PIECE_N[n % 4]:
                    own, w = PIECE_AT[n % 4] + k, PIECE_AT[n % 4] + k
                    passes = ((hi[:, own, :], w_hi[:, w, :]), (hi[:, own, :], w_lo[:, w, :]), (lo[:, own, :], w_hi[:, w, :]))
                else:
                    passes = ((raw[:, n % 4 // 2, :], ring[:, moe_slot(n), UNIT // 2:UNIT]), )
                for q, (x_part, w_part) in enumerate(passes):
                    for s in range(2):
                        ins = nc.tensor.matmul(banks[s], x_part, w_part[:, s * 512:(s + 1) * 512], start=False,
                                               stop=(last and k == order[1] and q == len(passes) - 1))
                if len(passes) == 1:
                    ins.then_inc(S["raw_used"], 1)
            ins.then_inc(S["unit_used"], 1)

        def expert_block(i):
            def turn_act(f):
                pe.wait_ge(S["act_ready"], i * 2 + f + 3)
                for k in range(4):
                    ins = turn(t_bank[0][:, k * P:(k + 1) * P], lin[:, f, k * P:(k + 1) * P])
                ins.then_inc(S["actT_filled"], 1)

            pe.wait_ge(S["sel_ready"], i + 1)
            for f in range(2):
                pe.wait_ge(S["gu_emptied"], i * 2 + f + 1)
                banks = [ps[:, 2 * f + s, :] for s in range(2)]
                for s in range(2):
                    nc.tensor.matmul(banks[s], sel_e[:, :], bias_parts[:, s * D + f * 512:s * D + (f + 1) * 512],
                                     start=True, stop=False)
                for j in range(4):
                    if f == 0 and j % 2 == 0:
                        pe.wait_ge(S["xT_ready"], i * 2 + j // 2 + 1)
                    products(i, 4 * f + j, banks, xT_hi, xT_lo, xT_raw, j == 3)
                    if (f, j) == (1, 1):
                        turn_act(0)

            banks = [ps[:, 4 + s, :] for s in range(2)]
            pe.wait_ge(S["y_copied"], i + 1)
            for s in range(2):
                ins = nc.tensor.matmul(banks[s], sel_e[:, :], bias_parts[:, 2 * D + s * 512:2 * D + (s + 1) * 512],
                                       start=True, stop=False)
            ins.then_inc(S["bias_done"], 1)
            pe.wait_ge(S["actT_ready"], i * 2 + 1)
            products(i, 8, banks, aT_hi, aT_lo, aT_raw, False)
            pe.wait_ge(S["gathered"], i * 16 + 32)
            turn_x(0, 1)
            turn_act(1)
            products(i, 9, banks, aT_hi, aT_lo, aT_raw, False)
            pe.wait_ge(S["actT_ready"], i * 2 + 2)
            products(i, 10, banks, aT_hi, aT_lo, aT_raw, False)
            pe.wait_ge(S["xT_ready"], i * 2 + 3)
            turn_x(1, 1)
            products(i, 11, banks, aT_hi, aT_lo, aT_raw, True)

        with pe.Fori(0, NE) as i:
            expert_block(i)
        pe.wait_ge(S["table_ready"], 1)
        n_ovf = pe.value_load(ovf_table[0:1, NOVF:NOVF + 1], min_val=0, max_val=NOVF)
        with pe.If(n_ovf > 0):
            with pe.Fori(NE, n_ovf + NE) as i:
                expert_block(i)

        pe.wait_ge(S["gu_emptied"], (n_ovf + NE) * 2 + 2)
        pe.wait_ge(S["parts_ready"], N_MOD)
        for k in range(2):
            for f in range(2):
                cols = slice((GATE_MOD + f) * 512, (GATE_MOD + f + 1) * 512)
                ins = nc.tensor.matmul(ps[:, 2 * k + f, :], kind_sel[:, k, :], mod_parts[:, cols], start=True, stop=True)
        ins.then_inc(S["gates_filled"], 1)

    stack.close()


def layouts(i):
    def c(a):
        return np.ascontiguousarray(a)

    def rows(a, n):
        return np.broadcast_to(a, (n,) + a.shape)

    k = shape_constants()
    x = np.concatenate([i["x_prompt"].reshape(NP_T, P, D), i["x_sample"].reshape(1, P, D)])
    cond = np.concatenate([i["c_prompt"], i["c_sample"]])
    ada = i["w_ada"][0].reshape(2, 4, P, N_MOD, 512).transpose(3, 0, 2, 1, 4)
    g2 = np.zeros((N_MOD, 512), np.float32)
    g2[2:4], g2[8:10] = i["g_attn_norm"][0].reshape(2, 512), i["g_ffn_norm"][0].reshape(2, 512)
    ada_rows = np.stack([i["b_ada"][0].reshape(N_MOD, 512), g2], axis=1)
    gu = i["w_gate_up"][0].reshape(NE, 4, 2, P, 2, 2, 512).transpose(0, 5, 1, 3, 2, 4, 6)
    dn = i["w_down"][0].reshape(NE, 4, 2, P, D).transpose(0, 1, 3, 2, 4)
    moe = np.concatenate([gu.reshape(NE, 8, P, UNIT), dn.reshape(NE, 4, P, UNIT)], axis=1)
    sk = i["swa_sinks"][0]
    w_in = i["w_in"][0]
    w_qs = w_in[:, O_QS:O_KS].reshape(D, KVH, GRP, HD).transpose(0, 2, 1, 3).reshape(D, H * HD)
    w_in = np.concatenate([w_in[:, :O_QS], w_qs, w_in[:, O_KS:]], axis=1)
    return {
        "x_in": c(x),
        "c_t": c(cond.T.reshape(KT, P, 9).transpose(1, 0, 2)),
        "cache_lat": c(i["cache_mla_latent"][0].reshape(NB_DEC, PAST // P, P, KVL).transpose(0, 2, 1, 3)),
        "cache_lat_t": c(i["cache_mla_latent"][0].reshape(NB_DEC, PAST, 2, P).transpose(0, 3, 2, 1)),
        "cache_kr_t": c(i["cache_mla_krope"][0].transpose(0, 2, 1)),
        "cache_k_t": c(i["cache_swa_k"][0].reshape(NB_DEC, WINDOW, KVH * HD).transpose(0, 2, 1)),
        "cache_v": c(i["cache_swa_v"][0].reshape(NB_DEC, WINDOW, KVH * HD)),
        "cache_k_rows": c(i["cache_swa_k"][0].reshape(NB_DEC, WINDOW, KVH * HD)),
        "ada_w": c(ada.reshape(N_MOD, 2, P, UNIT)),
        "ada_rows": c(np.broadcast_to(ada_rows[:, None], (N_MOD, 9, 2, 512))),
        "in_w": c(w_in.reshape(KT, P, 6, IN_COLS).transpose(2, 1, 0, 3).reshape(6, P, KT * IN_COLS)),
        "uq_w": c(i["w_uq"][0].reshape(3, P, H * QK).transpose(1, 0, 2)),
        "ukv_w": c(i["w_ukv"][0].reshape(2, P, H, NOPE + VD).transpose(1, 0, 2, 3)),
        "uk_t": c(i["w_ukv"][0][:, :, 0:NOPE].transpose(2, 1, 0)),
        "out_w": c(i["w_out"][0].reshape(KT, P, 4, OUT_COLS).transpose(2, 1, 0, 3).reshape(4, P, KT * OUT_COLS)),
        "rows_q_kv": c(rows(np.concatenate([i["g_q_norm"][0], i["g_kv_norm"][0]]), P)),
        "sink_cols": c(np.concatenate([rows(sk, P), np.repeat(sk, Q_DEC)[:, None]], axis=1)),
        "router_w": c(i["w_router"][0].reshape(KT, P, NE).transpose(1, 0, 2)),
        "router_b": c(rows(i["b_router"][0], P)),
        "moe_w": c(moe),
        "moe_b": c(np.concatenate([i["b_gate_up"][0], i["b_down"][0]], axis=1)),
        "g_final": c(rows(i["g_final"], P)),
        "c_ident": k["ident"], "c_rope": k["rope"], "c_causal": k["causal"], "c_dist": k["dist"],
        "c_alibi": k["alibi"], "c_kind": k["kind_sel"].reshape(96, 2 * P), "c_before": k["before"].reshape(P, 2 * P),
        "c_eid": k["expert_id"], "c_rowe": k["row_expert"], "c_blk": k["block_id"].reshape(P, NOVF, NE),
        "c_tok": k["token_id"], "c_slot": k["slot_id"],
    }


def kernel(**inputs):
    import concourse.bacc as _bacc
    from concourse.bass_utils import run_bass_kernel_spmd as _run

    nc = _bacc.Bacc("TRN2", target_bir_lowering=False, num_devices=1)
    arrays, ins, outs = {}, [], []
    for name, a in layouts({k: np.asarray(v) for k, v in inputs.items()}).items():
        arrays[f"in_{name}"] = a
        ins.append(nc.dram_tensor(f"in_{name}", a.shape, mybir.dt.from_np(a.dtype), kind="ExternalInput").ap())
    for n, shape in enumerate(OUT_SHAPES):
        outs.append(nc.dram_tensor(f"out_{n}", shape, F32, kind="ExternalOutput").ap())
    build(nc, ins, outs)
    r = _run(nc, [arrays], core_ids=[0])
    return tuple(r.results[0][f"out_{n}"] for n in range(len(OUT_SHAPES)))
```
